# Optimizing a Trainium2 kernel written in Bass

```python
import jax, jax.numpy as jnp
from jax import lax
import numpy as np
import math
import jax
import jax.numpy as jnp

D_MODEL = 2048
BATCH = 1
SEQ = 256
DEPTH = 1

EPS = 1e-6
SSD_WIDTH = D_MODEL // 2
SSD_HEAD_DIM = 64
SSD_HEADS = SSD_WIDTH // SSD_HEAD_DIM
SSD_GROUPS = 2
SSD_STATE = 128
SSD_CONV = 4
SSD_CHUNK = 128
ATT_WIDTH = D_MODEL - SSD_WIDTH
ATT_HEAD_DIM = 128
ATT_HEADS = ATT_WIDTH // ATT_HEAD_DIM
ATT_KV_HEADS = 4
IDX_HEADS = 16
IDX_HEAD_DIM = 64
IDX_TOPK_MAX = 256
Q_BLOCK = 128
D_FF = 4 * D_MODEL
MIX_WIDTH = SSD_WIDTH + ATT_WIDTH
DT_COL_SCALE = 0.1

N_Z = SSD_WIDTH
N_BC = SSD_GROUPS * SSD_STATE
CONV_CH = SSD_WIDTH + 2 * N_BC
N_DT = SSD_HEADS
N_Q = ATT_HEADS * ATT_HEAD_DIM
N_KV = ATT_KV_HEADS * ATT_HEAD_DIM
N_QI = IDX_HEADS * IDX_HEAD_DIM
N_KI = IDX_HEAD_DIM
N_WI = IDX_HEADS
IN_SIZES = (N_Z, CONV_CH, N_DT, N_Q, N_KV, N_KV, N_QI, N_KI, N_WI)
IN_WIDTH = N_Z + CONV_CH + N_DT + N_Q + 2 * N_KV + N_QI + N_KI + N_WI


def _split(t, sizes):
    pts = [int(v) for v in np.cumsum(sizes)[:-1]]
    return jnp.split(t, pts, axis=-1)

def rmsnorm(x, g):
    xf = x.astype(jnp.float32)
    y = xf * lax.rsqrt(jnp.mean(xf * xf, axis=-1, keepdims=True) + EPS)
    return (y * g.astype(jnp.float32)).astype(x.dtype)

def causal_dwconv(u, w, bias):
    ch = u.shape[-1]
    out = lax.conv_general_dilated(
        u, w[:, None, :], window_strides=(1,), padding=((SSD_CONV - 1, 0),),
        dimension_numbers=("NWC", "WIO", "NWC"), feature_group_count=ch)
    return out + bias

def ssd_chunked(xs, dt, a, bm, cm):
    b, l, h, p = xs.shape
    g, n = bm.shape[-2:]
    r = h // g
    q = SSD_CHUNK
    c = l // q
    xdt = (xs * dt[..., None]).reshape(b, c, q, g, r, p)
    adt = (dt * a).reshape(b, c, q, g, r)
    bm = bm.reshape(b, c, q, g, n)
    cm = cm.reshape(b, c, q, g, n)
    a_cum = jnp.cumsum(adt, axis=2)
    seg = a_cum[:, :, :, None] - a_cum[:, :, None, :]
    causal = jnp.tril(jnp.ones((q, q), dtype=bool))[None, None, :, :, None, None]
    decay = jnp.exp(jnp.where(causal, seg, -jnp.inf))
    cb = jnp.einsum("bclgn,bcsgn->bclsg", cm, bm)
    y_diag = jnp.einsum("bclsg,bclsgr,bcsgrp->bclgrp", cb, decay, xdt)
    decay_state = jnp.exp(a_cum[:, :, -1:] - a_cum)
    states = jnp.einsum("bcsgn,bcsgr,bcsgrp->bcgrpn", bm, decay_state, xdt)
    chunk_decay = jnp.exp(a_cum[:, :, -1])

    def step(carry, inp):
        st, dec = inp
        return carry * dec[..., None, None] + st, carry

    init = jnp.zeros((b, g, r, p, n), dtype=xs.dtype)
    _, prev = lax.scan(step, init, (jnp.swapaxes(states, 0, 1), jnp.swapaxes(chunk_decay, 0, 1)))
    prev = jnp.swapaxes(prev, 0, 1)
    y_off = jnp.einsum("bclgn,bcgrpn,bclgr->bclgrp", cm, prev, jnp.exp(a_cum))
    return (y_diag + y_off).reshape(b, l, h, p)

def dsa_attention(q, k, v, q_idx, k_idx, w_idx):
    b, l = q.shape[:2]
    topk = min(IDX_TOPK_MAX, l // 4)
    qb = min(Q_BLOCK, l)
    nb = l // qb
    rep = ATT_HEADS // ATT_KV_HEADS
    key_pos = jnp.arange(l)

    def to_blocks(t):
        return jnp.swapaxes(t.reshape(b, nb, qb, *t.shape[2:]), 0, 1)

    def one_block(args):
        q_b, qi_b, wi_b, start = args
        t_pos = start + jnp.arange(qb)
        s = jnp.einsum("bqhd,bsd->bqhs", qi_b, k_idx) * (IDX_HEAD_DIM ** -0.5)
        score = jnp.einsum("bqhs,bqh->bqs", jax.nn.relu(s), wi_b).astype(jnp.float32)
        admissible = key_pos[None, :] <= t_pos[:, None]
        score = jnp.where(admissible[None], score, -jnp.inf)
        _, sel = lax.top_k(score, topk)
        sel_ok = sel <= t_pos[None, :, None]
        k_sel = jax.vmap(lambda kk, ii: kk[ii])(k, sel)
        v_sel = jax.vmap(lambda vv, ii: vv[ii])(v, sel)
        qg = q_b.reshape(b, qb, ATT_KV_HEADS, rep, ATT_HEAD_DIM)
        logits = jnp.einsum("bqhgd,bqkhd->bqhgk", qg, k_sel).astype(jnp.float32) * (ATT_HEAD_DIM ** -0.5)
        logits = jnp.where(sel_ok[:, :, None, None, :], logits, -jnp.inf)
        prob = jax.nn.softmax(logits, axis=-1).astype(v.dtype)
        o = jnp.einsum("bqhgk,bqkhd->bqhgd", prob, v_sel)
        return o.reshape(b, qb, ATT_HEADS * ATT_HEAD_DIM)

    starts = jnp.arange(nb, dtype=jnp.int32) * qb
    out = lax.map(one_block, (to_blocks(q), to_blocks(q_idx), to_blocks(w_idx), starts))
    return jnp.swapaxes(out, 0, 1).reshape(b, l, ATT_HEADS * ATT_HEAD_DIM)

def hybrid_layer(x, g_mix, w_in, conv_w, conv_b, dt_bias, a_log, d_skip, g_ssd,
                 g_q, g_k, g_kidx, w_out, g_mlp, w_up, w_down):
    b, l, _ = x.shape
    h = rmsnorm(x, g_mix) @ w_in
    z, xbc, dt, q, k, v, qi, ki, wi = _split(h, IN_SIZES)

    xbc = jax.nn.silu(causal_dwconv(xbc, conv_w, conv_b))
    xs, bm, cm = _split(xbc, (SSD_WIDTH, N_BC, N_BC))
    xs_f = xs.astype(jnp.float32).reshape(b, l, SSD_HEADS, SSD_HEAD_DIM)
    dt_f = jax.nn.softplus(dt.astype(jnp.float32) + dt_bias.astype(jnp.float32))
    a = -jnp.exp(a_log.astype(jnp.float32))
    y = ssd_chunked(xs_f, dt_f, a,
                    bm.astype(jnp.float32).reshape(b, l, SSD_GROUPS, SSD_STATE),
                    cm.astype(jnp.float32).reshape(b, l, SSD_GROUPS, SSD_STATE))
    y = y + d_skip.astype(jnp.float32)[:, None] * xs_f
    y = y.reshape(b, l, SSD_WIDTH) * jax.nn.silu(z.astype(jnp.float32))
    yg = y.reshape(b, l, SSD_GROUPS, SSD_WIDTH // SSD_GROUPS)
    yg = yg * lax.rsqrt(jnp.mean(yg * yg, axis=-1, keepdims=True) + EPS)
    y_ssd = (yg.reshape(b, l, SSD_WIDTH) * g_ssd.astype(jnp.float32)).astype(x.dtype)

    q = rmsnorm(q.reshape(b, l, ATT_HEADS, ATT_HEAD_DIM), g_q)
    k = rmsnorm(k.reshape(b, l, ATT_KV_HEADS, ATT_HEAD_DIM), g_k)
    v = v.reshape(b, l, ATT_KV_HEADS, ATT_HEAD_DIM)
    qi = qi.reshape(b, l, IDX_HEADS, IDX_HEAD_DIM)
    ki = rmsnorm(ki, g_kidx)
    wi = wi * (IDX_HEADS ** -0.5)
    y_att = dsa_attention(q, k, v, qi, ki, wi)

    x = x + jnp.concatenate([y_ssd, y_att], axis=-1) @ w_out

    u = rmsnorm(x, g_mlp) @ w_up
    return x + jnp.square(jax.nn.relu(u)) @ w_down

def first_inputs(seed: int = 0) -> dict:
    key = jax.random.key(seed)
    ks = jax.random.split(key, 20)
    f32 = jnp.float32
    nrm = lambda k, shape, s: jax.random.normal(k, shape, f32) * s
    gain = lambda k, shape: 1.0 + 0.02 * jax.random.normal(k, shape, f32)

    x = jax.random.normal(ks[0], (BATCH, SEQ, D_MODEL), f32)
    col_scale = jnp.ones((IN_WIDTH,), f32).at[N_Z + CONV_CH:N_Z + CONV_CH + N_DT].set(DT_COL_SCALE)
    w_in = nrm(ks[1], (DEPTH, D_MODEL, IN_WIDTH), D_MODEL ** -0.5) * col_scale
    conv_w = nrm(ks[2], (DEPTH, SSD_CONV, CONV_CH), SSD_CONV ** -0.5)
    conv_b = nrm(ks[3], (DEPTH, CONV_CH), 0.01)
    u = jax.random.uniform(ks[4], (DEPTH, SSD_HEADS), f32)
    dt0 = jnp.exp(u * (jnp.log(0.1) - jnp.log(0.001)) + jnp.log(0.001))
    dt_bias = dt0 + jnp.log(-jnp.expm1(-dt0))
    a_log = jnp.log(jax.random.uniform(ks[5], (DEPTH, SSD_HEADS), f32, 1.0, 16.0))
    d_skip = 1.0 + 0.1 * jax.random.normal(ks[6], (DEPTH, SSD_HEADS), f32)
    return {
        "x": x,
        "g_mix": gain(ks[7], (DEPTH, D_MODEL)),
        "w_in": w_in,
        "conv_w": conv_w,
        "conv_b": conv_b,
        "dt_bias": dt_bias,
        "a_log": a_log,
        "d_skip": d_skip,
        "g_ssd": gain(ks[8], (DEPTH, SSD_WIDTH)),
        "g_q": gain(ks[9], (DEPTH, ATT_HEAD_DIM)),
        "g_k": gain(ks[10], (DEPTH, ATT_HEAD_DIM)),
        "g_kidx": gain(ks[11], (DEPTH, IDX_HEAD_DIM)),
        "w_out": nrm(ks[12], (DEPTH, MIX_WIDTH, D_MODEL), MIX_WIDTH ** -0.5),
        "g_mlp": gain(ks[13], (DEPTH, D_MODEL)),
        "w_up": nrm(ks[14], (DEPTH, D_MODEL, D_FF), D_MODEL ** -0.5),
        "w_down": nrm(ks[15], (DEPTH, D_FF, D_MODEL), D_FF ** -0.5),
    }

def first_block(x, g_mix, w_in, conv_w, conv_b, dt_bias, a_log, d_skip, g_ssd,
              g_q, g_k, g_kidx, w_out, g_mlp, w_up, w_down):
    for i in range(DEPTH):
        x = hybrid_layer(x, g_mix[i], w_in[i], conv_w[i], conv_b[i], dt_bias[i], a_log[i],
                         d_skip[i], g_ssd[i], g_q[i], g_k[i], g_kidx[i], w_out[i],
                         g_mlp[i], w_up[i], w_down[i])
    return x


NSA_HEADS = 8
NSA_KV_GROUPS = 2
NSA_HPG = NSA_HEADS // NSA_KV_GROUPS
NSA_HEAD_DIM = 128
NSA_WIDTH = NSA_HEADS * NSA_HEAD_DIM
NSA_KV_WIDTH = NSA_KV_GROUPS * NSA_HEAD_DIM
CMP_BLOCK = 32
CMP_STRIDE = 16
CMP_HIDDEN = 256
SEL_BLOCK = 64
SEL_TOP_N = 16
SEL_FORCE = 1000.0
WINDOW = 512
NSA_QBLOCK = 32

GDN_HEADS = 8
GDN_HEAD_DIM = 128
GDN_WIDTH = GDN_HEADS * GDN_HEAD_DIM
CONV_WIDTH = 4
GDN_CHUNK = 64

REL_BUCKETS = 32
REL_MAX_DIST = 128

D_FF_2 = 4 * D_MODEL
NORM_EPS = 1e-6

IN_SPLIT_SIZES = (NSA_WIDTH, 6 * NSA_KV_WIDTH, 3 * NSA_HEADS, 3 * GDN_WIDTH, GDN_WIDTH, GDN_HEADS, GDN_HEADS, 2 * D_MODEL)
IN_COLS = NSA_WIDTH + 6 * NSA_KV_WIDTH + 3 * NSA_HEADS + 3 * GDN_WIDTH + GDN_WIDTH + GDN_HEADS + GDN_HEADS + 2 * D_MODEL


def rms_norm(x, w):
    xf = x.astype(jnp.float32)
    y = xf * lax.rsqrt(jnp.mean(xf * xf, axis=-1, keepdims=True) + NORM_EPS)
    return (y * w.astype(jnp.float32)).astype(x.dtype)

def masked_softmax(s, valid):
    s = jnp.where(valid, s.astype(jnp.float32), -jnp.inf)
    m = jnp.max(s, axis=-1, keepdims=True)
    m = jnp.where(jnp.isfinite(m), m, 0.0)
    e = jnp.exp(s - m)
    return e / jnp.maximum(jnp.sum(e, axis=-1, keepdims=True), 1e-30)

def t5_bucket(dist):
    n = jnp.maximum(dist, 0)
    exact = REL_BUCKETS // 2
    nf = jnp.maximum(n, 1).astype(jnp.float32)
    large = exact + (jnp.log(nf / exact) / math.log(REL_MAX_DIST / exact) * (REL_BUCKETS - exact)).astype(jnp.int32)
    large = jnp.minimum(large, REL_BUCKETS - 1)
    return jnp.where(n < exact, n, large)

def rel_bias_grid(rel_table, dist):
    tq, tk = dist.shape
    b = rel_table[t5_bucket(dist)]
    return b.reshape(tq, tk, NSA_KV_GROUPS, NSA_HPG).transpose(2, 3, 0, 1)

def compress_tokens(kv, pe, w1, w2):
    b, s, g, dh = kv.shape
    n_sub = CMP_BLOCK // CMP_STRIDE
    n_cmp = s // CMP_STRIDE - n_sub + 1
    r = kv.reshape(b, s // CMP_STRIDE, CMP_STRIDE, g, dh)
    blocks = jnp.concatenate([r[:, j:j + n_cmp] for j in range(n_sub)], axis=2)
    blocks = blocks + pe[None, None, :, None, :]
    flat = blocks.transpose(0, 1, 3, 2, 4).reshape(b, n_cmp, g, CMP_BLOCK * dh)
    return jax.nn.gelu(flat @ w1) @ w2

def nsa_attention(q, kv, gate_logits, rel_table, pe_k, pe_v, w1_k, w2_k, w1_v, w2_v):
    b, s, _ = q.shape
    g_, j_, dh = NSA_KV_GROUPS, NSA_HPG, NSA_HEAD_DIM
    scale = dh ** -0.5
    q = q.reshape(b, s, g_, j_, dh)
    k_c, v_c, k_s, v_s, k_w, v_w = [t.reshape(b, s, g_, dh) for t in jnp.split(kv, 6, axis=-1)]
    kc = compress_tokens(k_c, pe_k, w1_k, w2_k)
    vc = compress_tokens(v_c, pe_v, w1_v, w2_v)
    n_cmp = kc.shape[1]
    n_sel = s // SEL_BLOCK
    top_n = min(SEL_TOP_N, n_sel)
    ks = k_s.reshape(b, n_sel, SEL_BLOCK, g_, dh).transpose(0, 3, 1, 2, 4)
    vs = v_s.reshape(b, n_sel, SEL_BLOCK, g_, dh).transpose(0, 3, 1, 2, 4)
    pad = ((0, 0), (WINDOW, 0), (0, 0), (0, 0))
    kw = jnp.pad(k_w, pad)
    vw = jnp.pad(v_w, pad)
    gates = jax.nn.sigmoid(gate_logits).reshape(b, s, g_, j_, 3)

    cmp_end = jnp.arange(n_cmp) * CMP_STRIDE + (CMP_BLOCK - 1)
    c_start = np.arange(n_cmp) * CMP_STRIDE
    s_start = np.arange(n_sel) * SEL_BLOCK
    cover = jnp.asarray(((c_start[:, None] <= s_start[None, :] + SEL_BLOCK - 1)
                         & (c_start[:, None] + CMP_BLOCK - 1 >= s_start[None, :])).astype(np.float32))
    sel_ids = jnp.arange(n_sel)
    rel_flat = rel_table.reshape(REL_BUCKETS, g_, j_).transpose(1, 0, 2).reshape(g_ * REL_BUCKETS, j_)
    group_off = jnp.arange(g_)[None, :, None, None, None] * REL_BUCKETS
    gather_blocks = jax.vmap(jax.vmap(lambda blk, ix: blk[ix]))

    def query_block(i):
        q0 = i * NSA_QBLOCK
        t = q0 + jnp.arange(NSA_QBLOCK)
        qb = lax.dynamic_slice_in_dim(q, q0, NSA_QBLOCK, axis=1)
        gb = lax.dynamic_slice_in_dim(gates, q0, NSA_QBLOCK, axis=1)

        dist_c = t[:, None] - cmp_end[None, :]
        s_c = jnp.einsum('btgjd,bngd->bgjtn', qb, kc) * scale + rel_bias_grid(rel_table, dist_c)
        p_c = masked_softmax(s_c, dist_c >= 0)
        o_c = jnp.einsum('bgjtn,bngd->btgjd', p_c.astype(vc.dtype), vc)

        imp = jnp.einsum('bgjtn,nm->btgm', p_c, cover)
        cur = t // SEL_BLOCK
        forced = (sel_ids[None, :] == 0) | (sel_ids[None, :] == cur[:, None]) | (sel_ids[None, :] == cur[:, None] - 1)
        causal_blk = sel_ids[None, :] <= cur[:, None]
        score = jnp.where(causal_blk[:, None, :], imp + jnp.where(forced, SEL_FORCE, 0.0)[:, None, :], -jnp.inf)
        top_val, top_idx = lax.top_k(score, top_n)
        top_idx = top_idx.transpose(0, 2, 1, 3)
        k_sel = gather_blocks(ks, top_idx)
        v_sel = gather_blocks(vs, top_idx)
        key_pos = top_idx[..., None] * SEL_BLOCK + jnp.arange(SEL_BLOCK)
        dist_s = t[None, None, :, None, None] - key_pos
        valid_s = jnp.isfinite(top_val).transpose(0, 2, 1, 3)[..., None] & (dist_s >= 0)
        bias_s = rel_flat[group_off + t5_bucket(dist_s)]
        s_s = jnp.einsum('btgjd,bgtnrd->bgjtnr', qb, k_sel) * scale + jnp.moveaxis(bias_s, -1, 2)
        n_keys = top_n * SEL_BLOCK
        p_s = masked_softmax(s_s.reshape(b, g_, j_, NSA_QBLOCK, n_keys),
                             valid_s.reshape(b, g_, 1, NSA_QBLOCK, n_keys))
        o_s = jnp.einsum('bgjtnr,bgtnrd->btgjd', p_s.reshape(s_s.shape).astype(v_sel.dtype), v_sel)

        kwb = lax.dynamic_slice_in_dim(kw, q0, WINDOW + NSA_QBLOCK, axis=1)
        vwb = lax.dynamic_slice_in_dim(vw, q0, WINDOW + NSA_QBLOCK, axis=1)
        kpos = q0 - WINDOW + jnp.arange(WINDOW + NSA_QBLOCK)
        dist_w = t[:, None] - kpos[None, :]
        valid_w = (dist_w >= 0) & (dist_w < WINDOW) & (kpos[None, :] >= 0)
        s_w = jnp.einsum('btgjd,bsgd->bgjts', qb, kwb) * scale + rel_bias_grid(rel_table, dist_w)
        p_w = masked_softmax(s_w, valid_w)
        o_w = jnp.einsum('bgjts,bsgd->btgjd', p_w.astype(vwb.dtype), vwb)

        return gb[..., 0:1] * o_c + gb[..., 1:2] * o_s + gb[..., 2:3] * o_w

    out = lax.map(query_block, jnp.arange(s // NSA_QBLOCK))
    return out.transpose(1, 0, 2, 3, 4, 5).reshape(b, s, NSA_WIDTH)

def causal_depthwise_conv(x, w):
    return lax.conv_general_dilated(x, w[:, None, :], window_strides=(1,), padding=[(CONV_WIDTH - 1, 0)],
                                    dimension_numbers=('NWC', 'WIO', 'NWC'), feature_group_count=x.shape[-1])

def l2_normalize(x):
    return x * lax.rsqrt(jnp.sum(x * x, axis=-1, keepdims=True) + NORM_EPS)

def gated_delta_rule(q, k, v, g, beta):
    b, s, h, dk = q.shape
    dv = v.shape[-1]
    c = GDN_CHUNK
    n = s // c
    q = l2_normalize(q) * dk ** -0.5
    k = l2_normalize(k)

    def chunks(t):
        return jnp.moveaxis(t.reshape(b, n, c, h, *t.shape[3:]), 3, 1)

    q, k, v, g, beta = (chunks(t) for t in (q, k, v, g, beta))
    g = jnp.cumsum(g, axis=-1)
    kb = k * beta[..., None]
    vb = v * beta[..., None]
    tri = jnp.tril(jnp.ones((c, c), dtype=bool))
    strict = jnp.tril(jnp.ones((c, c), dtype=bool), -1)
    diff = g[..., :, None] - g[..., None, :]
    decay = jnp.where(tri, jnp.exp(jnp.where(tri, diff, 0.0)), 0.0)
    lower = jnp.where(strict, jnp.einsum('bhncd,bhnsd->bhncs', kb, k) * decay, 0.0)
    eye = jnp.eye(c, dtype=q.dtype)
    tinv = lax.linalg.triangular_solve(eye + lower, jnp.broadcast_to(eye, lower.shape),
                                       left_side=True, lower=True, unit_diagonal=True)
    u = tinv @ vb
    w = tinv @ (kb * jnp.exp(g)[..., None])
    qk = jnp.einsum('bhncd,bhnsd->bhncs', q, k) * decay

    def step(state, inp):
        qn, kn, un, wn, gn, qkn = inp
        v_new = un - wn @ state
        o = (qn * jnp.exp(gn)[..., None]) @ state + qkn @ v_new
        g_last = gn[..., -1:]
        state = state * jnp.exp(g_last)[..., None] + jnp.einsum('bhck,bhcv->bhkv', kn * jnp.exp(g_last - gn)[..., None], v_new)
        return state, o

    xs = tuple(jnp.moveaxis(t, 2, 0) for t in (q, k, u, w, g, qk))
    state0 = jnp.zeros((b, h, dk, dv), q.dtype)
    _, o = lax.scan(step, state0, xs)
    return o.transpose(1, 0, 3, 2, 4).reshape(b, s, h, dv)

def gated_deltanet(qkv, z, a, bl, conv_w, a_log, dt_bias, norm_w):
    b, s, _ = qkv.shape
    dtype = qkv.dtype
    qkv = jax.nn.silu(causal_depthwise_conv(qkv, conv_w)).astype(jnp.float32)
    q, k, v = jnp.split(qkv, 3, axis=-1)
    shape = (b, s, GDN_HEADS, GDN_HEAD_DIM)
    beta = jax.nn.sigmoid(bl.astype(jnp.float32))
    g = -jnp.exp(a_log.astype(jnp.float32)) * jax.nn.softplus(a.astype(jnp.float32) + dt_bias.astype(jnp.float32))
    o = gated_delta_rule(q.reshape(shape), k.reshape(shape), v.reshape(shape), g, beta)
    o = o * lax.rsqrt(jnp.mean(o * o, axis=-1, keepdims=True) + NORM_EPS) * norm_w.astype(jnp.float32)
    o = o * jax.nn.silu(z.astype(jnp.float32)).reshape(shape)
    return o.reshape(b, s, GDN_WIDTH).astype(dtype)

def hybrid_layer_2(x, rel_table, ln1_w, w_in, pe_k, pe_v, w1_k, w2_k, w1_v, w2_v, conv_w, a_log, dt_bias,
                 gdn_norm_w, w_pa, w_pb, w_o, ln2_w, w_up, w_down):
    h = rms_norm(x, ln1_w)
    proj = h @ w_in
    offs = [int(o) for o in np.cumsum(IN_SPLIT_SIZES)[:-1]]
    nsa_q, nsa_kv, nsa_gate, gdn_qkv, gdn_z, gdn_a, gdn_b, merge = jnp.split(proj, offs, axis=-1)
    o_a = nsa_attention(nsa_q, nsa_kv, nsa_gate, rel_table, pe_k, pe_v, w1_k, w2_k, w1_v, w2_v)
    o_b = gated_deltanet(gdn_qkv, gdn_z, gdn_a, gdn_b, conv_w, a_log, dt_bias, gdn_norm_w)
    g_a, g_b = jnp.split(jax.nn.sigmoid(merge), 2, axis=-1)
    x = x + (g_a * (o_a @ w_pa) + g_b * (o_b @ w_pb)) @ w_o
    h = rms_norm(x, ln2_w)
    return x + jnp.square(jax.nn.relu(h @ w_up)) @ w_down

def second_inputs(seed: int = 0) -> dict:
    key = jax.random.key(seed)
    k = jax.random.split(key, 21)
    f32 = jnp.float32
    L = DEPTH

    def normal(kk, shape, scale):
        return jax.random.normal(kk, shape, f32) * scale

    cmp_in = CMP_BLOCK * NSA_HEAD_DIM
    dt = jnp.exp(jax.random.uniform(k[12], (L, GDN_HEADS), f32, math.log(1e-3), math.log(1e-1)))
    return {
        'x': normal(k[0], (BATCH, SEQ, D_MODEL), 1.0),
        'rel_table': normal(k[1], (REL_BUCKETS, NSA_HEADS), 0.5),
        'ln1_w': 1.0 + normal(k[2], (L, D_MODEL), 0.02),
        'w_in': normal(k[3], (L, D_MODEL, IN_COLS), D_MODEL ** -0.5),
        'cmp_pe_k': normal(k[4], (L, CMP_BLOCK, NSA_HEAD_DIM), 0.1),
        'cmp_pe_v': normal(k[5], (L, CMP_BLOCK, NSA_HEAD_DIM), 0.1),
        'cmp_w1_k': normal(k[6], (L, cmp_in, CMP_HIDDEN), cmp_in ** -0.5),
        'cmp_w2_k': normal(k[7], (L, CMP_HIDDEN, NSA_HEAD_DIM), CMP_HIDDEN ** -0.5),
        'cmp_w1_v': normal(k[8], (L, cmp_in, CMP_HIDDEN), cmp_in ** -0.5),
        'cmp_w2_v': normal(k[9], (L, CMP_HIDDEN, NSA_HEAD_DIM), CMP_HIDDEN ** -0.5),
        'conv_w': normal(k[10], (L, CONV_WIDTH, 3 * GDN_WIDTH), CONV_WIDTH ** -0.5),
        'a_log': jnp.log(jax.random.uniform(k[11], (L, GDN_HEADS), f32, 1.0, 16.0)),
        'dt_bias': dt + jnp.log(-jnp.expm1(-dt)),
        'gdn_norm_w': 1.0 + normal(k[13], (L, GDN_HEAD_DIM), 0.02),
        'w_pa': normal(k[14], (L, NSA_WIDTH, D_MODEL), NSA_WIDTH ** -0.5),
        'w_pb': normal(k[15], (L, GDN_WIDTH, D_MODEL), GDN_WIDTH ** -0.5),
        'w_o': normal(k[16], (L, D_MODEL, D_MODEL), D_MODEL ** -0.5),
        'ln2_w': 1.0 + normal(k[17], (L, D_MODEL), 0.02),
        'w_up': normal(k[18], (L, D_MODEL, D_FF_2), D_MODEL ** -0.5),
        'w_down': normal(k[19], (L, D_FF_2, D_MODEL), D_FF_2 ** -0.5),
        'ln_f_w': 1.0 + normal(k[20], (D_MODEL,), 0.02),
    }

def second_block(x, rel_table, ln1_w, w_in, cmp_pe_k, cmp_pe_v, cmp_w1_k, cmp_w2_k, cmp_w1_v, cmp_w2_v, conv_w,
              a_log, dt_bias, gdn_norm_w, w_pa, w_pb, w_o, ln2_w, w_up, w_down, ln_f_w):
    for l in range(DEPTH):
        x = hybrid_layer_2(x, rel_table, ln1_w[l], w_in[l], cmp_pe_k[l], cmp_pe_v[l], cmp_w1_k[l], cmp_w2_k[l],
                         cmp_w1_v[l], cmp_w2_v[l], conv_w[l], a_log[l], dt_bias[l], gdn_norm_w[l],
                         w_pa[l], w_pb[l], w_o[l], ln2_w[l], w_up[l], w_down[l])
    return rms_norm(x, ln_f_w)


def setup_inputs(seed=0):
    out = dict(first_inputs(seed))
    for name, value in second_inputs(seed + 1).items():
        if name != "x":
            out[name + "_2"] = value
    return out


def reference(
    x, g_mix, w_in, conv_w, conv_b, dt_bias, a_log, d_skip, g_ssd, g_q, g_k, g_kidx, w_out,
    g_mlp, w_up, w_down, rel_table_2, ln1_w_2, w_in_2, cmp_pe_k_2, cmp_pe_v_2, cmp_w1_k_2,
    cmp_w2_k_2, cmp_w1_v_2, cmp_w2_v_2, conv_w_2, a_log_2, dt_bias_2, gdn_norm_w_2, w_pa_2,
    w_pb_2, w_o_2, ln2_w_2, w_up_2, w_down_2, ln_f_w_2,
):
    x = first_block(
        x, g_mix, w_in, conv_w, conv_b, dt_bias, a_log, d_skip, g_ssd, g_q, g_k, g_kidx, w_out,
        g_mlp, w_up, w_down,
    )
    return second_block(
        x, rel_table_2, ln1_w_2, w_in_2, cmp_pe_k_2, cmp_pe_v_2, cmp_w1_k_2, cmp_w2_k_2,
        cmp_w1_v_2, cmp_w2_v_2, conv_w_2, a_log_2, dt_bias_2, gdn_norm_w_2, w_pa_2, w_pb_2,
        w_o_2, ln2_w_2, w_up_2, w_down_2, ln_f_w_2,
    )


_drawn_inputs = setup_inputs


def setup_inputs(seed=0):
    import zlib

    import numpy as np

    out = dict(_drawn_inputs(seed))
    spreads = {}
    factors = {'conv_b': 6.872,
     'g_ssd': 4.369,
     'g_q': 8.0,
     'g_k': 8.0,
     'g_kidx': 4.367,
     'g_mlp': 3.142,
     'ln1_w_2': 8.0,
     'cmp_pe_k_2': 114.632,
     'cmp_pe_v_2': 145.752,
     'cmp_w1_k_2': 2.863,
     'cmp_w2_k_2': 3.009,
     'gdn_norm_w_2': 23.385,
     'ln2_w_2': 17.614,
     'ln_f_w_2': 21.956,
     'rel_table_2': 20.045}
    for name, (base, spread) in spreads.items():
        noise = np.random.default_rng([zlib.crc32(name.encode()), seed]).standard_normal(out[name].shape)
        drawn = base * np.exp(spread * noise) if base else spread * noise
        out[name] = jnp.asarray(drawn.astype(out[name].dtype))
    for name, factor in factors.items():
        out[name] = (out[name] * factor).astype(out[name].dtype)
    return out
```

```python
from contextlib import ExitStack

import numpy as np

import concourse.bass as bass
from concourse import mybir

F32 = mybir.dt.float32
ALU = mybir.AluOpType
ACT = mybir.ActivationFunctionType
AX_X = mybir.AxisListType.X

P = 128
D = 2048
S = 256
KD = D // P
FF = 4 * D
EPS = 1e-6
NEG = -1e30
PICKED = -3e38

SSD_W, SSD_HEADS, SSD_GROUPS = 1024, 16, 2
CONV_TAPS = 4
XBC = 1536
ATT_HEADS, ATT_KV = 8, 4
IDX_HEADS, IDX_DIM, TOPK = 16, 64, 64
Z_T, XBC_T, Q_T, K_T, QI_T = 8, 12, 8, 4, 8
NSA_HEADS, NSA_GROUPS = 8, 2
CMP_STRIDE, CMP_BLOCK, N_CMP, CMP_HID = 16, 32, 15, 256
GDN_HEADS, CHUNK = 8, 64
HALF_HEADS = 4
REL_BUCKETS = 32
SCALE = float(P) ** -0.5

SLOT = 4096
SLOTS = 4
ARENA = 19900

VECS = dict(g_mix=16, g_ssd=8, g_q=1, g_k=1, g_ki=1, conv_w=48, conv_b=12, d_skip=8, dt_bias=16, a_log=16,
            g_mlp=16, ln1=16, conv_w2=96, a_log2=8, dt_bias2=8, gdn_norm=1, ln2=16, ln_f=16, pe_k=32, pe_v=32)
MATS = ["ident", "upto", "upto64", "ones64", "neg_after", "neg_after64", "neg_before"] + [
    f"level{b}" for b in (1, 2, 4, 8, 16, 32)]
LEVELS = (2, 4, 8, 16, 32)


def constants():
    i = np.arange(P)
    r, c = i[:, None], i[None, :]
    same = (r // CHUNK) == (c // CHUNK)
    m = {
        "ident": r == c,
        "upto": r <= c,
        "upto64": (r <= c) & same,
        "ones64": same,
        "neg_after": np.where(r <= c, 0.0, NEG),
        "neg_after64": np.where((r <= c) & same, 0.0, NEG),
        "neg_before": np.where(c <= r, 0.0, NEG),
    }
    for b in (1, 2, 4, 8, 16, 32):
        m[f"level{b}"] = (r // (2 * b) == c // (2 * b)) & (r % (2 * b) < b) & (c % (2 * b) >= b)
    mats = np.concatenate([np.asarray(m[n], np.float32) for n in MATS], axis=1)
    dist = (S - 1) - np.arange(2 * S)
    exact = REL_BUCKETS // 2
    near = np.maximum(dist, 1).astype(np.float32)
    far = exact + (np.log(near / exact) / np.log(np.float32(P / exact)) * (REL_BUCKETS - exact)).astype(np.int32)
    bucket = np.where(dist < exact, np.maximum(dist, 0), np.minimum(far, REL_BUCKETS - 1))
    hot = np.zeros((REL_BUCKETS + 1, 2 * S), np.float32)
    for j in range(2 * S):
        hot[bucket[j] if dist[j] >= 0 else REL_BUCKETS, j] = 1.0
    return mats, hot


class Engine:

    def __init__(self, name, sem):
        self.name, self.sem, self.count, self.items, self.seen = name, sem, 0, [], {}

    def wait(self, tokens):
        for t in tokens:
            if t is None:
                continue
            if isinstance(t, list):
                self.wait(t)
                continue
            sem, value = t
            if self.seen.get(id(sem), 0) < value:
                self.seen[id(sem)] = value
                self.items.append(lambda e, sem=sem, value=value: e.wait_ge(sem, value))

    def do(self, step, *after, signal=True):
        self.wait(after)
        if signal:
            self.count += 1
            self.items.append(lambda e: step(e).then_inc(self.sem, 1))
            return (self.sem, self.count)
        self.items.append(step)
        return None

    def run(self, e):
        for item in self.items:
            item(e)


def build(nc, t_in, x_out, bias_rows):
    ctx = ExitStack()
    with ctx:
        def sb(name, shape):
            return ctx.enter_context(nc.sbuf_tensor(name, shape, F32))

        def sem(name):
            return ctx.enter_context(nc.semaphore(name))

        pe = Engine("tensor", sem("pe_steps"))
        dve = Engine("vector", sem("dve_steps"))
        act = Engine("scalar", sem("act_steps"))
        pool = Engine("gpsimd", sem("pool_steps"))
        sp = Engine("sync", sem("sp_steps"))

        ring = sb("weight_ring", [P, SLOTS, SLOT])
        xT = sb("x_T", [P, KD * S])
        hT = sb("h_T", [P, KD * S])
        mixT = sb("mix_T", [P, KD * S])
        mats = sb("const_mats", [P, len(MATS) * P])
        ones = sb("ones", [P, P])
        vecs = sb("vecs", [P, sum(VECS.values())])
        w_dtwi = sb("w_dt_wi", [P, KD * 32])
        w_gab = sb("w_gates_a_b", [P, KD * 40])
        w_cmp2 = sb("w_cmp2", [P, 2 * 2 * P])
        eps = sb("eps", [P, 1])
        hot = sb("bucket_hot", [REL_BUCKETS + 1, 2 * S])
        rel = sb("rel_rows", [REL_BUCKETS + 1, NSA_HEADS])
        arena = sb("arena", [P, ARENA])
        psum = [ctx.enter_context(nc.psum_tensor(f"bank{i}", [P, 512], F32)) for i in range(8)]

        slot_sem = [sem(f"slot_loaded{i}") for i in range(SLOTS)]
        param_sem = sem("params_loaded")
        x_sem = sem("x_loaded")
        rows_sem = sem("bias_rows_written")
        toep_sem = sem("bias_grid_loaded")
        out_sem = sem("out_written")

        def mat(name):
            i = MATS.index(name)
            return mats[:, i * P:(i + 1) * P]

        vec_at = {}
        at = 0
        for name, w in VECS.items():
            vec_at[name] = at
            at += w

        def vec(name, i=0, n=1):
            return vecs[:, vec_at[name] + i:vec_at[name] + i + n]

        def pair(buf, j):
            return buf[:, 2 * j * S:(2 * j + 2) * S]

        def tile(buf, k):
            return buf[:, k * S:(k + 1) * S]

        cursor = [0]

        def take(n):
            a = cursor[0]
            cursor[0] += n
            assert cursor[0] <= ARENA, cursor[0]
            return arena[:, a:a + n]

        def barrier():
            now = [(e.sem, e.count) for e in (pe, dve, act, pool) if e.count]
            for e in (pe, dve, act, pool):
                e.wait([t for t in now if t[0] is not e.sem or e is not pe])
            return now

        class Turns:

            def __init__(self, bufs):
                self.bufs, self.free, self.n = bufs, [None] * len(bufs), 0

            def take(self):
                i = self.n % len(self.bufs)
                self.n += 1
                return i, self.bufs[i], self.free[i]

            def give(self, i, *tokens):
                self.free[i] = list(tokens)

        gemm_banks = Turns([psum[i] for i in (0, 1, 2)])
        side_banks = Turns([psum[i] for i in (3, 4, 5, 6, 7)])

        loaded = [0] * SLOTS
        freed = [None] * SLOTS
        taken = [0]

        def next_slot(src):
            i = taken[0] % SLOTS
            taken[0] += 1
            sp.wait([freed[i]])
            n = src.shape[1]
            sp.items.append(lambda e: e.dma_start(ring[:, i, 0:n], src).then_inc(slot_sem[i], 16))
            loaded[i] += 16
            return i, ring[:, i, :], (slot_sem[i], loaded[i])

        def mm(out, lhsT, rhs, start, stop, *after, signal=False):
            return pe.do(lambda e: nc.tensor.matmul(out, lhsT, rhs, start=start, stop=stop), *after, signal=signal)

        def turn(out, src, *after, signal=False):
            k = src.shape[0]
            return pe.do(lambda e: nc.tensor.transpose(out, src, mat("ident")[0:k, 0:k]), *after, signal=signal)

        def v_tt(out, a, b, op, *after):
            return dve.do(lambda e: nc.vector.tensor_tensor(out, a, b, op), *after)

        def v_ts(out, a, s1, s2, op0, op1, *after):
            if op1 is None:
                return dve.do(lambda e: nc.vector.tensor_scalar(out, a, s1, None, op0), *after)
            return dve.do(lambda e: nc.vector.tensor_scalar(out, a, s1, s2, op0, op1), *after)

        def v_stt(out, a, s, b, op0, op1, *after):
            return dve.do(lambda e: nc.vector.scalar_tensor_tensor(out=out, in0=a, scalar=s, in1=b, op0=op0, op1=op1),
                          *after)

        def v_rec(out, a, *after):
            return dve.do(lambda e: nc.vector.reciprocal(out, a), *after)

        def v_copy(out, a, *after):
            return dve.do(lambda e: nc.vector.tensor_copy(out, a), *after)

        def v_red(out, a, op, *after, negate=None):
            return dve.do(lambda e: nc.vector.tensor_reduce(out, a, AX_X, op, negate=negate), *after)

        def a_act(out, a, func, *after, scale=1.0, bias=0.0, accum=None):
            kw = {} if accum is None else dict(accum_out=accum)
            return act.do(lambda e: nc.scalar.activation(out, a, func, bias=bias, scale=scale, **kw), *after)

        def a_copy(out, a, *after):
            return act.do(lambda e: nc.scalar.copy(out, a), *after)

        def wide(ap, n):
            return ap.unsqueeze(2).to_broadcast([ap.shape[0], ap.shape[1], n])

        def over(ap, n):
            return ap.unsqueeze(1).to_broadcast([ap.shape[0], n, ap.shape[1]])

        def split(ap, n):
            return ap.rearrange("p (a b) -> p a b", a=n)

        def project(w, slots, rhs, rhs_ready, evacuate, k_tiles=KD, cols=2):
            for s in range(slots):
                i, slot, slot_ready = next_slot(w[s])
                b, bank, bank_free = gemm_banks.take()
                for j in range(cols):
                    for k in range(k_tiles):
                        o = (j * k_tiles + k) * P
                        last = j == cols - 1 and k == k_tiles - 1
                        done = mm(bank[:, j * S:(j + 1) * S], slot[:, o:o + P], tile(rhs, k), k == 0,
                                  k == k_tiles - 1, slot_ready, bank_free, rhs_ready[k], signal=last)
                freed[i] = done
                gemm_banks.give(b, *evacuate(s, bank, done))
                yield

        def project_values(w, out, rhs, rhs_ready, ready):
            s0 = next_slot(w[0])
            s1 = next_slot(w[1])
            for c in range(2):
                b, bank, bank_free = gemm_banks.take()
                for k in range(KD):
                    i, slot, slot_ready = (s0, s1)[k // 8]
                    o = (k % 8) * 512
                    done = mm(bank[:, :], tile(rhs, k)[:, c * P:(c + 1) * P], slot[:, o:o + 512], k == 0, k == KD - 1,
                              slot_ready, bank_free, rhs_ready[k], signal=k in (7, 15))
                    if c == 1 and k % 8 == 7:
                        freed[i] = done
                t = a_copy(out[:, c * 512:(c + 1) * 512], bank[:, :], done)
                ready.append(t)
                gemm_banks.give(b, t)
                yield

        def sums(bank, src, n, *after):
            return mm(bank[:, 0:n], ones[:, :], src, True, True, *after, signal=True)

        def rstd(out, bank, n, scale, *after):
            root = a_act(out[:, 0:n], bank[:, 0:n], ACT.Sqrt, *after, scale=scale, bias=eps[:, 0:1])
            return v_rec(out[:, 0:n], out[:, 0:n], root), root

        def norm(gain, x_ready, sq, root_buf, out=None):
            b, bank, bank_free = side_banks.take()
            for j in range(KD // 2):
                i, buf, buf_free = sq.take()
                squared = a_act(buf, pair(xT, j), ACT.Square, x_ready[j], buf_free)
                mm(bank[:, 0:S], ones[:, :], buf[:, 0:S], j == 0, False, squared, bank_free)
                done = mm(bank[:, 0:S], ones[:, :], buf[:, S:2 * S], False, j == KD // 2 - 1, signal=True)
                sq.give(i, done)
            ready, read = rstd(root_buf, bank, S, 1.0 / D, done)
            side_banks.give(b, read)
            out = hT if out is None else out
            return [v_stt(tile(out, k), tile(xT, k), vec(gain, k), root_buf[:, 0:S], ALU.mult, ALU.mult, ready)
                    for k in range(KD)]

        def head_norm(out, bank, gains, done, sq, roots, scale=1.0 / P, factor=None):
            i, buf, buf_free = sq.take()
            r, root, root_free = roots.take()
            squared = a_act(buf, bank, ACT.Square, done, buf_free)
            b, total, total_free = side_banks.take()
            summed = sums(total, buf, 512, squared, total_free)
            sq.give(i, summed)
            ready, read = rstd(root, total, 512, scale, summed, root_free)
            side_banks.give(b, read)
            t = v_stt(out, bank, gains if factor is None else factor, root, ALU.mult, ALU.mult, ready)
            roots.give(r, t)
            return t

        def residual(x_ready):
            def evacuate(s, bank, done):
                t = v_tt(pair(xT, s), pair(xT, s), bank[:, :], ALU.add, done, x_ready[s])
                x_ready[s] = t
                return [t]
            return evacuate

        def drain(*gens):
            gens = list(gens)
            while gens:
                for g in list(gens):
                    try:
                        next(g)
                    except StopIteration:
                        gens.remove(g)

        def mlp(w_up, w_down, gain, x_ready):
            uT = take(FF // P * S)
            sq = Turns([take(512), take(512)])
            root = take(S)
            h_ready = norm(gain, x_ready, sq, root)
            u_ready = [None] * (FF // P)

            def squared_relu(s, bank, done):
                r = a_act(pair(uT, s), bank[:, :], ACT.Relu, done)
                t = v_tt(pair(uT, s), pair(uT, s), pair(uT, s), ALU.mult, r)
                u_ready[2 * s] = u_ready[2 * s + 1] = t
                return [r]

            drain(project(w_up, FF // P // 2, hT, h_ready, squared_relu))
            add = residual(x_ready)
            for j in range(KD // 2):
                b, bank, bank_free = gemm_banks.take()
                for c in range(2):
                    for half in range(2):
                        i, slot, slot_ready = next_slot(w_down[(2 * j + c) * 2 + half])
                        for k in range(32):
                            kk = 32 * half + k
                            done = mm(bank[:, c * S:(c + 1) * S], slot[:, k * P:(k + 1) * P], tile(uT, kk), kk == 0,
                                      kk == 63, slot_ready, bank_free, u_ready[kk], signal=k == 31)
                        freed[i] = done
                gemm_banks.give(b, *add(j, bank, done))

        for dst, name in ((vecs, "vecs"), (mats, "mats"), (w_dtwi, "w_dtwi"), (w_gab, "w_gab"), (w_cmp2, "w_cmp2"),
                          (hot, "hot"), (rel, "rel")):
            act.items.append(lambda e, dst=dst, name=name: e.dma_start(dst[:, :], t_in[name]).then_inc(param_sem, 16))
        params = (param_sem, 16 * 7)
        x_ready = [(x_sem, 16)] * (KD // 2)
        sp.items.append(lambda e: e.dma_start(xT[:, :], t_in["x"]).then_inc(x_sem, 16))
        ones_ready = pool.do(lambda e: nc.gpsimd.memset(ones[:, :], 1.0))
        eps_ready = pool.do(lambda e: nc.gpsimd.memset(eps[:, :], EPS))
        for e in (pe, dve, act):
            e.wait([params, ones_ready, eps_ready])
        pool.wait([params])

        for h in range(NSA_HEADS):
            b, bank, bank_free = side_banks.take()
            rows_done = mm(bank[:, :], rel[:, h:h + 1].to_broadcast([REL_BUCKETS + 1, P]), hot[:, :], True, True,
                           bank_free, signal=True)
            rows_copied = v_copy(mixT[:, 512 * h:512 * h + 512], bank[:, :], rows_done)
            side_banks.give(b, rows_copied)
        pool.wait([rows_copied])
        pool.items.append(lambda e: e.dma_start(bias_rows, mixT[:, :]).then_inc(rows_sem, 16))

        qT, kT, val, qiT = take(Q_T * S), take(K_T * S), take(2 * 512), take(QI_T * S)
        kiT = take(2 * S)
        xbcT, zT = mixT, None
        zT = take(Z_T * S)
        xbcT = take(XBC_T * S)
        small = take(2 * 32)
        sq = Turns([take(512), take(512)])
        roots = Turns([take(512)])
        conv_acc = Turns([take(512)])
        keep = cursor[0]
        h_ready = norm("g_mix", x_ready, sq, roots.bufs[0])

        b, bank, bank_free = side_banks.take()
        for c in range(2):
            for k in range(KD):
                small_done = mm(bank[:, 32 * c:32 * c + 32], tile(hT, k)[:, c * P:(c + 1) * P],
                                w_dtwi[:, 32 * k:32 * k + 32], k == 0, k == KD - 1, bank_free, h_ready[k],
                                signal=k == KD - 1)
        small_ready = v_copy(small, bank[:, 0:64], small_done)
        side_banks.give(b, small_ready)
        dtwi = split(small, 2)

        ki_clear = dve.do(lambda e: nc.vector.memset(kiT, 0.0))
        ki_ready = []

        def evacuate_ki(s, bank, done):
            i, buf, buf_free = sq.take()
            r, root, root_free = roots.take()
            squared = a_act(buf[:, 0:S], bank[:, 0:S], ACT.Square, done, buf_free)
            bb, total, total_free = side_banks.take()
            summed = sums(total, buf[:, 0:S], S, squared, total_free)
            sq.give(i, summed)
            ready, read = rstd(root, total, S, 1.0 / P, summed, root_free)
            side_banks.give(bb, read)
            for half in range(2):
                p = slice(64 * half, 64 * half + 64)
                t = v_stt(kiT[p, half * S:(half + 1) * S], bank[p, 0:S], vec("g_ki")[p, :], root[p, 0:S], ALU.mult,
                          ALU.mult, ready, ki_clear)
            ki_ready.append(t)
            roots.give(r, t)
            return [t]

        qi_ready = [None] * (QI_T // 2)

        def evacuate_qi(s, bank, done):
            qi_ready[s] = a_copy(pair(qiT, s), bank[:, :], done)
            return [qi_ready[s]]

        drain(project(t_in["w_ki"], 1, hT, h_ready, evacuate_ki, cols=1))
        drain(project(t_in["w_qi"], QI_T // 2, hT, h_ready, evacuate_qi))

        score = [take(P), take(S)]
        sel_neg = [take(P), take(S)]
        best = take(8)
        relu_buf = Turns([take(512), take(512)])
        score_ready = [None, None]
        sel_ready = [None, None]
        wi = take(32)
        wi_ready = v_ts(split(wi, 2), dtwi[:, :, 16:32], float(IDX_HEADS) ** -0.5, None, ALU.mult, None, small_ready)

        def scoring():
            for t in range(QI_T):
                for qb in range(2):
                    nk = P * (qb + 1)
                    b, bank, bank_free = side_banks.take()
                    done = mm(bank[:, :], tile(qiT, t)[:, qb * P:(qb + 1) * P], kiT, True, True, bank_free,
                              ki_ready[0], qi_ready[t // 2], signal=True)
                    i, buf, buf_free = relu_buf.take()
                    relu = a_act(split(buf, 2)[:, :, 0:nk], split(bank[:, :], 2)[:, :, 0:nk], ACT.Relu, done, buf_free,
                                 scale=float(IDX_DIM) ** -0.5)
                    side_banks.give(b, relu)
                    for j in range(2):
                        h = 2 * t + j
                        col = wi[:, 16 * qb + h:16 * qb + h + 1]
                        src = buf[:, j * S:j * S + nk]
                        if h == 0:
                            score_ready[qb] = v_ts(score[qb], src, col, None, ALU.mult, None, relu, wi_ready)
                        else:
                            score_ready[qb] = v_stt(score[qb], src, col, score[qb], ALU.mult, ALU.add, relu,
                                                    score_ready[qb])
                    relu_buf.give(i, score_ready[qb])
                    yield
            for qb in range(2):
                n = qb * P
                ready = v_tt(score[qb][:, n:n + P], score[qb][:, n:n + P], mat("neg_before"), ALU.add,
                             score_ready[qb])
                for _ in range(TOPK // 8):
                    top = dve.do(lambda e, qb=qb: nc.vector.max(best, score[qb]), ready)
                    ready = dve.do(lambda e, qb=qb: nc.vector.match_replace(score[qb], best, score[qb], PICKED), top)
                ready = v_ts(sel_neg[qb], score[qb], PICKED / 2, NEG, ALU.is_gt, ALU.mult, ready)
                sel_ready[qb] = v_tt(sel_neg[qb][:, n:n + P], sel_neg[qb][:, n:n + P], mat("neg_before"), ALU.add,
                                     ready)
                yield

        q_ready, k_ready, v_ready = [None] * 4, [None] * 2, []

        def evacuate_q(s, bank, done):
            q_ready[s] = head_norm(pair(qT, s), bank[:, :], vec("g_q"), done, sq, roots)
            return [q_ready[s]]

        def evacuate_k(s, bank, done):
            k_ready[s] = head_norm(pair(kT, s), bank[:, :], vec("g_k"), done, sq, roots)
            return [k_ready[s]]

        def conv_silu(name, tiles, dst, ready, bias=None):
            def evacuate(s, bank, done):
                i, acc, acc_free = conv_acc.take()
                for j in range(2):
                    t = 2 * s + j
                    src, a = bank[:, j * S:(j + 1) * S], acc[:, j * S:(j + 1) * S]
                    tap = [vec(name, k * tiles + t) for k in range(CONV_TAPS)]
                    if bias:
                        step = v_ts(a, src, tap[3], vec(bias, t), ALU.mult, ALU.add, done, acc_free)
                    else:
                        step = v_ts(a, src, tap[3], None, ALU.mult, None, done, acc_free)
                    for back in (1, 2, 3):
                        step = v_stt(a[:, back:S], src[:, 0:S - back], tap[3 - back], a[:, back:S], ALU.mult, ALU.add,
                                     step)
                ready[s] = a_act(dst(s), acc, ACT.Silu, step)
                conv_acc.give(i, ready[s])
                return [step]
            return evacuate

        xbc_ready = [None] * (XBC_T // 2)
        z_ready = [None] * (Z_T // 2)

        def evacuate_z(s, bank, done):
            z_ready[s] = a_act(pair(zT, s), bank[:, :], ACT.Silu, done)
            return [z_ready[s]]

        def projections_1():
            yield from project(t_in["w_q"], Q_T // 2, hT, h_ready, evacuate_q)
            yield from project(t_in["w_k"], K_T // 2, hT, h_ready, evacuate_k)
            yield from project_values(t_in["w_v"], val, hT, h_ready, v_ready)

        def projections_2():
            yield from project(t_in["w_xbc"], XBC_T // 2, hT, h_ready,
                               conv_silu("conv_w", XBC_T, lambda s: pair(xbcT, s), xbc_ready, "conv_b"))
            yield from project(t_in["w_z"], Z_T // 2, hT, h_ready, evacuate_z)

        drain(projections_1(), scoring())

        prob = Turns([take(512), take(512)])
        probT = Turns([take(512), take(512)])
        stats = Turns([take(8), take(8)])
        att_ready = []

        def attention():
            for qb in range(2):
                nk, nh = P * (qb + 1), 4 // (qb + 1)
                for h0 in range(0, ATT_HEADS, nh):
                    b, bank, bank_free = side_banks.take()
                    for j in range(nh):
                        h = h0 + j
                        done = mm(bank[:, j * nk:(j + 1) * nk], tile(qT, h)[:, qb * P:(qb + 1) * P],
                                  tile(kT, h // 2)[:, 0:nk], True, True, bank_free, q_ready[h // 2], k_ready[h // 4],
                                  signal=j == nh - 1)
                    i, pr, pr_free = prob.take()
                    si, st, st_free = stats.take()
                    masked = v_stt(split(pr, nh), split(bank[:, :], nh), SCALE, over(sel_neg[qb], nh), ALU.mult,
                                   ALU.add, done, pr_free, sel_ready[qb])
                    side_banks.give(b, masked)
                    top = v_red(st[:, 0:nh], split(pr, nh), ALU.max, masked, st_free, negate=True)
                    for j in range(nh):
                        e = a_act(pr[:, j * nk:(j + 1) * nk], pr[:, j * nk:(j + 1) * nk], ACT.Exp, top,
                                  bias=st[:, j:j + 1], accum=st[:, 4 + j:5 + j])
                    inv = v_rec(st[:, 4:4 + nh], st[:, 4:4 + nh], e)
                    normed = v_tt(split(pr, nh), split(pr, nh), wide(st[:, 4:4 + nh], nk), ALU.mult, inv)
                    stats.give(si, normed)
                    yield
                    b, bank, bank_free = side_banks.take()
                    for j in range(4):
                        turned = turn(bank[:, j * P:(j + 1) * P], pr[:, j * P:(j + 1) * P], normed, bank_free,
                                      signal=j == 3)
                    prob.give(i, turned)
                    i, pt, pt_free = probT.take()
                    copied = a_copy(pt, bank[:, :], turned, pt_free)
                    side_banks.give(b, copied)
                    b, bank, bank_free = side_banks.take()
                    for j in range(nh):
                        kv = (h0 + j) // 2
                        for c in range(qb + 1):
                            o = (j * (qb + 1) + c) * P
                            done = mm(bank[:, j * P:(j + 1) * P], val[:, c * 512 + kv * P:c * 512 + (kv + 1) * P],
                                      pt[:, o:o + P], c == 0, c == qb, copied, bank_free, v_ready,
                                      signal=j == nh - 1 and c == qb)
                    probT.give(i, done)
                    dst = split(mixT[:, (8 + h0) * S:(8 + h0 + nh) * S], nh)[:, :, qb * P:(qb + 1) * P]
                    t = a_copy(dst, split(bank[:, 0:nh * P], nh), done, (rows_sem, 16))
                    att_ready.append(t)
                    side_banks.give(b, t)
                    yield

        drain(attention(), projections_2())
        barrier()

        cursor[0] = 512
        state_T = take(1024)
        xdt = [take(1024), take(1024)]
        xds = take(1024)
        b_tok = take(2 * P)
        cbT = [[take(P), take(P)], [take(P), take(P)]]
        limit = 512 + Q_T * S + K_T * S + 2 * 512 + QI_T * S + 2 * S
        assert cursor[0] <= limit
        cursor[0] = keep
        dt, adt, acum, tmp = take(32), take(32), take(32), take(32)
        ea, dstate = take(16), take(16)
        decay = Turns([take(512), take(512)])
        c_decayed = Turns([take(512)])
        ysq = Turns([take(512), take(512)])
        sq, roots = ysq, Turns([take(512)])

        def softplus(out, x, t0, n, ready):
            t = a_act(t0, x, ACT.Abs, ready)
            t = a_act(t0, t0, ACT.Exp, t, scale=-1.0)
            t = a_act(t0, t0, ACT.Ln, t, bias=ones[:, 0:1])
            return v_stt(out, x, 0.0, t0, ALU.max, ALU.add, t)

        biased = v_tt(split(dt, 2), dtwi[:, :, 0:16], over(vec("dt_bias", 0, 16), 2), ALU.add, small_ready)
        dt_ready = softplus(dt, dt, tmp, 32, biased)
        ea_ready = a_act(ea, vec("a_log", 0, 16), ACT.Exp)
        adt_ready = v_stt(split(adt, 2), split(dt, 2), -1.0, over(ea, 2), ALU.mult, ALU.mult, dt_ready, ea_ready)
        b, bank, bank_free = side_banks.take()
        for c in range(2):
            mm(bank[:, 16 * c:16 * c + 16], mat("upto"), adt[:, 16 * c:16 * c + 16], True, True, bank_free, adt_ready)
        done = mm(bank[:, 32:48], ones[:, :], adt[:, 0:16], True, True, signal=True)
        acum_ready = v_copy(acum, bank[:, 0:32], done)
        t = v_tt(dstate, bank[:, 32:48], acum[:, 0:16], ALU.subtract, acum_ready)
        side_banks.give(b, t)
        ds_ready = a_act(dstate, dstate, ACT.Exp, t)
        xdt_ready = [[None, None], [None, None]]
        for c in range(2):
            for g in range(2):
                b, bank, bank_free = side_banks.take()
                for j in range(4):
                    done = turn(bank[:, j * P:(j + 1) * P], tile(xbcT, 4 * g + j)[:, c * P:(c + 1) * P], bank_free,
                                xbc_ready[2 * g + j // 2], signal=j == 3)
                dst = xdt[c][:, 512 * g:512 * g + 512]
                t = v_tt(split(dst, 8), split(bank[:, :], 8), wide(dt[:, 16 * c + 8 * g:16 * c + 8 * g + 8], 64),
                         ALU.mult, done, dt_ready)
                xdt_ready[c][g] = t
                side_banks.give(b, t)
                if c == 0:
                    xds_ready = v_tt(split(xds[:, 512 * g:512 * g + 512], 8), split(dst, 8),
                                     wide(dstate[:, 8 * g:8 * g + 8], 64), ALU.mult, t, ds_ready)
        b, bank, bank_free = side_banks.take()
        for g in range(2):
            done = turn(bank[:, g * P:(g + 1) * P], tile(xbcT, 8 + g)[:, 0:P], bank_free, xbc_ready[4],
                        signal=g == 1)
        b_ready = a_copy(b_tok, bank[:, 0:2 * P], done)
        side_banks.give(b, b_ready)
        b, bank, bank_free = side_banks.take()
        for g in range(2):
            for c in range(2):
                done = mm(bank[:, (2 * g + c) * P:(2 * g + c + 1) * P], tile(xbcT, 8 + g)[:, c * P:(c + 1) * P],
                          tile(xbcT, 10 + g)[:, c * P:(c + 1) * P], True, True, bank_free, xbc_ready[4:6],
                          signal=g + c == 2)
        for g in range(2):
            for c in range(2):
                cb_ready = a_copy(cbT[g][c], bank[:, (2 * g + c) * P:(2 * g + c + 1) * P], done)
        side_banks.give(b, cb_ready)
        for g in range(2):
            b, bank, bank_free = side_banks.take()
            done = mm(bank[:, :], b_tok[:, g * P:(g + 1) * P], xds[:, 512 * g:512 * g + 512], True, True, bank_free,
                      b_ready, xds_ready, signal=True)
            state_ready = a_copy(state_T[:, 512 * g:512 * g + 512], bank[:, :], done)
            side_banks.give(b, state_ready)
        y_ready = [[None] * 8, [None] * 8]
        for c in range(2):
            for q4 in range(4):
                g = q4 // 2
                b, bank, bank_free = side_banks.take()
                for j in range(4):
                    h = 4 * q4 + j
                    done = mm(bank[:, j * P:(j + 1) * P],
                              adt[:, 16 * c + h:16 * c + h + 1].to_broadcast([P, P]), mat("upto"), True, True,
                              bank_free, adt_ready, signal=j == 3)
                i, dec, dec_free = decay.take()
                t = v_tt(split(dec, 4), split(bank[:, :], 4),
                         wide(acum[:, 16 * c + 4 * q4:16 * c + 4 * q4 + 4], P), ALU.subtract, done, dec_free, acum_ready)
                readers = [t]
                if c == 1:
                    ci, cd, cd_free = c_decayed.take()
                    grown = a_act(cd, bank[:, :], ACT.Exp, t, cd_free)
                    readers.append(grown)
                    cd_ready = v_tt(split(cd, 4), split(cd, 4), over(tile(xbcT, 10 + g)[:, P:2 * P], 4), ALU.mult,
                                    grown)
                side_banks.give(b, *readers)
                t = v_tt(split(dec, 4), split(dec, 4), over(mat("neg_after"), 4), ALU.add, t)
                t = a_act(dec, dec, ACT.Exp, t)
                t = v_tt(split(dec, 4), split(dec, 4), over(cbT[g][c], 4), ALU.mult, t, cb_ready)
                b, bank, bank_free = side_banks.take()
                for j in range(2):
                    ch = 2 * q4 + j
                    out = bank[:, j * 2 * P:(j + 1) * 2 * P]
                    done = mm(out, xdt[c][:, ch * P:(ch + 1) * P], dec[:, j * 2 * P:(j + 1) * 2 * P], True, c == 0, t,
                              bank_free, xdt_ready[c][g], signal=j == 1)
                    if c == 1:
                        done = mm(out, state_T[:, ch * P:(ch + 1) * P], cd[:, j * 2 * P:(j + 1) * 2 * P], False, True,
                                  cd_ready, state_ready, signal=j == 1)
                decay.give(i, done)
                if c == 1:
                    c_decayed.give(ci, done)
                for j in range(2):
                    ch = 2 * q4 + j
                    for half in range(2):
                        p = slice(64 * half, 64 * half + 64)
                        xs = tile(xbcT, ch)[p, c * P:(c + 1) * P]
                        t = v_stt(xs, xs, vec("d_skip", ch)[p, :], bank[p, (2 * j + half) * P:(2 * j + half + 1) * P],
                                  ALU.mult, ALU.add, done, xdt_ready[c][g])
                    y_ready[c][ch] = t
                side_banks.give(b, t)
        for g in range(2):
            b, bank, bank_free = side_banks.take()
            for j in range(2):
                s = 2 * g + j
                t = v_tt(pair(zT, s), pair(zT, s), pair(xbcT, s), ALU.mult, z_ready[s], y_ready[1][2 * s + 1],
                         y_ready[0][2 * s + 1])
                i, buf, buf_free = ysq.take()
                squared = a_act(buf, pair(zT, s), ACT.Square, t, buf_free)
                mm(bank[:, 0:S], ones[:, :], buf[:, 0:S], j == 0, False, squared, bank_free)
                done = mm(bank[:, 0:S], ones[:, :], buf[:, S:2 * S], False, j == 1, signal=True)
                ysq.give(i, done)
            r, root, root_free = roots.take()
            ready, read = rstd(root, bank, S, 1.0 / (SSD_W // SSD_GROUPS), done, root_free)
            side_banks.give(b, read)
            for k in range(4 * g, 4 * g + 4):
                ssd_ready = v_stt(tile(mixT, k), tile(zT, k), vec("g_ssd", k), root[:, 0:S], ALU.mult, ALU.mult, ready)
            roots.give(r, ssd_ready)

        drain(project(t_in["w_out"], KD // 2, mixT, [ssd_ready] * 8 + [att_ready[-1]] * 8, residual(x_ready)))
        barrier()
        cursor[0] = 0
        mlp(t_in["w_up"], t_in["w_down"], "g_mlp", x_ready)
        now = barrier()

        cursor[0] = 0
        bias = take(NSA_HEADS * S)
        bias3 = split(bias, NSA_HEADS)
        pool.wait([(rows_sem, 16)])
        grid = bass.AP(tensor=bias_rows.tensor, offset=P - 1,
                       ap=[[NSA_HEADS * 2 * S - 1, P], [2 * S, NSA_HEADS], [1, S]])
        pool.items.append(lambda e: e.dma_start(bias3, grid).then_inc(toep_sem, 16))
        bias_ready = (toep_sem, 16)
        gdn_in = [take(3 * HALF_HEADS * S), None]
        gdn_z = [take(HALF_HEADS * S), None]
        keep2 = cursor[0]
        gab = take(80)
        qT = take(NSA_HEADS * S)
        kcvc = take(4 * S)
        kskw = take(4 * S)
        vsvw = take(2 * 512)
        sq = Turns([take(512), take(512)])
        roots = Turns([take(512)])
        conv_acc = Turns([take(512)])
        blocks = [take(CMP_BLOCK * 2 * N_CMP), take(CMP_BLOCK * 2 * N_CMP)]
        hid = [take(2 * 2 * N_CMP), take(2 * 2 * N_CMP)]
        kcmpT = take(2 * N_CMP)
        vcmp = take(2 * P)
        h_ready = norm("ln1", x_ready, sq, roots.bufs[0])

        b, bank, bank_free = side_banks.take()
        for c in range(2):
            for k in range(KD):
                done = mm(bank[:, 40 * c:40 * c + 40], tile(hT, k)[:, c * P:(c + 1) * P],
                          w_gab[:, 40 * k:40 * k + 40], k == 0, k == KD - 1, bank_free, h_ready[k],
                          signal=k == KD - 1)
        gab3 = split(gab, 2)
        gab_ready = v_copy(gab, bank[:, 0:80], done)
        side_banks.give(b, gab_ready)

        kv_ready = [None] * 4

        def evacuate_kv(s, bank, done):
            kv_ready[s] = a_copy(pair(kcvc, s) if s < 2 else pair(kskw, s - 2), bank[:, :], done)
            return [kv_ready[s]]

        nq_ready = [None] * 4

        def evacuate_nq(s, bank, done):
            nq_ready[s] = a_copy(pair(qT, s), bank[:, :], done)
            return [nq_ready[s]]

        vs_ready = []
        drain(project(t_in["w_kv"], 4, hT, h_ready, evacuate_kv))
        gates = take(48)
        gates_ready = a_act(split(gates, 2), gab3[:, :, 0:24], ACT.Sigmoid, gab_ready)
        beta = take(16)
        beta_ready = a_act(split(beta, 2), gab3[:, :, 32:40], ACT.Sigmoid, gab_ready)

        def compress():
            blk_ready = [None, None]
            for m in range(2):
                for g in range(2):
                    src = kcvc[:, (2 * m + g) * S:(2 * m + g + 1) * S].rearrange("p (m r) -> p r m", r=CMP_STRIDE)
                    dst = split(blocks[m], CMP_BLOCK)[:, :, g * N_CMP:(g + 1) * N_CMP]
                    for half in range(2):
                        rr = slice(half * CMP_STRIDE, (half + 1) * CMP_STRIDE)
                        pe_cols = vec(("pe_k", "pe_v")[m], half * CMP_STRIDE, CMP_STRIDE)
                        blk_ready[m] = v_tt(dst[:, rr, :], src[:, :, half:half + N_CMP], wide(pe_cols, N_CMP), ALU.add,
                                            kv_ready[m])
            yield
            n = 2 * N_CMP
            for m in range(2):
                b, bank, bank_free = side_banks.take()
                s0 = next_slot(t_in["w_cmp1"][2 * m])
                s1 = next_slot(t_in["w_cmp1"][2 * m + 1])
                for hh in range(2):
                    for r in range(CMP_BLOCK):
                        i, slot, slot_ready = (s0, s1)[r // 16]
                        o = (r % 16) * CMP_HID + hh * P
                        done = mm(bank[:, hh * n:(hh + 1) * n], slot[:, o:o + P], blocks[m][:, r * n:(r + 1) * n],
                                  r == 0, r == CMP_BLOCK - 1, slot_ready, bank_free, blk_ready[m], signal=r % 16 == 15)
                        if hh == 1 and r % 16 == 15:
                            freed[i] = done
                gelu = a_act(hid[m], bank[:, 0:2 * n], ACT.Gelu_apprx_tanh, done)
                side_banks.give(b, gelu)
                yield
                b, bank, bank_free = side_banks.take()
                if m == 0:
                    for hh in range(2):
                        done = mm(bank[:, 0:n], w_cmp2[:, hh * P:(hh + 1) * P], hid[0][:, hh * n:(hh + 1) * n],
                                  hh == 0, hh == 1, gelu, bank_free, signal=hh == 1)
                    cmp_ready.append(a_copy(kcmpT, bank[:, 0:n], done))
                else:
                    for g in range(2):
                        for hh in range(2):
                            done = mm(bank[0:N_CMP, g * P:(g + 1) * P],
                                      hid[1][:, hh * n + g * N_CMP:hh * n + (g + 1) * N_CMP],
                                      w_cmp2[:, (2 + hh) * P:(3 + hh) * P], hh == 0, hh == 1, gelu, bank_free,
                                      signal=g + hh == 2)
                    cmp_ready.append(a_copy(vcmp[0:N_CMP, :], bank[0:N_CMP, 0:2 * P], done))
                side_banks.give(b, cmp_ready[-1])
                yield

        cmp_ready = []

        def nsa_projections():
            yield from project(t_in["w_nq"], 4, hT, h_ready, evacuate_nq)
            yield from project_values(t_in["w_vsvw"], vsvw, hT, h_ready, vs_ready)

        drain(compress(), nsa_projections())

        gdn_ready = [[None] * 6, [None] * 6]
        gdn_z_ready = [[None] * 2, [None] * 2]

        def gdn_projections(half):
            def evacuate_z2(s, bank, done):
                gdn_z_ready[half][s] = a_act(pair(gdn_z[half], s), bank[:, :], ACT.Silu, done)
                return [gdn_z_ready[half][s]]

            def taps(s):
                return s
            yield from project(t_in[f"w_gdn{half}"], 6, hT, h_ready,
                               conv_silu2(half, lambda s: pair(gdn_in[half], s), gdn_ready[half]))
            yield from project(t_in[f"w_gz{half}"], 2, hT, h_ready, evacuate_z2)

        def conv_silu2(half, dst, ready):
            def evacuate(s, bank, done):
                i, acc, acc_free = conv_acc.take()
                for j in range(2):
                    t = 12 * half + 2 * s + j
                    src, a = bank[:, j * S:(j + 1) * S], acc[:, j * S:(j + 1) * S]
                    step = v_ts(a, src, vec("conv_w2", 3 * 24 + t), None, ALU.mult, None, done, acc_free)
                    for back in (1, 2, 3):
                        step = v_stt(a[:, back:S], src[:, 0:S - back], vec("conv_w2", (3 - back) * 24 + t),
                                     a[:, back:S], ALU.mult, ALU.add, step)
                ready[s] = a_act(dst(s), acc, ACT.Silu, step)
                conv_acc.give(i, ready[s])
                return [step]
            return evacuate

        p_cmp = [take(NSA_HEADS * 7), take(NSA_HEADS * N_CMP)]
        cst = take(3 * NSA_HEADS)
        pc_ready = [None, None]

        def compressed():
            for qb in range(2):
                nc_ = (7, N_CMP)[qb]
                b, bank, bank_free = side_banks.take()
                for h in range(NSA_HEADS):
                    g = h // 4
                    done = mm(bank[:, h * nc_:(h + 1) * nc_], tile(qT, h)[:, qb * P:(qb + 1) * P],
                              kcmpT[:, g * N_CMP:g * N_CMP + nc_], True, True, bank_free, nq_ready[h // 2],
                              cmp_ready[0], signal=h == NSA_HEADS - 1)
                pc = p_cmp[qb].rearrange("p (h n) -> p h n", h=NSA_HEADS)
                off = P - P * qb
                grid_c = bias3[:, :, off + 31:off + 31 + CMP_STRIDE * (nc_ - 1) + 1:CMP_STRIDE]
                t = v_stt(pc, bank[:, 0:NSA_HEADS * nc_].rearrange("p (h n) -> p h n", h=NSA_HEADS), SCALE, grid_c,
                          ALU.mult, ALU.add, done, bias_ready)
                side_banks.give(b, t)
                m, keep_m, s = cst[:, 0:8], cst[:, 8:16], cst[:, 16:24]
                t = v_red(m, pc, ALU.max, t, pc_ready[0])
                t = v_ts(keep_m, m, NEG / 10, None, ALU.is_gt, None, t)
                t = v_tt(m, m, keep_m, ALU.mult, t)
                t = v_tt(pc, pc, wide(m, nc_), ALU.subtract, t)
                t = a_act(p_cmp[qb], p_cmp[qb], ACT.Exp, t)
                t = v_red(s, pc, ALU.add, t)
                t = v_ts(s, s, 1e-30, None, ALU.max, None, t)
                t = v_rec(s, s, t)
                gate = gates[:, 24 * qb:24 * qb + 24].rearrange("p (h b) -> p h b", b=3)[:, :, 0]
                t = v_tt(s, s, gate, ALU.mult, t, gates_ready)
                pc_ready[qb] = v_tt(pc, pc, wide(s, nc_), ALU.mult, t)
                yield

        prob = Turns([take(512), take(512)])
        probT = Turns([take(640), take(640)])
        stats = Turns([take(4), take(4)])
        nsa_ready = []

        def nsa():
            for qb in range(2):
                nk, nc_, off = P * (qb + 1), (7, N_CMP)[qb], P - P * qb
                for h in range(NSA_HEADS):
                    g = h // 4
                    b, bank, bank_free = side_banks.take()
                    for br in range(2):
                        done = mm(bank[:, br * nk:(br + 1) * nk], tile(qT, h)[:, qb * P:(qb + 1) * P],
                                  tile(kskw, 2 * br + g)[:, 0:nk], True, True, bank_free, nq_ready[h // 2],
                                  kv_ready[2:4], signal=br == 1)
                    i, pr, pr_free = prob.take()
                    si, st, st_free = stats.take()
                    pr3 = split(pr[:, 0:2 * nk], 2)
                    t = v_stt(pr3, split(bank[:, 0:2 * nk], 2), SCALE, over(bias3[:, h, off:off + nk], 2), ALU.mult,
                              ALU.add, done, pr_free, bias_ready)
                    side_banks.give(b, t)
                    t = v_red(st[:, 0:2], pr3, ALU.max, t, st_free, negate=True)
                    for br in range(2):
                        e = a_act(pr3[:, br, :], pr3[:, br, :], ACT.Exp, t, bias=st[:, br:br + 1],
                                  accum=st[:, 2 + br:3 + br])
                    t = v_rec(st[:, 2:4], st[:, 2:4], e)
                    t = v_tt(st[:, 2:4], st[:, 2:4], gates[:, 24 * qb + 3 * h + 1:24 * qb + 3 * h + 3], ALU.mult, t,
                             gates_ready)
                    normed = v_tt(pr3, pr3, wide(st[:, 2:4], nk), ALU.mult, t)
                    stats.give(si, normed)
                    yield
                    b, bank, bank_free = side_banks.take()
                    blocks_n = 2 * (qb + 1)
                    for j in range(blocks_n):
                        turned = turn(bank[:, j * P:(j + 1) * P], pr[:, j * P:(j + 1) * P], normed, bank_free,
                                      signal=j == blocks_n - 1)
                    prob.give(i, turned)
                    bc, bank_c, bank_c_free = side_banks.take()
                    pc = p_cmp[qb].rearrange("p (h n) -> p h n", h=NSA_HEADS)
                    turned_c = turn(bank_c[0:nc_, 0:P], pc[:, h, :], pc_ready[qb], bank_c_free, signal=True)
                    i, pt, pt_free = probT.take()
                    t1 = a_copy(pt[:, 0:blocks_n * P], bank[:, 0:blocks_n * P], turned, pt_free)
                    t2 = v_copy(pt[0:nc_, 512:640], bank_c[0:nc_, 0:P], turned_c, pt_free)
                    side_banks.give(b, t1)
                    side_banks.give(bc, t2)
                    b, bank, bank_free = side_banks.take()
                    for j in range(blocks_n):
                        br, c = j // (qb + 1), j % (qb + 1)
                        mm(bank[:, 0:P], vsvw[:, c * 512 + br * S + g * P:c * 512 + br * S + (g + 1) * P],
                           pt[:, j * P:(j + 1) * P], j == 0, False, t1, bank_free, vs_ready)
                    done = mm(bank[:, 0:P], vcmp[0:nc_, g * P:(g + 1) * P], pt[0:nc_, 512:640], False, True, t2,
                              cmp_ready[1], signal=True)
                    probT.give(i, done)
                    t = a_copy(tile(mixT, h)[:, qb * P:(qb + 1) * P], bank[:, 0:P], done)
                    nsa_ready.append(t)
                    side_banks.give(b, t)
                    yield

        drain(compressed())
        drain(nsa(), gdn_projections(0))
        barrier()

        cursor[0] = 0
        spare = NSA_HEADS * S
        graw, gcum, glast, gtmp = take(16), take(16), take(16), take(16)
        ea2 = take(8)
        k_scale, kd_scale = take(16), take(16)
        state = take(HALF_HEADS * P)
        vb, kbg = take(512), take(512)
        assert cursor[0] <= spare
        cursor[0] = keep2
        gab2 = take(80)
        eg = take(HALF_HEADS * S)
        decT, LT, LTm, Xs = take(512), take(512), take(512), take(512)
        E_, D_ = take(512), take(512)
        qkT = [take(512), take(512)]
        kd = [take(512), take(512)]
        u = [take(512), take(512)]
        wT = [take(512), take(512)]
        assert cursor[0] <= ARENA
        sq = Turns([decT, LT])
        roots = Turns([LTm])
        beta2 = take(16)
        half_in = [gdn_in[0], take(3 * HALF_HEADS * S)]
        half_z = [gdn_z[0], take(HALF_HEADS * S)]
        gdn_in[1], gdn_z[1] = half_in[1], half_z[1]
        conv_acc = Turns([take(512)])
        beta_kept = v_copy(beta2, beta, beta_ready)
        bar = barrier()

        biased = v_tt(split(graw, 2), gab3[:, :, 24:32], over(vec("dt_bias2", 0, 8), 2), ALU.add, gab_ready, beta_kept)
        sp_ready = softplus(graw, graw, gtmp, 16, biased)
        ea_ready = a_act(ea2, vec("a_log2", 0, 8), ACT.Exp)
        graw_ready = v_stt(split(graw, 2), split(graw, 2), -1.0, over(ea2, 2), ALU.mult, ALU.mult, sp_ready, ea_ready)
        b, bank, bank_free = side_banks.take()
        mm(bank[:, 0:16], mat("upto64"), graw, True, True, graw_ready, bank_free)
        done = mm(bank[:, 16:32], mat("ones64"), graw, True, True, signal=True)
        gcum_ready = v_copy(gcum, bank[:, 0:16], done)
        t = v_tt(glast, bank[:, 16:32], gcum, ALU.subtract, gcum_ready)
        side_banks.give(b, t)
        kd_ready = a_act(kd_scale, glast, ACT.Exp, t)
        t = a_act(k_scale, gcum, ACT.Exp, gcum_ready)
        ks_ready = v_tt(k_scale, k_scale, beta2, ALU.mult, t, beta_kept)

        def delta_rule(half):
            qkv, z = gdn_in[half], gdn_z[half]
            in_ready, z_ok = gdn_ready[half], gdn_z_ready[half]
            nq, nk_, nv = qkv[:, 0:1024], qkv[:, 1024:2048], qkv[:, 2048:3072]
            h0 = HALF_HEADS * half
            unit = [None] * 4
            for s in range(4):
                src = pair(qkv, s)
                i, buf, buf_free = sq.take()
                r, root, root_free = roots.take()
                squared = a_act(buf, src, ACT.Square, in_ready[s], buf_free)
                b, total, total_free = side_banks.take()
                summed = sums(total, buf, 512, squared, total_free)
                sq.give(i, summed)
                ready, read = rstd(root, total, 512, 1.0, summed, root_free)
                side_banks.give(b, read)
                unit[s] = v_stt(src, src, SCALE if s < 2 else 1.0, root, ALU.mult, ALU.mult, ready)
                roots.give(r, unit[s])
                yield
            prepared = [None, None]
            for p in range(2):
                tok = slice(p * P, (p + 1) * P)
                col = slice(8 * p + h0, 8 * p + h0 + HALF_HEADS)
                b, bank, bank_free = side_banks.take()
                for j in range(HALF_HEADS):
                    c0 = 8 * p + h0 + j
                    done = mm(bank[:, j * P:(j + 1) * P], graw[:, c0:c0 + 1].to_broadcast([P, P]), mat("upto64"),
                              True, True, graw_ready, bank_free, signal=j == 3)
                t = v_tt(split(decT, 4), split(bank[:, :], 4), wide(gcum[:, col], P), ALU.subtract, done, gcum_ready,
                         unit)
                eg_p = split(eg, HALF_HEADS)[:, :, tok]
                grown = a_act(eg_p, split(bank[:, :], 4), ACT.Exp, t)
                side_banks.give(b, grown, t)
                t = v_tt(split(decT, 4), split(decT, 4), over(mat("neg_after64"), 4), ALU.add, t)
                dec_ready = a_act(decT, decT, ACT.Exp, t)
                bb, bank_b, bank_b_free = side_banks.take()
                for j in range(HALF_HEADS):
                    c0 = 8 * p + h0 + j
                    beta_done = mm(bank_b[:, j * P:(j + 1) * P], beta2[:, c0:c0 + 1].to_broadcast([P, P]),
                                   mat("ident"), True, True, bank_b_free, beta_kept, signal=j == 3)
                b, bank, bank_free = side_banks.take()
                for j in range(HALF_HEADS):
                    kj = tile(nk_, j)[:, tok]
                    done = mm(bank[:, j * P:(j + 1) * P], kj, kj, True, True, bank_free, unit, signal=j == 3)
                t = v_tt(LT, bank[:, :], decT, ALU.mult, done, dec_ready)
                side_banks.give(b, t)
                lt_ready = v_tt(LT, LT, bank_b[:, :], ALU.mult, t, beta_done)
                side_banks.give(bb, lt_ready)
                yield
                b, bank, bank_free = side_banks.take()
                for j in range(HALF_HEADS):
                    done = mm(bank[:, j * P:(j + 1) * P], tile(nk_, j)[:, tok], tile(nq, j)[:, tok], True, True,
                              bank_free, unit, signal=j == 3)
                qk_ready = v_tt(qkT[p], bank[:, :], decT, ALU.mult, done, dec_ready)
                side_banks.give(b, qk_ready)
                t = v_tt(split(E_, 4), split(LT, 4), over(mat("level1"), 4), ALU.mult, lt_ready)
                e_ready = v_tt(split(E_, 4), over(mat("ident"), 4), split(E_, 4), ALU.subtract, t)
                b, bank, bank_free = side_banks.take()
                for j in range(HALF_HEADS):
                    done = turn(bank[:, j * P:(j + 1) * P], E_[:, j * P:(j + 1) * P], e_ready, bank_free,
                                signal=j == 3)
                d_ready = a_copy(D_, bank[:, :], done)
                side_banks.give(b, d_ready)
                yield
                xe_done = None
                for b_size in LEVELS:
                    m_ready = v_tt(split(LTm, 4), split(LT, 4), over(mat(f"level{b_size}"), 4), ALU.mult, lt_ready,
                                   xe_done)
                    b, bank, bank_free = side_banks.take()
                    for j in range(HALF_HEADS):
                        q = slice(j * P, (j + 1) * P)
                        done = mm(bank[:, q], LTm[:, q], D_[:, q], True, True, m_ready, d_ready, bank_free,
                                  signal=j == 3)
                    x_ok = a_copy(Xs, bank[:, :], done, xe_done)
                    side_banks.give(b, x_ok)
                    b, bank, bank_free = side_banks.take()
                    for j in range(HALF_HEADS):
                        q = slice(j * P, (j + 1) * P)
                        xe_done = mm(bank[:, q], Xs[:, q], E_[:, q], True, True, x_ok, e_ready, bank_free,
                                     signal=j == 3)
                    if b_size != LEVELS[-1]:
                        b2, bank2, bank2_free = side_banks.take()
                        for j in range(HALF_HEADS):
                            q = slice(j * P, (j + 1) * P)
                            dx_done = mm(bank2[:, q], E_[:, q], Xs[:, q], True, True, x_ok, e_ready, bank2_free,
                                         signal=j == 3)
                        xe_done = dx_done
                        d_ready = v_tt(D_, D_, bank2[:, :], ALU.subtract, dx_done)
                        side_banks.give(b2, d_ready)
                    e_ready = v_tt(E_, E_, bank[:, :], ALU.subtract, xe_done)
                    side_banks.give(b, e_ready)
                    yield
                b, bank, bank_free = side_banks.take()
                for j in range(HALF_HEADS):
                    done = turn(bank[:, j * P:(j + 1) * P], tile(nk_, j)[:, tok], bank_free, unit, signal=j == 3)
                t1 = v_tt(split(kbg, 4), split(bank[:, :], 4), wide(k_scale[:, col], P), ALU.mult, done, ks_ready,
                          prepared[0])
                t2 = v_tt(split(kd[p], 4), split(bank[:, :], 4), wide(kd_scale[:, col], P), ALU.mult, done, kd_ready)
                side_banks.give(b, t2)
                b, bank, bank_free = side_banks.take()
                for j in range(HALF_HEADS):
                    done = turn(bank[:, j * P:(j + 1) * P], tile(nv, j)[:, tok], bank_free, in_ready[4:6],
                                signal=j == 3)
                t3 = v_tt(split(vb, 4), split(bank[:, :], 4), wide(beta2[:, col], P), ALU.mult, done, prepared[0])
                side_banks.give(b, t3)
                b, bank, bank_free = side_banks.take()
                for j in range(HALF_HEADS):
                    q = slice(j * P, (j + 1) * P)
                    done = mm(bank[:, q], E_[:, q], vb[:, q], True, True, e_ready, t3, bank_free, signal=j == 3)
                u_ok = a_copy(u[p], bank[:, :], done)
                side_banks.give(b, u_ok)
                b, bank, bank_free = side_banks.take()
                for j in range(HALF_HEADS):
                    q = slice(j * P, (j + 1) * P)
                    done = mm(bank[:, q], kbg[:, q], E_[:, q], True, True, e_ready, t1, bank_free, signal=j == 3)
                w_ok = a_copy(wT[p], bank[:, :], done)
                side_banks.give(b, w_ok)
                q3 = split(nq, HALF_HEADS)[:, :, tok]
                qg_ok = v_tt(q3, q3, eg_p, ALU.mult, grown, qk_ready)
                prepared[p] = [u_ok, w_ok, qg_ok, qk_ready, t2, done]
                yield
            o3 = split(nv, HALF_HEADS)
            o_ready = None
            state_ok = None
            for c in range(S // CHUNK):
                p, odd = c // 2, c % 2
                rows = slice(CHUNK * odd, CHUNK * odd + CHUNK)
                ready = prepared[p]
                if c:
                    b, bank, bank_free = side_banks.take()
                    for j in range(HALF_HEADS):
                        q = slice(j * P, (j + 1) * P)
                        done = mm(bank[:, q], wT[p][:, q], state[:, q], True, True, ready, state_ok, bank_free,
                                  signal=j == 3)
                    new_v = v_tt(u[p][rows, :], u[p][rows, :], bank[rows, :], ALU.subtract, done, ready, state_ok,
                                 o_ready)
                    side_banks.give(b, new_v)
                    ready = [ready, new_v]
                b, bank, bank_free = side_banks.take()
                for j in range(HALF_HEADS):
                    q = slice(j * P, (j + 1) * P)
                    out = bank[:, j * CHUNK:(j + 1) * CHUNK]
                    if c:
                        mm(out, state[:, q], tile(nq, j)[:, c * CHUNK:(c + 1) * CHUNK], True, False, ready, state_ok,
                           bank_free)
                    o_done = mm(out, u[p][:, q], qkT[p][:, j * P + CHUNK * odd:j * P + CHUNK * odd + CHUNK], c == 0,
                                True, ready, bank_free, signal=j == 3)
                o_ready = a_copy(o3[:, :, c * CHUNK:(c + 1) * CHUNK], split(bank[:, 0:4 * CHUNK], 4), o_done)
                side_banks.give(b, o_ready)
                if c < S // CHUNK - 1:
                    b, bank, bank_free = side_banks.take()
                    for j in range(HALF_HEADS):
                        q = slice(j * P, (j + 1) * P)
                        done = mm(bank[:, q], kd[p][rows, q], u[p][rows, q], True, True, ready, bank_free,
                                  signal=j == 3)
                    last = c * CHUNK + CHUNK - 1
                    for j in range(HALF_HEADS):
                        q = slice(j * P, (j + 1) * P)
                        if c == 0:
                            state_ok = v_copy(state[:, q], bank[:, q], done)
                        else:
                            state_ok = v_stt(state[:, q], state[:, q], eg[:, j * S + last:j * S + last + 1],
                                             bank[:, q], ALU.mult, ALU.add, done, state_ok)
                    side_banks.give(b, state_ok)
                yield
            for s in range(2):
                i, buf, buf_free = sq.take()
                r, root, root_free = roots.take()
                squared = a_act(buf, pair(nv, s), ACT.Square, o_ready, buf_free)
                b, total, total_free = side_banks.take()
                summed = sums(total, buf, 512, squared, total_free)
                sq.give(i, summed)
                ready, read = rstd(root, total, 512, 1.0 / P, summed, root_free)
                side_banks.give(b, read)
                t = v_stt(root, pair(nv, s), vec("gdn_norm"), root, ALU.mult, ALU.mult, ready)
                dst = mixT[:, (8 + h0 + 2 * s) * S:(8 + h0 + 2 * s + 2) * S]
                gdn_done.append(v_tt(dst, root, pair(z, s), ALU.mult, t, z_ok[s]))
                roots.give(r, gdn_done[-1])
                yield

        gdn_done = []
        drain(delta_rule(0), gdn_projections(1))
        barrier()
        drain(delta_rule(1))
        barrier()

        cursor[0] = 0
        merged = take(KD * S)
        ga, gb = Turns([take(512), take(512)]), Turns([take(512), take(512)])
        part = Turns([take(512), take(512)])
        merge_ready = [None] * KD

        for j in range(KD // 2):
            gate_tok = []
            for m in range(2):
                i, slot, slot_ready = next_slot(t_in["w_merge"][2 * j + m])
                b, bank, bank_free = gemm_banks.take()
                for c in range(2):
                    for k in range(KD):
                        o = (c * KD + k) * P
                        done = mm(bank[:, c * S:(c + 1) * S], slot[:, o:o + P], tile(hT, k), k == 0, k == KD - 1,
                                  slot_ready, bank_free, h_ready[k], signal=c == 1 and k == KD - 1)
                freed[i] = done
                gi, gbuf, g_free = (ga, gb)[m].take()
                t = a_act(gbuf, bank[:, :], ACT.Sigmoid, done, g_free)
                gemm_banks.give(b, t)
                gate_tok.append((gi, gbuf, t))
            i, slot, slot_ready = next_slot(t_in["w_papb"][j])
            prods = []
            for m in range(2):
                b, bank, bank_free = side_banks.take()
                for c in range(2):
                    for k in range(8):
                        o = ((2 * m + c) * 8 + k) * P
                        done = mm(bank[:, c * S:(c + 1) * S], slot[:, o:o + P], tile(mixT, 8 * m + k), k == 0, k == 7,
                                  slot_ready, bank_free, nsa_ready, gdn_done, signal=c == 1 and k == 7)
                prods.append((b, bank, done))
            freed[i] = done
            pi, pbuf, p_free = part.take()
            t1 = v_tt(pbuf, prods[0][1][:, :], gate_tok[0][1], ALU.mult, prods[0][2], gate_tok[0][2], p_free)
            side_banks.give(prods[0][0], t1)
            ga.give(gate_tok[0][0], t1)
            t2 = v_tt(pair(merged, j), prods[1][1][:, :], gate_tok[1][1], ALU.mult, prods[1][2], gate_tok[1][2])
            side_banks.give(prods[1][0], t2)
            gb.give(gate_tok[1][0], t2)
            t3 = v_tt(pair(merged, j), pair(merged, j), pbuf, ALU.add, t1, t2)
            part.give(pi, t3)
            merge_ready[2 * j] = merge_ready[2 * j + 1] = t3

        drain(project(t_in["w_o"], KD // 2, merged, merge_ready, residual(x_ready)))
        barrier()
        cursor[0] = 0
        mlp(t_in["w_up2"], t_in["w_down2"], "ln2", x_ready)
        barrier()
        cursor[0] = 0
        sq = Turns([take(512), take(512)])
        y_tok = norm("ln_f", x_ready, sq, take(S))
        for j in range(4):
            sp.wait([y_tok[4 * j + 3]])
            sp.items.append(lambda e, j=j: e.dma_start(x_out[:, j * 1024:(j + 1) * 1024],
                                                       hT[:, j * 1024:(j + 1) * 1024]).then_inc(out_sem, 16))
        sp.wait([(out_sem, 64), (rows_sem, 16)])

        block = ctx.enter_context(nc.Block())

        @block.sync
        def _(e):
            sp.run(e)

        @block.tensor
        def _(e):
            pe.run(e)

        @block.vector
        def _(e):
            dve.run(e)

        @block.scalar
        def _(e):
            act.run(e)

        @block.gpsimd
        def _(e):
            pool.run(e)


def col_slots(w, k_tiles, cols):
    n = w.shape[1] // P // cols
    return np.ascontiguousarray(w.reshape(k_tiles, P, n, cols, P).transpose(2, 1, 3, 0, 4)).reshape(n, P, -1)


def row_tiles(w, k_tiles):
    return np.ascontiguousarray(w.reshape(k_tiles, P, -1).transpose(1, 0, 2)).reshape(P, -1)


def channels(v):
    return np.ascontiguousarray(v.reshape(-1, P).T)


def everywhere(v):
    return np.broadcast_to(v.reshape(1, -1), (P, v.size))


def kernel(**inputs):
    import numpy as _np
    import concourse.bacc as _bacc
    from concourse import mybir as _mybir
    from concourse.bass_utils import run_bass_kernel_spmd as _run

    a = {k: _np.asarray(v) for k, v in inputs.items()}
    w_in, w_in2 = a["w_in"][0], a["w_in_2"][0]
    at, cut = 0, {}
    for name, n in (("z", 1024), ("xbc", 1536), ("dt", 16), ("q", 1024), ("k", 512), ("v", 512), ("qi", 1024),
                    ("ki", 64), ("wi", 16)):
        cut[name] = w_in[:, at:at + n]
        at += n
    at = 0
    for name, n in (("nq", 1024), ("kv", 1536), ("gate", 24), ("qkv", 3072), ("gz", 1024), ("a", 8), ("b", 8),
                    ("merge", 4096)):
        cut[name] = w_in2[:, at:at + n]
        at += n
    kv = [cut["kv"][:, 256 * i:256 * i + 256] for i in range(6)]
    half = [_np.concatenate([cut["qkv"][:, 1024 * m + 512 * h:1024 * m + 512 * h + 512] for m in range(3)], axis=1)
            for h in range(2)]
    conv2 = a["conv_w_2"][0]
    conv2 = _np.concatenate([conv2[:, 1024 * m + 512 * h:1024 * m + 512 * h + 512] for h in range(2)
                             for m in range(3)], axis=1)
    merge = [col_slots(cut["merge"][:, 2048 * m:2048 * m + 2048], KD, 2) for m in range(2)]
    papb = [col_slots(a[n][0], 8, 2) for n in ("w_pa_2", "w_pb_2")]
    down = lambda w: _np.ascontiguousarray(
        w.reshape(2, 32, P, KD, P).transpose(3, 0, 2, 1, 4)).reshape(2 * KD, P, SLOT)
    mats, hot = constants()
    vec_parts = dict(
        g_mix=channels(a["g_mix"][0]), g_ssd=channels(a["g_ssd"][0]), g_q=channels(a["g_q"][0]),
        g_k=channels(a["g_k"][0]), g_ki=channels(_np.concatenate([a["g_kidx"][0], a["g_kidx"][0]])),
        conv_w=channels(a["conv_w"][0]), conv_b=channels(a["conv_b"][0]),
        d_skip=channels(_np.repeat(a["d_skip"][0], 64)), dt_bias=everywhere(a["dt_bias"][0]),
        a_log=everywhere(a["a_log"][0]), g_mlp=channels(a["g_mlp"][0]), ln1=channels(a["ln1_w_2"][0]),
        conv_w2=channels(conv2), a_log2=everywhere(a["a_log_2"][0]), dt_bias2=everywhere(a["dt_bias_2"][0]),
        gdn_norm=channels(a["gdn_norm_w_2"][0]), ln2=channels(a["ln2_w_2"][0]), ln_f=channels(a["ln_f_w_2"]),
        pe_k=a["cmp_pe_k_2"][0].T, pe_v=a["cmp_pe_v_2"][0].T)
    arrays = {
        "x": row_tiles(a["x"][0].T, KD),
        "vecs": _np.concatenate([vec_parts[n] for n in VECS], axis=1),
        "mats": mats,
        "hot": hot,
        "rel": _np.concatenate([a["rel_table_2"], _np.full((1, NSA_HEADS), NEG, _np.float32)], axis=0),
        "w_dtwi": row_tiles(_np.concatenate([cut["dt"], cut["wi"]], axis=1), KD),
        "w_gab": row_tiles(_np.concatenate([cut["gate"], cut["a"], cut["b"]], axis=1), KD),
        "w_cmp2": _np.concatenate([row_tiles(a["cmp_w2_k_2"][0], 2), row_tiles(a["cmp_w2_v_2"][0], 2)], axis=1),
        "w_ki": col_slots(_np.concatenate([cut["ki"], cut["ki"]], axis=1), KD, 1),
        "w_qi": col_slots(cut["qi"], KD, 2),
        "w_q": col_slots(cut["q"], KD, 2),
        "w_k": col_slots(cut["k"], KD, 2),
        "w_v": _np.stack([row_tiles(cut["v"][0:1024], 8), row_tiles(cut["v"][1024:2048], 8)]),
        "w_xbc": col_slots(cut["xbc"], KD, 2),
        "w_z": col_slots(cut["z"], KD, 2),
        "w_out": col_slots(a["w_out"][0], KD, 2),
        "w_up": col_slots(a["w_up"][0], KD, 2),
        "w_down": down(a["w_down"][0]),
        "w_kv": col_slots(_np.concatenate([kv[0], kv[1], kv[2], kv[4]], axis=1), KD, 2),
        "w_nq": col_slots(cut["nq"], KD, 2),
        "w_vsvw": _np.stack([row_tiles(_np.concatenate([kv[3][r:r + 1024], kv[5][r:r + 1024]], axis=1), 8)
                             for r in (0, 1024)]),
        "w_cmp1": _np.concatenate([row_tiles(a[n][0], 32).reshape(P, 2, SLOT).transpose(1, 0, 2)
                                   for n in ("cmp_w1_k_2", "cmp_w1_v_2")]),
        "w_gdn0": col_slots(half[0], KD, 2),
        "w_gdn1": col_slots(half[1], KD, 2),
        "w_gz0": col_slots(cut["gz"][:, 0:512], KD, 2),
        "w_gz1": col_slots(cut["gz"][:, 512:1024], KD, 2),
        "w_merge": _np.stack(merge, axis=1).reshape(KD, P, SLOT),
        "w_papb": _np.concatenate(papb, axis=2),
        "w_o": col_slots(a["w_o_2"][0], KD, 2),
        "w_up2": col_slots(a["w_up_2"][0], KD, 2),
        "w_down2": down(a["w_down_2"][0]),
    }
    nc = _bacc.Bacc("TRN2", target_bir_lowering=False, num_devices=1)
    t_in, feed = {}, {}
    for name, v in arrays.items():
        v = _np.ascontiguousarray(v)
        feed[f"in_{name}"] = v
        t_in[name] = nc.dram_tensor(f"in_{name}", v.shape, _mybir.dt.float32, kind="ExternalInput").ap()
    x_out = nc.dram_tensor("x_out", (P, KD * S), _mybir.dt.float32, kind="ExternalOutput").ap()
    bias_rows = nc.dram_tensor("bias_rows", (P, NSA_HEADS * 2 * S), _mybir.dt.float32).ap()
    build(nc, t_in, x_out, bias_rows)
    r = _run(nc, [feed], core_ids=[0])
    y = r.results[0]["x_out"]
    return _np.ascontiguousarray(y.reshape(P, KD, S).transpose(2, 1, 0).reshape(1, S, D))
```

```python
from contextlib import ExitStack

import numpy as np

import concourse.bass as bass
from concourse import mybir

F32 = mybir.dt.float32
F32R = mybir.dt.float32r
ALU = mybir.AluOpType
ACT = mybir.ActivationFunctionType
AX_X = mybir.AxisListType.X

P = 128
D = 2048
S = 256
KD = D // P
FF = 4 * D
EPS = 1e-6
NEG = -1e30
PICKED = -3e38

SSD_W, SSD_HEADS, SSD_GROUPS = 1024, 16, 2
CONV_TAPS = 4
XBC = 1536
ATT_HEADS, ATT_KV = 8, 4
IDX_HEADS, IDX_DIM, TOPK = 16, 64, 64
Z_T, XBC_T, Q_T, K_T, QI_T = 8, 12, 8, 4, 8
NSA_HEADS, NSA_GROUPS = 8, 2
CMP_STRIDE, CMP_BLOCK, N_CMP, CMP_HID = 16, 32, 15, 256
GDN_HEADS, CHUNK = 8, 64
HALF_HEADS = 4
REL_BUCKETS = 32
SCALE = float(P) ** -0.5

PIECE = 2048
UNIT = 1024
UNIT_K = UNIT // P
PIECES = 4
UNITS = 4
ARENA = 18128
X_AT = ARENA - KD * S

VECS = dict(g_mix=16, g_ssd=8, g_q=1, g_k=1, g_ki=1, conv_w=48, conv_b=12, d_skip=8, dt_bias=16, a_log=16,
            g_mlp=16, ln1=16, conv_w2=96, a_log2=8, dt_bias2=8, gdn_norm=1, ln2=16, ln_f=16, pe_k=32, pe_v=32)
MATS = ["ident", "upto", "upto64", "ones64", "neg_after", "neg_after64", "neg_before"] + [
    f"level{b}" for b in (1, 2, 4, 8, 16, 32)]
LEVELS = (2, 4, 8, 16, 32)


def constants():
    i = np.arange(P)
    r, c = i[:, None], i[None, :]
    same = (r // CHUNK) == (c // CHUNK)
    m = {
        "ident": r == c,
        "upto": r <= c,
        "upto64": (r <= c) & same,
        "ones64": same,
        "neg_after": np.where(r <= c, 0.0, NEG),
        "neg_after64": np.where((r <= c) & same, 0.0, NEG),
        "neg_before": np.where(c <= r, 0.0, NEG),
    }
    for b in (1, 2, 4, 8, 16, 32):
        m[f"level{b}"] = (r // (2 * b) == c // (2 * b)) & (r % (2 * b) < b) & (c % (2 * b) >= b)
    mats = np.concatenate([np.asarray(m[n], np.float32) for n in MATS], axis=1)
    dist = (S - 1) - np.arange(2 * S)
    exact = REL_BUCKETS // 2
    near = np.maximum(dist, 1).astype(np.float32)
    far = exact + (np.log(near / exact) / np.log(np.float32(P / exact)) * (REL_BUCKETS - exact)).astype(np.int32)
    bucket = np.where(dist < exact, np.maximum(dist, 0), np.minimum(far, REL_BUCKETS - 1))
    hot = np.zeros((REL_BUCKETS + 1, 2 * S), np.float32)
    for j in range(2 * S):
        hot[bucket[j] if dist[j] >= 0 else REL_BUCKETS, j] = 1.0
    return mats, hot


class Engine:

    def __init__(self, sem):
        self.sem, self.count, self.items, self.seen = sem, 0, [], {}

    def wait(self, tokens):
        for t in tokens:
            if t is None:
                continue
            if isinstance(t, list):
                self.wait(t)
                continue
            sem, value = t
            if self.seen.get(id(sem), 0) < value:
                self.seen[id(sem)] = value
                self.items.append(lambda e, sem=sem, value=value: e.wait_ge(sem, value))

    def do(self, step, *after, signal=True):
        self.wait(after)
        if signal:
            self.count += 1
            self.items.append(lambda e: step(e).then_inc(self.sem, 1))
            return (self.sem, self.count)
        self.items.append(step)
        return None

    def run(self, e):
        for item in self.items:
            item(e)


def build(nc, t_in, x_out, bias_rows, x_kept):
    ctx = ExitStack()
    with ctx:
        def sb(name, shape):
            return ctx.enter_context(nc.sbuf_tensor(name, shape, F32))

        def sem(name):
            return ctx.enter_context(nc.semaphore(name))

        engine_sems = [sem(f"{n}_steps") for n in ("pe", "dve", "act", "pool", "sp")]

        def sb_r(name, shape):
            return ctx.enter_context(nc.sbuf_tensor(name, shape, F32R))

        ring = sb("weight_ring", [P, PIECES, PIECE])
        w_split = (sb_r("w_hi", [P, UNITS, UNIT]), sb_r("w_lo", [P, UNITS, UNIT]))
        hn = (sb_r("h_hi", [P, KD * S]), sb_r("h_lo", [P, KD * S]))
        mix = (sb_r("mix_hi", [P, KD * S]), sb_r("mix_lo", [P, KD * S]))
        mats = sb("const_mats", [P, len(MATS) * P])
        ones = sb("ones", [P, P])
        vecs = sb("vecs", [P, sum(VECS.values())])
        eps = sb("eps", [P, 1])
        arena = sb("arena", [P, ARENA])
        xT = arena[:, X_AT:ARENA]
        psum = [ctx.enter_context(nc.psum_tensor(f"bank{i}", [P, 512], F32)) for i in range(8)]

        piece_sem = [sem(f"piece_loaded{i}") for i in range(PIECES)]
        cmp2_sem = sem("w_cmp2_loaded")
        x_saved_sem = sem("x_saved")
        x_back_sem = sem("x_back")
        param_sem = sem("params_loaded")
        x_sem = sem("x_loaded")
        rows_sem = sem("bias_rows_written")
        toep_sem = sem("bias_grid_loaded")
        out_sem = sem("out_written")

        def emit(plan):
            pe, dve, act, pool, sp = [Engine(s) for s in engine_sems]

            def mat(name):
                i = MATS.index(name)
                return mats[:, i * P:(i + 1) * P]

            vec_at = {}
            at = 0
            for name, w in VECS.items():
                vec_at[name] = at
                at += w

            def vec(name, i=0, n=1):
                return vecs[:, vec_at[name] + i:vec_at[name] + i + n]

            def pair(buf, j):
                return buf[:, 2 * j * S:(2 * j + 2) * S]

            def tile(buf, k):
                return buf[:, k * S:(k + 1) * S]

            cursor = [0]

            def take(n):
                a = cursor[0]
                cursor[0] += n
                assert cursor[0] <= ARENA, cursor[0]
                return arena[:, a:a + n]

            def barrier():
                now = [(e.sem, e.count) for e in (pe, dve, act, pool) if e.count]
                for e in (pe, dve, act, pool):
                    e.wait([t for t in now if t[0] is not e.sem or e is not pe])
                return now

            class Turns:

                def __init__(self, bufs):
                    self.bufs, self.free, self.n = bufs, [None] * len(bufs), 0

                def take(self):
                    i = self.n % len(self.bufs)
                    self.n += 1
                    return i, self.bufs[i], self.free[i]

                def give(self, i, *tokens):
                    self.free[i] = list(tokens)

            gemm_banks = Turns([psum[i] for i in (0, 1, 2)])
            side_banks = Turns([psum[i] for i in (3, 4, 5, 6, 7)])

            def mm(out, lhsT, rhs, start, stop, *after, signal=False):
                return pe.do(lambda e: nc.tensor.matmul(out, lhsT, rhs, start=start, stop=stop), *after, signal=signal)

            def turn(out, src, *after, signal=False):
                k = src.shape[0]
                return pe.do(lambda e: nc.tensor.transpose(out, src, mat("ident")[0:k, 0:k]), *after, signal=signal)

            def v_tt(out, a, b, op, *after):
                return dve.do(lambda e: nc.vector.tensor_tensor(out, a, b, op), *after)

            def v_ts(out, a, s1, s2, op0, op1, *after):
                if op1 is None:
                    return dve.do(lambda e: nc.vector.tensor_scalar(out, a, s1, None, op0), *after)
                return dve.do(lambda e: nc.vector.tensor_scalar(out, a, s1, s2, op0, op1), *after)

            def v_stt(out, a, s, b, op0, op1, *after):
                return dve.do(lambda e: nc.vector.scalar_tensor_tensor(out=out, in0=a, scalar=s, in1=b, op0=op0, op1=op1),
                              *after)

            def v_rec(out, a, *after):
                return dve.do(lambda e: nc.vector.reciprocal(out, a), *after)

            def v_copy(out, a, *after):
                return dve.do(lambda e: nc.vector.tensor_copy(out, a), *after)

            def v_red(out, a, op, *after, negate=None):
                return dve.do(lambda e: nc.vector.tensor_reduce(out, a, AX_X, op, negate=negate), *after)

            def a_act(out, a, func, *after, scale=1.0, bias=0.0, accum=None):
                kw = {} if accum is None else dict(accum_out=accum)
                return act.do(lambda e: nc.scalar.activation(out, a, func, bias=bias, scale=scale, **kw), *after)

            def a_copy(out, a, *after):
                return act.do(lambda e: nc.scalar.copy(out, a), *after)

            def wide(ap, n):
                return ap.unsqueeze(2).to_broadcast([ap.shape[0], ap.shape[1], n])

            def over(ap, n):
                return ap.unsqueeze(1).to_broadcast([ap.shape[0], n, ap.shape[1]])

            def split(ap, n):
                return ap.rearrange("p (a b) -> p a b", a=n)

            order = []
            planned = order if plan is None else plan
            ahead = 1 if plan is None else UNITS
            stream = dict(loaded=0, split=0, used=0)
            piece_free, unit_free, unit_ready = [None] * PIECES, [None] * UNITS, [None] * UNITS

            def load_next():
                n = stream["loaded"]
                if n < len(planned):
                    i, src = n % PIECES, planned[n]
                    sp.wait([piece_free[i]])
                    sp.items.append(lambda e: e.dma_start(ring[:, i, :], src).then_inc(piece_sem[i], 16))
                    stream["loaded"] += 1

            def split_next():
                u = stream["split"]
                n, i = u // 2, u % UNITS
                while stream["loaded"] <= n:
                    load_next()
                loaded = (piece_sem[n % PIECES], 16 * (n // PIECES + 1))
                src = ring[:, n % PIECES, (u % 2) * UNIT:(u % 2 + 1) * UNIT]
                hi, lo = w_split[0][:, i, :], w_split[1][:, i, :]
                high = a_copy(hi, src, loaded, unit_free[i])
                unit_ready[i] = v_tt(lo, src, hi.bitcast(F32), ALU.subtract, high, loaded, unit_free[i])
                stream["split"] += 1
                if u % 2:
                    piece_free[n % PIECES] = unit_ready[i]
                    load_next()

            def weights(src):
                u = stream["used"]
                if u % 2 == 0:
                    order.append(src)
                stream["used"] += 1
                while stream["split"] < min(u + ahead, 2 * len(planned)):
                    split_next()
                i = u % UNITS
                return i, (w_split[0][:, i, :], w_split[1][:, i, :]), unit_ready[i]

            def products(out, lhsT, rhs, first, last, *after, signal=False):
                mm(out, lhsT[0], rhs[0], first, False, *after)
                mm(out, lhsT[0], rhs[1], False, False)
                return mm(out, lhsT[1], rhs[0], False, last, signal=signal)

            def store_split(parts, src, *after):
                high = a_copy(parts[0], src, *after)
                return v_tt(parts[1], src, parts[0].bitcast(F32), ALU.subtract, high, *after)

            def both(x, a, b):
                return (x[0][:, a:b], x[1][:, a:b])

            def column(out, w, rhs, ready, k_tiles, *after):
                for k in range(k_tiles):
                    if k % UNIT_K == 0:
                        i, unit, split_done = weights(w(k // UNIT_K))
                    o = (k % UNIT_K) * P
                    done = products(out, [part[:, o:o + P] for part in unit], rhs(k), k == 0, k == k_tiles - 1,
                                    split_done, ready[k], *after, signal=k % UNIT_K == UNIT_K - 1)
                    if k % UNIT_K == UNIT_K - 1:
                        unit_free[i] = done
                return done

            def project(w, tiles, x, x_ready, evacuate, first=0):
                for s in range((tiles + 1) // 2):
                    b, bank, bank_free = gemm_banks.take()
                    for j in range(min(2, tiles - 2 * s)):
                        if j:
                            yield
                        done = column(bank[:, j * S:(j + 1) * S], lambda u: w[first + 2 * s + j],
                                      lambda k: both(x, k * S, (k + 1) * S), x_ready, KD, bank_free)
                    gemm_banks.give(b, *evacuate(s, bank, done))
                    yield

            def project_tokens(w, width, n, x, x_ready, evacuate):
                banks = [gemm_banks.take() for _ in range(2)]
                per_unit = UNIT // width
                for k in range(KD):
                    if k % per_unit == 0:
                        i, unit, split_done = weights(w(k // per_unit))
                    o = (k % per_unit) * width
                    last = k % per_unit == per_unit - 1
                    for c in range(2):
                        done = products(banks[c][1][:, 0:n], both(x, k * S + c * P, k * S + (c + 1) * P),
                                        [part[:, o:o + n] for part in unit], k == 0, k == KD - 1, split_done,
                                        banks[c][2], x_ready[k], signal=last)
                    if last:
                        unit_free[i] = done
                for c in range(2):
                    gemm_banks.give(banks[c][0], evacuate(c, banks[c][1], done))

            def values(w, out, x, x_ready, ready):
                def evacuate(c, bank, done):
                    ready.append(a_copy(out[:, c * 512:(c + 1) * 512], bank[:, :], done))
                    return ready[-1]
                project_tokens(lambda u: w[u // 2], 512, 512, x, x_ready, evacuate)
                yield

            def sums(bank, src, n, *after):
                return mm(bank[:, 0:n], ones[:, :], src, True, True, *after, signal=True)

            def rstd(out, bank, n, scale, *after):
                root = a_act(out[:, 0:n], bank[:, 0:n], ACT.Sqrt, *after, scale=scale, bias=eps[:, 0:1])
                return v_rec(out[:, 0:n], out[:, 0:n], root), root

            def norm(gain, x_ready, sq, root_buf, out=None):
                b, bank, bank_free = side_banks.take()
                for j in range(KD // 2):
                    i, buf, buf_free = sq.take()
                    squared = a_act(buf, pair(xT, j), ACT.Square, x_ready[j], buf_free)
                    mm(bank[:, 0:S], ones[:, :], buf[:, 0:S], j == 0, False, squared, bank_free)
                    done = mm(bank[:, 0:S], ones[:, :], buf[:, S:2 * S], False, j == KD // 2 - 1, signal=True)
                    sq.give(i, done)
                ready, read = rstd(root_buf, bank, S, 1.0 / D, done)
                side_banks.give(b, read)
                if out is not None:
                    return [v_stt(tile(out, k), tile(xT, k), vec(gain, k), root_buf[:, 0:S], ALU.mult, ALU.mult, ready)
                            for k in range(KD)]
                tokens = []
                for j in range(KD // 2):
                    i, buf, buf_free = sq.take()
                    for k in (2 * j, 2 * j + 1):
                        t = v_stt(buf[:, (k % 2) * S:(k % 2 + 1) * S], tile(xT, k), vec(gain, k), root_buf[:, 0:S],
                                  ALU.mult, ALU.mult, ready, buf_free)
                    t = store_split(both(hn, 2 * j * S, 2 * (j + 1) * S), buf, t)
                    sq.give(i, t)
                    tokens += [t, t]
                return tokens

            def head_norm(out, bank, gains, done, sq, roots, scale=1.0 / P, factor=None):
                i, buf, buf_free = sq.take()
                r, root, root_free = roots.take()
                squared = a_act(buf, bank, ACT.Square, done, buf_free)
                b, total, total_free = side_banks.take()
                summed = sums(total, buf, 512, squared, total_free)
                sq.give(i, summed)
                ready, read = rstd(root, total, 512, scale, summed, root_free)
                side_banks.give(b, read)
                t = v_stt(out, bank, gains if factor is None else factor, root, ALU.mult, ALU.mult, ready)
                roots.give(r, t)
                return t

            def residual(x_ready):
                def evacuate(s, bank, done):
                    t = v_tt(pair(xT, s), pair(xT, s), bank[:, :], ALU.add, done, x_ready[s])
                    x_ready[s] = t
                    return [t]
                return evacuate

            def drain(*gens):
                gens = list(gens)
                while gens:
                    for g in list(gens):
                        try:
                            next(g)
                        except StopIteration:
                            gens.remove(g)

            def mlp(w_up, w_down, gain, x_ready):
                sq = Turns([take(512), take(512)])
                root = take(S)
                relu = Turns([take(512), take(512), take(512)])
                h_ready = norm(gain, x_ready, sq, root)
                add = residual(x_ready)
                u_ready = [None] * KD

                def squared_relu(s, bank, done):
                    i, buf, buf_free = relu.take()
                    r = a_act(buf, bank[:, :], ACT.Relu, done, buf_free)
                    t = v_tt(buf, buf, buf, ALU.mult, r)
                    t = store_split(both(mix, 2 * s * S, 2 * (s + 1) * S), buf, t)
                    relu.give(i, t)
                    u_ready[2 * s] = u_ready[2 * s + 1] = t
                    return [r]

                for f in range(FF // D):
                    drain(project(w_up, KD, hn, h_ready, squared_relu, first=f * KD))
                    drain(project(w_down, KD, mix, u_ready, add, first=f * KD))

            hot, rel = arena[0:REL_BUCKETS + 1, 0:2 * S], arena[0:REL_BUCKETS + 1, 2 * S:2 * S + NSA_HEADS]
            for dst, name in ((vecs[:, :], "vecs"), (mats[:, :], "mats"), (hot, "hot"), (rel, "rel")):
                act.items.append(lambda e, dst=dst, name=name: e.dma_start(dst, t_in[name]).then_inc(param_sem, 16))
            params = (param_sem, 16 * 4)
            x_ready = [(x_sem, 16)] * (KD // 2)
            sp.items.append(lambda e: e.dma_start(xT, t_in["x"]).then_inc(x_sem, 16))
            ones_ready = pool.do(lambda e: nc.gpsimd.memset(ones[:, :], 1.0))
            eps_ready = pool.do(lambda e: nc.gpsimd.memset(eps[:, :], EPS))
            for e in (pe, dve, act):
                e.wait([params, ones_ready, eps_ready])
            pool.wait([params])

            rows = arena[:, X_AT - 5120:X_AT - 1024]
            for hd in range(NSA_HEADS):
                b, bank, bank_free = side_banks.take()
                rows_done = mm(bank[:, :], rel[:, hd:hd + 1].to_broadcast([REL_BUCKETS + 1, P]), hot, True, True,
                               bank_free, signal=True)
                rows_copied = v_copy(rows[:, 512 * hd:512 * hd + 512], bank[:, :], rows_done)
                side_banks.give(b, rows_copied)
            pool.wait([rows_copied])
            pool.items.append(lambda e: e.dma_start(bias_rows, rows).then_inc(rows_sem, 16))

            qT, kT = arena[:, X_AT:X_AT + Q_T * S], arena[:, X_AT + Q_T * S:X_AT + (Q_T + K_T) * S]
            val = arena[:, X_AT + (Q_T + K_T) * S:ARENA]
            xbcT = arena[:, X_AT - XBC_T * S:X_AT]
            zT = arena[:, X_AT - (XBC_T + Z_T) * S:X_AT - XBC_T * S]
            work_end = X_AT - (XBC_T + Z_T) * S
            small = take(2 * 32)
            qiT, kiT = take(QI_T * S), take(2 * S)
            sq = Turns([take(512), take(512)])
            roots = Turns([take(512)])
            conv_acc = Turns([take(512)])
            h_ready = norm("g_mix", x_ready, sq, roots.bufs[0])

            dtwi = split(small, 2)

            def evacuate_small(c, bank, done):
                small_tokens.append(v_copy(small[:, 32 * c:32 * c + 32], bank[:, 0:32], done))
                return small_tokens[-1]

            small_tokens = []
            project_tokens(lambda u: t_in["w_dtwi"][0], P, 32, hn, h_ready, evacuate_small)
            small_ready = small_tokens[-1]

            ki_clear = dve.do(lambda e: nc.vector.memset(kiT, 0.0))
            ki_ready = []

            def evacuate_ki(s, bank, done):
                i, buf, buf_free = sq.take()
                r, root, root_free = roots.take()
                squared = a_act(buf[:, 0:S], bank[:, 0:S], ACT.Square, done, buf_free)
                bb, total, total_free = side_banks.take()
                summed = sums(total, buf[:, 0:S], S, squared, total_free)
                sq.give(i, summed)
                ready, read = rstd(root, total, S, 1.0 / P, summed, root_free)
                side_banks.give(bb, read)
                for half in range(2):
                    p = slice(64 * half, 64 * half + 64)
                    t = v_stt(kiT[p, half * S:(half + 1) * S], bank[p, 0:S], vec("g_ki")[p, :], root[p, 0:S], ALU.mult,
                              ALU.mult, ready, ki_clear)
                ki_ready.append(t)
                roots.give(r, t)
                return [t]

            qi_ready = [None] * (QI_T // 2)

            def evacuate_qi(s, bank, done):
                qi_ready[s] = a_copy(pair(qiT, s), bank[:, :], done)
                return [qi_ready[s]]

            drain(project(t_in["w_ki"], 1, hn, h_ready, evacuate_ki))
            drain(project(t_in["w_qi"], QI_T, hn, h_ready, evacuate_qi))

            score = [take(P), take(S)]
            sel_neg = [take(P), take(S)]
            best = take(8)
            relu_buf = Turns([take(512), take(512)])
            score_ready = [None, None]
            sel_ready = [None, None]
            wi = take(32)
            wi_ready = v_ts(split(wi, 2), dtwi[:, :, 16:32], float(IDX_HEADS) ** -0.5, None, ALU.mult, None, small_ready)

            def scoring():
                for t in range(QI_T):
                    for qb in range(2):
                        nk = P * (qb + 1)
                        b, bank, bank_free = side_banks.take()
                        done = mm(bank[:, :], tile(qiT, t)[:, qb * P:(qb + 1) * P], kiT, True, True, bank_free,
                                  ki_ready[0], qi_ready[t // 2], signal=True)
                        i, buf, buf_free = relu_buf.take()
                        relu = a_act(split(buf, 2)[:, :, 0:nk], split(bank[:, :], 2)[:, :, 0:nk], ACT.Relu, done, buf_free,
                                     scale=float(IDX_DIM) ** -0.5)
                        side_banks.give(b, relu)
                        for j in range(2):
                            h = 2 * t + j
                            col = wi[:, 16 * qb + h:16 * qb + h + 1]
                            src = buf[:, j * S:j * S + nk]
                            if h == 0:
                                score_ready[qb] = v_ts(score[qb], src, col, None, ALU.mult, None, relu, wi_ready)
                            else:
                                score_ready[qb] = v_stt(score[qb], src, col, score[qb], ALU.mult, ALU.add, relu,
                                                        score_ready[qb])
                        relu_buf.give(i, score_ready[qb])
                        yield
                for qb in range(2):
                    n = qb * P
                    ready = v_tt(score[qb][:, n:n + P], score[qb][:, n:n + P], mat("neg_before"), ALU.add,
                                 score_ready[qb])
                    for _ in range(TOPK // 8):
                        top = dve.do(lambda e, qb=qb: nc.vector.max(best, score[qb]), ready)
                        ready = dve.do(lambda e, qb=qb: nc.vector.match_replace(score[qb], best, score[qb], PICKED), top)
                    ready = v_ts(sel_neg[qb], score[qb], PICKED / 2, NEG, ALU.is_gt, ALU.mult, ready)
                    sel_ready[qb] = v_tt(sel_neg[qb][:, n:n + P], sel_neg[qb][:, n:n + P], mat("neg_before"), ALU.add,
                                         ready)
                    yield

            q_ready, k_ready, v_ready = [None] * 4, [None] * 2, []

            def evacuate_q(s, bank, done):
                q_ready[s] = head_norm(pair(qT, s), bank[:, :], vec("g_q"), done, sq, roots)
                return [q_ready[s]]

            def evacuate_k(s, bank, done):
                k_ready[s] = head_norm(pair(kT, s), bank[:, :], vec("g_k"), done, sq, roots)
                return [k_ready[s]]

            def conv_silu(name, tiles, dst, ready, bias=None):
                def evacuate(s, bank, done):
                    i, acc, acc_free = conv_acc.take()
                    for j in range(2):
                        t = 2 * s + j
                        src, a = bank[:, j * S:(j + 1) * S], acc[:, j * S:(j + 1) * S]
                        tap = [vec(name, k * tiles + t) for k in range(CONV_TAPS)]
                        if bias:
                            step = v_ts(a, src, tap[3], vec(bias, t), ALU.mult, ALU.add, done, acc_free)
                        else:
                            step = v_ts(a, src, tap[3], None, ALU.mult, None, done, acc_free)
                        for back in (1, 2, 3):
                            step = v_stt(a[:, back:S], src[:, 0:S - back], tap[3 - back], a[:, back:S], ALU.mult, ALU.add,
                                         step)
                    ready[s] = a_act(dst(s), acc, ACT.Silu, step, (rows_sem, 16))
                    conv_acc.give(i, ready[s])
                    return [step]
                return evacuate

            xbc_ready = [None] * (XBC_T // 2)
            z_ready = [None] * (Z_T // 2)

            def evacuate_z(s, bank, done):
                z_ready[s] = a_act(pair(zT, s), bank[:, :], ACT.Silu, done, (rows_sem, 16))
                return [z_ready[s]]

            def projections_1():
                yield from project(t_in["w_q"], Q_T, hn, h_ready, evacuate_q)
                yield from project(t_in["w_k"], K_T, hn, h_ready, evacuate_k)
                yield from values(t_in["w_v"], val, hn, h_ready, v_ready)

            def projections_2():
                yield from project(t_in["w_xbc"], XBC_T, hn, h_ready,
                                   conv_silu("conv_w", XBC_T, lambda s: pair(xbcT, s), xbc_ready, "conv_b"))
                yield from project(t_in["w_z"], Z_T, hn, h_ready, evacuate_z)

            drain(projections_1(), scoring())

            prob = Turns(relu_buf.bufs)
            prob.free = list(relu_buf.free)
            probT = Turns([take(512), take(512)])
            stats = Turns([take(8), take(8)])
            att_ready = []
            assert cursor[0] <= work_end

            def attention():
                for qb in range(2):
                    nk, nh = P * (qb + 1), 4 // (qb + 1)
                    for h0 in range(0, ATT_HEADS, nh):
                        b, bank, bank_free = side_banks.take()
                        for j in range(nh):
                            h = h0 + j
                            done = mm(bank[:, j * nk:(j + 1) * nk], tile(qT, h)[:, qb * P:(qb + 1) * P],
                                      tile(kT, h // 2)[:, 0:nk], True, True, bank_free, q_ready[h // 2], k_ready[h // 4],
                                      signal=j == nh - 1)
                        i, pr, pr_free = prob.take()
                        si, st, st_free = stats.take()
                        masked = v_stt(split(pr, nh), split(bank[:, :], nh), SCALE, over(sel_neg[qb], nh), ALU.mult,
                                       ALU.add, done, pr_free, sel_ready[qb])
                        side_banks.give(b, masked)
                        top = v_red(st[:, 0:nh], split(pr, nh), ALU.max, masked, st_free, negate=True)
                        for j in range(nh):
                            e = a_act(pr[:, j * nk:(j + 1) * nk], pr[:, j * nk:(j + 1) * nk], ACT.Exp, top,
                                      bias=st[:, j:j + 1], accum=st[:, 4 + j:5 + j])
                        inv = v_rec(st[:, 4:4 + nh], st[:, 4:4 + nh], e)
                        normed = v_tt(split(pr, nh), split(pr, nh), wide(st[:, 4:4 + nh], nk), ALU.mult, inv)
                        stats.give(si, normed)
                        yield
                        b, bank, bank_free = side_banks.take()
                        for j in range(4):
                            turned = turn(bank[:, j * P:(j + 1) * P], pr[:, j * P:(j + 1) * P], normed, bank_free,
                                          signal=j == 3)
                        prob.give(i, turned)
                        i, pt, pt_free = probT.take()
                        copied = a_copy(pt, bank[:, :], turned, pt_free)
                        side_banks.give(b, copied)
                        b, bank, bank_free = side_banks.take()
                        for j in range(nh):
                            kv = (h0 + j) // 2
                            for c in range(qb + 1):
                                o = (j * (qb + 1) + c) * P
                                done = mm(bank[:, j * P:(j + 1) * P], val[:, c * 512 + kv * P:c * 512 + (kv + 1) * P],
                                          pt[:, o:o + P], c == 0, c == qb, copied, bank_free, v_ready,
                                          signal=j == nh - 1 and c == qb)
                        probT.give(i, done)
                        dst = [split(part[:, (8 + h0) * S:(8 + h0 + nh) * S], nh)[:, :, qb * P:(qb + 1) * P]
                               for part in mix]
                        t = store_split(dst, split(bank[:, 0:nh * P], nh), done)
                        att_ready.append(t)
                        side_banks.give(b, t)
                        yield

            drain(attention(), projections_2())
            now = barrier()
            pool.items.append(lambda e: e.dma_start(xT, t_in["x"]).then_inc(x_back_sem, 16))
            x_ready = [(x_back_sem, 16)] * (KD // 2)

            cursor[0] = 64
            state_T = take(1024)
            xdt = [take(1024), take(1024)]
            xds = take(1024)
            b_tok = take(2 * P)
            cbT = [[take(P), take(P)], [take(P), take(P)]]
            dt, adt, acum, tmp = take(32), take(32), take(32), take(32)
            ea, dstate = take(16), take(16)
            decay = Turns([take(512), take(512)])
            c_decayed = Turns([take(512)])
            ysq = Turns([take(512), take(512)])
            roots = Turns([take(512)])
            assert cursor[0] <= work_end

            def softplus(out, x, t0, n, ready):
                t = a_act(t0, x, ACT.Abs, ready)
                t = a_act(t0, t0, ACT.Exp, t, scale=-1.0)
                t = a_act(t0, t0, ACT.Ln, t, bias=ones[:, 0:1])
                return v_stt(out, x, 0.0, t0, ALU.max, ALU.add, t)

            biased = v_tt(split(dt, 2), dtwi[:, :, 0:16], over(vec("dt_bias", 0, 16), 2), ALU.add, small_ready)
            dt_ready = softplus(dt, dt, tmp, 32, biased)
            ea_ready = a_act(ea, vec("a_log", 0, 16), ACT.Exp)
            adt_ready = v_stt(split(adt, 2), split(dt, 2), -1.0, over(ea, 2), ALU.mult, ALU.mult, dt_ready, ea_ready)
            b, bank, bank_free = side_banks.take()
            for c in range(2):
                mm(bank[:, 16 * c:16 * c + 16], mat("upto"), adt[:, 16 * c:16 * c + 16], True, True, bank_free, adt_ready)
            done = mm(bank[:, 32:48], ones[:, :], adt[:, 0:16], True, True, signal=True)
            acum_ready = v_copy(acum, bank[:, 0:32], done)
            t = v_tt(dstate, bank[:, 32:48], acum[:, 0:16], ALU.subtract, acum_ready)
            side_banks.give(b, t)
            ds_ready = a_act(dstate, dstate, ACT.Exp, t)
            xdt_ready = [[None, None], [None, None]]
            for c in range(2):
                for g in range(2):
                    b, bank, bank_free = side_banks.take()
                    for j in range(4):
                        done = turn(bank[:, j * P:(j + 1) * P], tile(xbcT, 4 * g + j)[:, c * P:(c + 1) * P], bank_free,
                                    xbc_ready[2 * g + j // 2], signal=j == 3)
                    dst = xdt[c][:, 512 * g:512 * g + 512]
                    t = v_tt(split(dst, 8), split(bank[:, :], 8), wide(dt[:, 16 * c + 8 * g:16 * c + 8 * g + 8], 64),
                             ALU.mult, done, dt_ready)
                    xdt_ready[c][g] = t
                    side_banks.give(b, t)
                    if c == 0:
                        xds_ready = v_tt(split(xds[:, 512 * g:512 * g + 512], 8), split(dst, 8),
                                         wide(dstate[:, 8 * g:8 * g + 8], 64), ALU.mult, t, ds_ready)
            b, bank, bank_free = side_banks.take()
            for g in range(2):
                done = turn(bank[:, g * P:(g + 1) * P], tile(xbcT, 8 + g)[:, 0:P], bank_free, xbc_ready[4],
                            signal=g == 1)
            b_ready = a_copy(b_tok, bank[:, 0:2 * P], done)
            side_banks.give(b, b_ready)
            b, bank, bank_free = side_banks.take()
            for g in range(2):
                for c in range(2):
                    done = mm(bank[:, (2 * g + c) * P:(2 * g + c + 1) * P], tile(xbcT, 8 + g)[:, c * P:(c + 1) * P],
                              tile(xbcT, 10 + g)[:, c * P:(c + 1) * P], True, True, bank_free, xbc_ready[4:6],
                              signal=g + c == 2)
            for g in range(2):
                for c in range(2):
                    cb_ready = a_copy(cbT[g][c], bank[:, (2 * g + c) * P:(2 * g + c + 1) * P], done)
            side_banks.give(b, cb_ready)
            for g in range(2):
                b, bank, bank_free = side_banks.take()
                done = mm(bank[:, :], b_tok[:, g * P:(g + 1) * P], xds[:, 512 * g:512 * g + 512], True, True, bank_free,
                          b_ready, xds_ready, signal=True)
                state_ready = a_copy(state_T[:, 512 * g:512 * g + 512], bank[:, :], done)
                side_banks.give(b, state_ready)
            y_ready = [[None] * 8, [None] * 8]
            for c in range(2):
                for q4 in range(4):
                    g = q4 // 2
                    b, bank, bank_free = side_banks.take()
                    for j in range(4):
                        h = 4 * q4 + j
                        done = mm(bank[:, j * P:(j + 1) * P],
                                  adt[:, 16 * c + h:16 * c + h + 1].to_broadcast([P, P]), mat("upto"), True, True,
                                  bank_free, adt_ready, signal=j == 3)
                    i, dec, dec_free = decay.take()
                    t = v_tt(split(dec, 4), split(bank[:, :], 4),
                             wide(acum[:, 16 * c + 4 * q4:16 * c + 4 * q4 + 4], P), ALU.subtract, done, dec_free, acum_ready)
                    readers = [t]
                    if c == 1:
                        ci, cd, cd_free = c_decayed.take()
                        grown = a_act(cd, bank[:, :], ACT.Exp, t, cd_free)
                        readers.append(grown)
                        cd_ready = v_tt(split(cd, 4), split(cd, 4), over(tile(xbcT, 10 + g)[:, P:2 * P], 4), ALU.mult,
                                        grown)
                    side_banks.give(b, *readers)
                    t = v_tt(split(dec, 4), split(dec, 4), over(mat("neg_after"), 4), ALU.add, t)
                    t = a_act(dec, dec, ACT.Exp, t)
                    t = v_tt(split(dec, 4), split(dec, 4), over(cbT[g][c], 4), ALU.mult, t, cb_ready)
                    b, bank, bank_free = side_banks.take()
                    for j in range(2):
                        ch = 2 * q4 + j
                        out = bank[:, j * 2 * P:(j + 1) * 2 * P]
                        done = mm(out, xdt[c][:, ch * P:(ch + 1) * P], dec[:, j * 2 * P:(j + 1) * 2 * P], True, c == 0, t,
                                  bank_free, xdt_ready[c][g], signal=j == 1)
                        if c == 1:
                            done = mm(out, state_T[:, ch * P:(ch + 1) * P], cd[:, j * 2 * P:(j + 1) * 2 * P], False, True,
                                      cd_ready, state_ready, signal=j == 1)
                    decay.give(i, done)
                    if c == 1:
                        c_decayed.give(ci, done)
                    for j in range(2):
                        ch = 2 * q4 + j
                        for half in range(2):
                            p = slice(64 * half, 64 * half + 64)
                            xs = tile(xbcT, ch)[p, c * P:(c + 1) * P]
                            t = v_stt(xs, xs, vec("d_skip", ch)[p, :], bank[p, (2 * j + half) * P:(2 * j + half + 1) * P],
                                      ALU.mult, ALU.add, done, xdt_ready[c][g])
                        y_ready[c][ch] = t
                    side_banks.give(b, t)
            ssd_ready = []
            for g in range(2):
                b, bank, bank_free = side_banks.take()
                for j in range(2):
                    s = 2 * g + j
                    t = v_tt(pair(zT, s), pair(zT, s), pair(xbcT, s), ALU.mult, z_ready[s], y_ready[1][2 * s + 1],
                             y_ready[0][2 * s + 1])
                    i, buf, buf_free = ysq.take()
                    squared = a_act(buf, pair(zT, s), ACT.Square, t, buf_free)
                    mm(bank[:, 0:S], ones[:, :], buf[:, 0:S], j == 0, False, squared, bank_free)
                    done = mm(bank[:, 0:S], ones[:, :], buf[:, S:2 * S], False, j == 1, signal=True)
                    ysq.give(i, done)
                r, root, root_free = roots.take()
                ready, read = rstd(root, bank, S, 1.0 / (SSD_W // SSD_GROUPS), done, root_free)
                side_banks.give(b, read)
                for k in range(4 * g, 4 * g + 4):
                    t = v_stt(tile(zT, k), tile(zT, k), vec("g_ssd", k), root[:, 0:S], ALU.mult, ALU.mult, ready)
                    if k % 2:
                        t = store_split(both(mix, (k - 1) * S, (k + 1) * S), pair(zT, k // 2), t)
                        ssd_ready += [t, t]
                roots.give(r, t)

            drain(project(t_in["w_out"], KD, mix, ssd_ready + [att_ready[-1]] * 8, residual(x_ready)))
            barrier()
            cursor[0] = 0
            mlp(t_in["w_up"], t_in["w_down"], "g_mlp", x_ready)
            barrier()
            pool.items.append(lambda e: e.dma_start(x_kept, xT).then_inc(x_saved_sem, 16))
            x_saved = (x_saved_sem, 16)

            cursor[0] = 0
            bias = take(NSA_HEADS * S)
            bias3 = split(bias, NSA_HEADS)
            pool.wait([(rows_sem, 16)])
            grid = bass.AP(tensor=bias_rows.tensor, offset=P - 1,
                           ap=[[NSA_HEADS * 2 * S - 1, P], [2 * S, NSA_HEADS], [1, S]])
            pool.items.append(lambda e: e.dma_start(bias3, grid).then_inc(toep_sem, 16))
            bias_ready = (toep_sem, 16)
            first_half_at = cursor[0]
            gdn_in = [take(3 * HALF_HEADS * S), None]
            gdn_z = [take(HALF_HEADS * S), None]
            gab, gates, beta = take(80), take(48), take(16)
            keep2 = cursor[0]
            w_cmp2 = take(4 * P)
            pool.items.append(lambda e: e.dma_start(w_cmp2, t_in["w_cmp2"]).then_inc(cmp2_sem, 16))
            cmp2_ready = (cmp2_sem, 16)
            qT, kcvc, kskw = [arena[:, X_AT + a * S:X_AT + b * S] for a, b in ((0, 8), (8, 12), (12, 16))]
            vsvw = take(2 * 512)
            sq = Turns([take(512), take(512)])
            roots = Turns([take(512)])
            conv_acc = Turns([take(512)])
            shared_at = cursor[0]
            blocks = [take(CMP_BLOCK * 2 * N_CMP), take(CMP_BLOCK * 2 * N_CMP)]
            cursor[0] = shared_at + 2 * 512 + 2 * 640
            hid = [take(2 * 2 * N_CMP), take(2 * 2 * N_CMP)]
            kcmpT = take(2 * N_CMP)
            vcmp = take(2 * P)
            h_ready = norm("ln1", x_ready, sq, roots.bufs[0])

            gab3 = split(gab, 2)
            gab_tokens = []

            def evacuate_gab(c, bank, done):
                gab_tokens.append(v_copy(gab[:, 40 * c:40 * c + 40], bank[:, 0:40], done))
                return gab_tokens[-1]

            project_tokens(lambda u: t_in["w_gab"][0], P, 40, hn, h_ready, evacuate_gab)
            gab_ready = gab_tokens[-1]

            kv_ready = [None] * 4

            def evacuate_kv(s, bank, done):
                kv_ready[s] = a_copy(pair(kcvc, s) if s < 2 else pair(kskw, s - 2), bank[:, :], done, x_saved)
                return [kv_ready[s]]

            nq_ready = [None] * 4

            def evacuate_nq(s, bank, done):
                nq_ready[s] = a_copy(pair(qT, s), bank[:, :], done)
                return [nq_ready[s]]

            vs_ready = []
            drain(project(t_in["w_kv"], 8, hn, h_ready, evacuate_kv))
            gates_ready = a_act(split(gates, 2), gab3[:, :, 0:24], ACT.Sigmoid, gab_ready)
            beta_ready = a_act(split(beta, 2), gab3[:, :, 32:40], ACT.Sigmoid, gab_ready)

            def compress():
                blk_ready, blk_parts = [None, None], [None, None]
                for m in range(2):
                    for g in range(2):
                        src = kcvc[:, (2 * m + g) * S:(2 * m + g + 1) * S].rearrange("p (m r) -> p r m", r=CMP_STRIDE)
                        dst = split(blocks[m], CMP_BLOCK)[:, :, g * N_CMP:(g + 1) * N_CMP]
                        for half in range(2):
                            rr = slice(half * CMP_STRIDE, (half + 1) * CMP_STRIDE)
                            pe_cols = vec(("pe_k", "pe_v")[m], half * CMP_STRIDE, CMP_STRIDE)
                            blk_ready[m] = v_tt(dst[:, rr, :], src[:, :, half:half + N_CMP], wide(pe_cols, N_CMP), ALU.add,
                                                kv_ready[m])
                    lo_at = 8 * S + m * CMP_BLOCK * 2 * N_CMP
                    blk_parts[m] = both(mix, lo_at, lo_at + CMP_BLOCK * 2 * N_CMP)
                    blk_ready[m] = store_split(blk_parts[m], blocks[m], blk_ready[m])
                yield
                n = 2 * N_CMP
                for m in range(2):
                    b, bank, bank_free = side_banks.take()
                    for hh in range(2):
                        done = column(bank[:, hh * n:(hh + 1) * n], lambda u: t_in["w_cmp1"][4 * m + 2 * hh + u // 2],
                                      lambda r: both(blk_parts[m], r * n, (r + 1) * n), [blk_ready[m]] * CMP_BLOCK,
                                      CMP_BLOCK, bank_free)
                        if hh == 0:
                            yield
                    gelu = a_act(hid[m], bank[:, 0:2 * n], ACT.Gelu_apprx_tanh, done)
                    side_banks.give(b, gelu)
                    yield
                    b, bank, bank_free = side_banks.take()
                    if m == 0:
                        for hh in range(2):
                            done = mm(bank[:, 0:n], w_cmp2[:, hh * P:(hh + 1) * P], hid[0][:, hh * n:(hh + 1) * n],
                                      hh == 0, hh == 1, gelu, bank_free, cmp2_ready, signal=hh == 1)
                        cmp_ready.append(a_copy(kcmpT, bank[:, 0:n], done))
                    else:
                        for g in range(2):
                            for hh in range(2):
                                done = mm(bank[0:N_CMP, g * P:(g + 1) * P],
                                          hid[1][:, hh * n + g * N_CMP:hh * n + (g + 1) * N_CMP],
                                          w_cmp2[:, (2 + hh) * P:(3 + hh) * P], hh == 0, hh == 1, gelu, bank_free, cmp2_ready,
                                          signal=g + hh == 2)
                        cmp_ready.append(a_copy(vcmp[0:N_CMP, :], bank[0:N_CMP, 0:2 * P], done))
                    side_banks.give(b, cmp_ready[-1])
                    yield

            cmp_ready = []

            def nsa_projections():
                yield from project(t_in["w_nq"], 8, hn, h_ready, evacuate_nq)
                yield from values(t_in["w_vsvw"], vsvw, hn, h_ready, vs_ready)

            drain(compress(), nsa_projections())

            gdn_ready = [[None] * 6, [None] * 6]
            gdn_z_ready = [[None] * 2, [None] * 2]

            def gdn_projections(half):
                def evacuate_z2(s, bank, done):
                    gdn_z_ready[half][s] = a_act(pair(gdn_z[half], s), bank[:, :], ACT.Silu, done)
                    return [gdn_z_ready[half][s]]

                yield from project(t_in[f"w_gdn{half}"], 12, hn, h_ready,
                                   conv_silu2(half, lambda s: pair(gdn_in[half], s), gdn_ready[half]))
                yield from project(t_in[f"w_gz{half}"], 4, hn, h_ready, evacuate_z2)

            def conv_silu2(half, dst, ready):
                def evacuate(s, bank, done):
                    i, acc, acc_free = conv_acc.take()
                    for j in range(2):
                        t = 12 * half + 2 * s + j
                        src, a = bank[:, j * S:(j + 1) * S], acc[:, j * S:(j + 1) * S]
                        step = v_ts(a, src, vec("conv_w2", 3 * 24 + t), None, ALU.mult, None, done, acc_free)
                        for back in (1, 2, 3):
                            step = v_stt(a[:, back:S], src[:, 0:S - back], vec("conv_w2", (3 - back) * 24 + t),
                                         a[:, back:S], ALU.mult, ALU.add, step)
                    ready[s] = a_act(dst(s), acc, ACT.Silu, step)
                    conv_acc.give(i, ready[s])
                    return [step]
                return evacuate

            p_cmp = [take(NSA_HEADS * 7), take(NSA_HEADS * N_CMP)]
            cst = take(3 * NSA_HEADS)
            pc_ready = [None, None]

            def compressed():
                for qb in range(2):
                    nc_ = (7, N_CMP)[qb]
                    b, bank, bank_free = side_banks.take()
                    for h in range(NSA_HEADS):
                        g = h // 4
                        done = mm(bank[:, h * nc_:(h + 1) * nc_], tile(qT, h)[:, qb * P:(qb + 1) * P],
                                  kcmpT[:, g * N_CMP:g * N_CMP + nc_], True, True, bank_free, nq_ready[h // 2],
                                  cmp_ready[0], signal=h == NSA_HEADS - 1)
                    pc = p_cmp[qb].rearrange("p (h n) -> p h n", h=NSA_HEADS)
                    off = P - P * qb
                    grid_c = bias3[:, :, off + 31:off + 31 + CMP_STRIDE * (nc_ - 1) + 1:CMP_STRIDE]
                    t = v_stt(pc, bank[:, 0:NSA_HEADS * nc_].rearrange("p (h n) -> p h n", h=NSA_HEADS), SCALE, grid_c,
                              ALU.mult, ALU.add, done, bias_ready)
                    side_banks.give(b, t)
                    m, keep_m, s = cst[:, 0:8], cst[:, 8:16], cst[:, 16:24]
                    t = v_red(m, pc, ALU.max, t, pc_ready[0])
                    t = v_ts(keep_m, m, NEG / 10, None, ALU.is_gt, None, t)
                    t = v_tt(m, m, keep_m, ALU.mult, t)
                    t = v_tt(pc, pc, wide(m, nc_), ALU.subtract, t)
                    t = a_act(p_cmp[qb], p_cmp[qb], ACT.Exp, t)
                    t = v_red(s, pc, ALU.add, t)
                    t = v_ts(s, s, 1e-30, None, ALU.max, None, t)
                    t = v_rec(s, s, t)
                    gate = gates[:, 24 * qb:24 * qb + 24].rearrange("p (h b) -> p h b", b=3)[:, :, 0]
                    t = v_tt(s, s, gate, ALU.mult, t, gates_ready)
                    pc_ready[qb] = v_tt(pc, pc, wide(s, nc_), ALU.mult, t)
                    yield

            stats = Turns([take(4), take(4)])
            assert cursor[0] <= X_AT
            cursor[0] = shared_at
            prob = Turns([take(512), take(512)])
            probT = Turns([take(640), take(640)])
            nsa_ready = []

            def nsa():
                for qb in range(2):
                    nk, nc_, off = P * (qb + 1), (7, N_CMP)[qb], P - P * qb
                    for hd in range(NSA_HEADS):
                        g = hd // 4
                        b, bank, bank_free = side_banks.take()
                        for br in range(2):
                            done = mm(bank[:, br * nk:(br + 1) * nk], tile(qT, hd)[:, qb * P:(qb + 1) * P],
                                      tile(kskw, 2 * br + g)[:, 0:nk], True, True, bank_free, nq_ready[hd // 2],
                                      kv_ready[2:4], signal=br == 1)
                        i, pr, pr_free = prob.take()
                        si, st, st_free = stats.take()
                        pr3 = split(pr[:, 0:2 * nk], 2)
                        t = v_stt(pr3, split(bank[:, 0:2 * nk], 2), SCALE, over(bias3[:, hd, off:off + nk], 2), ALU.mult,
                                  ALU.add, done, pr_free, bias_ready)
                        side_banks.give(b, t)
                        t = v_red(st[:, 0:2], pr3, ALU.max, t, st_free, negate=True)
                        for br in range(2):
                            e = a_act(pr3[:, br, :], pr3[:, br, :], ACT.Exp, t, bias=st[:, br:br + 1],
                                      accum=st[:, 2 + br:3 + br])
                        t = v_rec(st[:, 2:4], st[:, 2:4], e)
                        t = v_tt(st[:, 2:4], st[:, 2:4], gates[:, 24 * qb + 3 * hd + 1:24 * qb + 3 * hd + 3], ALU.mult, t,
                                 gates_ready)
                        normed = v_tt(pr3, pr3, wide(st[:, 2:4], nk), ALU.mult, t)
                        stats.give(si, normed)
                        yield
                        b, bank, bank_free = side_banks.take()
                        blocks_n = 2 * (qb + 1)
                        for j in range(blocks_n):
                            turned = turn(bank[:, j * P:(j + 1) * P], pr[:, j * P:(j + 1) * P], normed, bank_free,
                                          signal=j == blocks_n - 1)
                        prob.give(i, turned)
                        bc, bank_c, bank_c_free = side_banks.take()
                        pc = p_cmp[qb].rearrange("p (h n) -> p h n", h=NSA_HEADS)
                        turned_c = turn(bank_c[0:nc_, 0:P], pc[:, hd, :], pc_ready[qb], bank_c_free, signal=True)
                        i, pt, pt_free = probT.take()
                        t1 = a_copy(pt[:, 0:blocks_n * P], bank[:, 0:blocks_n * P], turned, pt_free)
                        t2 = v_copy(pt[0:nc_, 512:640], bank_c[0:nc_, 0:P], turned_c, pt_free)
                        side_banks.give(b, t1)
                        side_banks.give(bc, t2)
                        b, bank, bank_free = side_banks.take()
                        for j in range(blocks_n):
                            br, c = j // (qb + 1), j % (qb + 1)
                            mm(bank[:, 0:P], vsvw[:, c * 512 + br * S + g * P:c * 512 + br * S + (g + 1) * P],
                               pt[:, j * P:(j + 1) * P], j == 0, False, t1, bank_free, vs_ready)
                        done = mm(bank[:, 0:P], vcmp[0:nc_, g * P:(g + 1) * P], pt[0:nc_, 512:640], False, True, t2,
                                  cmp_ready[1], signal=True)
                        probT.give(i, done)
                        t = store_split(both(mix, hd * S + qb * P, hd * S + (qb + 1) * P), bank[:, 0:P], done)
                        nsa_ready.append(t)
                        side_banks.give(b, t)
                        yield

            drain(compressed())
            drain(nsa(), gdn_projections(0))
            barrier()

            cursor[0] = 0
            spare = NSA_HEADS * S
            graw, gcum, glast, gtmp = take(16), take(16), take(16), take(16)
            ea2 = take(8)
            k_scale, kd_scale = take(16), take(16)
            state = take(HALF_HEADS * P)
            conv_acc = Turns([take(512)])
            D_ = take(512)
            assert cursor[0] <= spare
            cursor[0] = keep2
            eg = take(HALF_HEADS * S)
            decT, LT, LTm, Xs = take(512), take(512), take(512), take(512)
            vb, kbg = LTm, Xs
            E_ = take(512)
            qkT = [take(512), take(512)]
            kd = [take(512), take(512)]
            u = [take(512), take(512)]
            wT = [take(512), take(512)]
            sq = Turns([decT, LT])
            roots = Turns([LTm])
            gdn_in[1], gdn_z[1] = take(3 * HALF_HEADS * S), take(HALF_HEADS * S)
            beta2, beta_kept = beta, beta_ready

            biased = v_tt(split(graw, 2), gab3[:, :, 24:32], over(vec("dt_bias2", 0, 8), 2), ALU.add, gab_ready, beta_kept)
            sp_ready = softplus(graw, graw, gtmp, 16, biased)
            ea_ready = a_act(ea2, vec("a_log2", 0, 8), ACT.Exp)
            graw_ready = v_stt(split(graw, 2), split(graw, 2), -1.0, over(ea2, 2), ALU.mult, ALU.mult, sp_ready, ea_ready)
            b, bank, bank_free = side_banks.take()
            mm(bank[:, 0:16], mat("upto64"), graw, True, True, graw_ready, bank_free)
            done = mm(bank[:, 16:32], mat("ones64"), graw, True, True, signal=True)
            gcum_ready = v_copy(gcum, bank[:, 0:16], done)
            t = v_tt(glast, bank[:, 16:32], gcum, ALU.subtract, gcum_ready)
            side_banks.give(b, t)
            kd_ready = a_act(kd_scale, glast, ACT.Exp, t)
            t = a_act(k_scale, gcum, ACT.Exp, gcum_ready)
            ks_ready = v_tt(k_scale, k_scale, beta2, ALU.mult, t, beta_kept)

            def delta_rule(half):
                qkv, z = gdn_in[half], gdn_z[half]
                in_ready, z_ok = gdn_ready[half], gdn_z_ready[half]
                nq, nk_, nv = qkv[:, 0:1024], qkv[:, 1024:2048], qkv[:, 2048:3072]
                h0 = HALF_HEADS * half
                unit = [None] * 4
                for s in range(4):
                    src = pair(qkv, s)
                    i, buf, buf_free = sq.take()
                    r, root, root_free = roots.take()
                    squared = a_act(buf, src, ACT.Square, in_ready[s], buf_free)
                    b, total, total_free = side_banks.take()
                    summed = sums(total, buf, 512, squared, total_free)
                    sq.give(i, summed)
                    ready, read = rstd(root, total, 512, 1.0, summed, root_free)
                    side_banks.give(b, read)
                    unit[s] = v_stt(src, src, SCALE if s < 2 else 1.0, root, ALU.mult, ALU.mult, ready)
                    roots.give(r, unit[s])
                    yield
                prepared = [None, None]
                for p in range(2):
                    tok = slice(p * P, (p + 1) * P)
                    col = slice(8 * p + h0, 8 * p + h0 + HALF_HEADS)
                    b, bank, bank_free = side_banks.take()
                    for j in range(HALF_HEADS):
                        c0 = 8 * p + h0 + j
                        done = mm(bank[:, j * P:(j + 1) * P], graw[:, c0:c0 + 1].to_broadcast([P, P]), mat("upto64"),
                                  True, True, graw_ready, bank_free, signal=j == 3)
                    t = v_tt(split(decT, 4), split(bank[:, :], 4), wide(gcum[:, col], P), ALU.subtract, done, gcum_ready,
                             unit)
                    eg_p = split(eg, HALF_HEADS)[:, :, tok]
                    grown = a_act(eg_p, split(bank[:, :], 4), ACT.Exp, t)
                    side_banks.give(b, grown, t)
                    t = v_tt(split(decT, 4), split(decT, 4), over(mat("neg_after64"), 4), ALU.add, t)
                    dec_ready = a_act(decT, decT, ACT.Exp, t)
                    bb, bank_b, bank_b_free = side_banks.take()
                    for j in range(HALF_HEADS):
                        c0 = 8 * p + h0 + j
                        beta_done = mm(bank_b[:, j * P:(j + 1) * P], beta2[:, c0:c0 + 1].to_broadcast([P, P]),
                                       mat("ident"), True, True, bank_b_free, beta_kept, signal=j == 3)
                    b, bank, bank_free = side_banks.take()
                    for j in range(HALF_HEADS):
                        kj = tile(nk_, j)[:, tok]
                        done = mm(bank[:, j * P:(j + 1) * P], kj, kj, True, True, bank_free, unit, signal=j == 3)
                    t = v_tt(LT, bank[:, :], decT, ALU.mult, done, dec_ready)
                    side_banks.give(b, t)
                    lt_ready = v_tt(LT, LT, bank_b[:, :], ALU.mult, t, beta_done)
                    side_banks.give(bb, lt_ready)
                    yield
                    b, bank, bank_free = side_banks.take()
                    for j in range(HALF_HEADS):
                        done = mm(bank[:, j * P:(j + 1) * P], tile(nk_, j)[:, tok], tile(nq, j)[:, tok], True, True,
                                  bank_free, unit, signal=j == 3)
                    qk_ready = v_tt(qkT[p], bank[:, :], decT, ALU.mult, done, dec_ready)
                    side_banks.give(b, qk_ready)
                    t = v_tt(split(E_, 4), split(LT, 4), over(mat("level1"), 4), ALU.mult, lt_ready)
                    e_ready = v_tt(split(E_, 4), over(mat("ident"), 4), split(E_, 4), ALU.subtract, t)
                    b, bank, bank_free = side_banks.take()
                    for j in range(HALF_HEADS):
                        done = turn(bank[:, j * P:(j + 1) * P], E_[:, j * P:(j + 1) * P], e_ready, bank_free,
                                    signal=j == 3)
                    d_ready = a_copy(D_, bank[:, :], done)
                    side_banks.give(b, d_ready)
                    yield
                    xe_done = None
                    for b_size in LEVELS:
                        m_ready = v_tt(split(LTm, 4), split(LT, 4), over(mat(f"level{b_size}"), 4), ALU.mult, lt_ready,
                                       xe_done, prepared[0])
                        b, bank, bank_free = side_banks.take()
                        for j in range(HALF_HEADS):
                            q = slice(j * P, (j + 1) * P)
                            done = mm(bank[:, q], LTm[:, q], D_[:, q], True, True, m_ready, d_ready, bank_free,
                                      signal=j == 3)
                        x_ok = a_copy(Xs, bank[:, :], done, xe_done)
                        side_banks.give(b, x_ok)
                        b, bank, bank_free = side_banks.take()
                        for j in range(HALF_HEADS):
                            q = slice(j * P, (j + 1) * P)
                            xe_done = mm(bank[:, q], Xs[:, q], E_[:, q], True, True, x_ok, e_ready, bank_free,
                                         signal=j == 3)
                        if b_size != LEVELS[-1]:
                            b2, bank2, bank2_free = side_banks.take()
                            for j in range(HALF_HEADS):
                                q = slice(j * P, (j + 1) * P)
                                dx_done = mm(bank2[:, q], E_[:, q], Xs[:, q], True, True, x_ok, e_ready, bank2_free,
                                             signal=j == 3)
                            xe_done = dx_done
                            d_ready = v_tt(D_, D_, bank2[:, :], ALU.subtract, dx_done)
                            side_banks.give(b2, d_ready)
                        e_ready = v_tt(E_, E_, bank[:, :], ALU.subtract, xe_done)
                        side_banks.give(b, e_ready)
                        yield
                    b, bank, bank_free = side_banks.take()
                    for j in range(HALF_HEADS):
                        done = turn(bank[:, j * P:(j + 1) * P], tile(nk_, j)[:, tok], bank_free, unit, signal=j == 3)
                    t1 = v_tt(split(kbg, 4), split(bank[:, :], 4), wide(k_scale[:, col], P), ALU.mult, done, ks_ready,
                              xe_done)
                    t2 = v_tt(split(kd[p], 4), split(bank[:, :], 4), wide(kd_scale[:, col], P), ALU.mult, done, kd_ready)
                    side_banks.give(b, t2)
                    b, bank, bank_free = side_banks.take()
                    for j in range(HALF_HEADS):
                        done = turn(bank[:, j * P:(j + 1) * P], tile(nv, j)[:, tok], bank_free, in_ready[4:6],
                                    signal=j == 3)
                    t3 = v_tt(split(vb, 4), split(bank[:, :], 4), wide(beta2[:, col], P), ALU.mult, done, xe_done)
                    side_banks.give(b, t3)
                    b, bank, bank_free = side_banks.take()
                    for j in range(HALF_HEADS):
                        q = slice(j * P, (j + 1) * P)
                        done = mm(bank[:, q], E_[:, q], vb[:, q], True, True, e_ready, t3, bank_free, signal=j == 3)
                    u_ok = a_copy(u[p], bank[:, :], done)
                    side_banks.give(b, u_ok)
                    b, bank, bank_free = side_banks.take()
                    for j in range(HALF_HEADS):
                        q = slice(j * P, (j + 1) * P)
                        done = mm(bank[:, q], kbg[:, q], E_[:, q], True, True, e_ready, t1, bank_free, signal=j == 3)
                    w_ok = a_copy(wT[p], bank[:, :], done)
                    side_banks.give(b, w_ok)
                    q3 = split(nq, HALF_HEADS)[:, :, tok]
                    qg_ok = v_tt(q3, q3, eg_p, ALU.mult, grown, qk_ready)
                    prepared[p] = [u_ok, w_ok, qg_ok, qk_ready, t2, done]
                    yield
                o3 = split(nv, HALF_HEADS)
                o_ready = None
                state_ok = None
                for c in range(S // CHUNK):
                    p, odd = c // 2, c % 2
                    rows = slice(CHUNK * odd, CHUNK * odd + CHUNK)
                    ready = prepared[p]
                    if c:
                        b, bank, bank_free = side_banks.take()
                        for j in range(HALF_HEADS):
                            q = slice(j * P, (j + 1) * P)
                            done = mm(bank[:, q], wT[p][:, q], state[:, q], True, True, ready, state_ok, bank_free,
                                      signal=j == 3)
                        new_v = v_tt(u[p][rows, :], u[p][rows, :], bank[rows, :], ALU.subtract, done, ready, state_ok,
                                     o_ready)
                        side_banks.give(b, new_v)
                        ready = [ready, new_v]
                    b, bank, bank_free = side_banks.take()
                    for j in range(HALF_HEADS):
                        q = slice(j * P, (j + 1) * P)
                        out = bank[:, j * CHUNK:(j + 1) * CHUNK]
                        if c:
                            mm(out, state[:, q], tile(nq, j)[:, c * CHUNK:(c + 1) * CHUNK], True, False, ready, state_ok,
                               bank_free)
                        o_done = mm(out, u[p][:, q], qkT[p][:, j * P + CHUNK * odd:j * P + CHUNK * odd + CHUNK], c == 0,
                                    True, ready, bank_free, signal=j == 3)
                    o_ready = a_copy(o3[:, :, c * CHUNK:(c + 1) * CHUNK], split(bank[:, 0:4 * CHUNK], 4), o_done)
                    side_banks.give(b, o_ready)
                    if c < S // CHUNK - 1:
                        b, bank, bank_free = side_banks.take()
                        for j in range(HALF_HEADS):
                            q = slice(j * P, (j + 1) * P)
                            done = mm(bank[:, q], kd[p][rows, q], u[p][rows, q], True, True, ready, bank_free,
                                      signal=j == 3)
                        last = c * CHUNK + CHUNK - 1
                        for j in range(HALF_HEADS):
                            q = slice(j * P, (j + 1) * P)
                            if c == 0:
                                state_ok = v_copy(state[:, q], bank[:, q], done)
                            else:
                                state_ok = v_stt(state[:, q], state[:, q], eg[:, j * S + last:j * S + last + 1],
                                                 bank[:, q], ALU.mult, ALU.add, done, state_ok)
                        side_banks.give(b, state_ok)
                    yield
                for s in range(2):
                    i, buf, buf_free = sq.take()
                    r, root, root_free = roots.take()
                    squared = a_act(buf, pair(nv, s), ACT.Square, o_ready, buf_free)
                    b, total, total_free = side_banks.take()
                    summed = sums(total, buf, 512, squared, total_free)
                    sq.give(i, summed)
                    ready, read = rstd(root, total, 512, 1.0 / P, summed, root_free)
                    side_banks.give(b, read)
                    t = v_stt(root, pair(nv, s), vec("gdn_norm"), root, ALU.mult, ALU.mult, ready)
                    t = v_tt(root, root, pair(z, s), ALU.mult, t, z_ok[s])
                    at = (8 + h0 + 2 * s) * S
                    gdn_done.append(store_split(both(mix, at, at + 2 * S), root, t))
                    roots.give(r, gdn_done[-1])
                    yield

            gdn_done = []
            drain(delta_rule(0), gdn_projections(1))
            barrier()
            merged = arena[:, first_half_at:first_half_at + KD * S]
            merge_ready = [None] * (KD // 2)

            def merge(m, out_ready, gate_buf):
                for s in range(KD // 2):
                    gb, bank, bank_free = gemm_banks.take()
                    for j in range(2):
                        done = column(bank[:, j * S:(j + 1) * S], lambda u: t_in["w_merge"][KD * m + 2 * s + j],
                                      lambda k: both(hn, k * S, (k + 1) * S), h_ready, KD, bank_free)
                        yield
                    i, gate, gate_free = gate_buf.take()
                    open_ = a_act(gate, bank[:, :], ACT.Sigmoid, done, gate_free)
                    gemm_banks.give(gb, open_)
                    b, bank, bank_free = gemm_banks.take()
                    for j in range(2):
                        done = column(bank[:, j * S:(j + 1) * S], lambda u: t_in["w_papb"][(KD // 2) * m + s],
                                      lambda k: both(mix, (8 * m + k) * S, (8 * m + k + 1) * S), [out_ready] * 8, 8,
                                      bank_free)
                    if m == 0:
                        t = v_tt(pair(merged, s), bank[:, :], gate, ALU.mult, done, open_)
                        gate_buf.give(i, t)
                        gemm_banks.give(b, t)
                    else:
                        t = v_tt(gate, bank[:, :], gate, ALU.mult, done, open_)
                        gemm_banks.give(b, t)
                        t = v_tt(pair(merged, s), pair(merged, s), gate, ALU.add, t, merge_ready[s])
                        gate_buf.give(i, t)
                    merge_ready[s] = t
                    yield

            drain(delta_rule(1), merge(0, nsa_ready, Turns([conv_acc.bufs[0]])))
            barrier()

            pool.items.append(lambda e: e.dma_start(xT, x_kept).then_inc(x_back_sem, 16))
            x_ready = [(x_back_sem, 32)] * (KD // 2)
            cursor[0] = 0
            drain(merge(1, gdn_done, Turns([take(512), take(512)])))
            h_free = (pe.sem, pe.count)
            merged_ready = []
            for s in range(KD // 2):
                t = store_split(both(hn, 2 * s * S, 2 * (s + 1) * S), pair(merged, s), merge_ready[s], h_free)
                merged_ready += [t, t]
            drain(project(t_in["w_o"], KD, hn, merged_ready, residual(x_ready)))
            barrier()
            cursor[0] = 0
            mlp(t_in["w_up2"], t_in["w_down2"], "ln2", x_ready)
            barrier()
            cursor[0] = 0
            sq = Turns([take(512), take(512)])
            root = take(S)
            y = take(KD * S)
            y_tok = norm("ln_f", x_ready, sq, root, out=y)
            for j in range(4):
                sp.wait([y_tok[4 * j + 3]])
                sp.items.append(lambda e, j=j: e.dma_start(x_out[:, j * 1024:(j + 1) * 1024],
                                                           y[:, j * 1024:(j + 1) * 1024]).then_inc(out_sem, 16))
            sp.wait([(out_sem, 64), (rows_sem, 16), x_saved])
            return (pe, dve, act, pool, sp), order

        _, plan = emit(None)
        (pe, dve, act, pool, sp), _ = emit(plan)

        block = ctx.enter_context(nc.Block())

        @block.sync
        def _(e):
            sp.run(e)

        @block.tensor
        def _(e):
            pe.run(e)

        @block.vector
        def _(e):
            dve.run(e)

        @block.scalar
        def _(e):
            act.run(e)

        @block.gpsimd
        def _(e):
            pool.run(e)


def columns(w, k_tiles=KD):
    n = w.shape[1] // P
    return np.ascontiguousarray(w.reshape(k_tiles, P, n, P).transpose(2, 1, 0, 3)).reshape(n, P, -1)


def pieces(w, width):
    return np.ascontiguousarray(w.reshape(KD, P, width).transpose(1, 0, 2).reshape(P, -1, PIECE).transpose(1, 0, 2))


def padded(w):
    return np.concatenate([w, np.zeros((w.shape[0], P - w.shape[1]), w.dtype)], axis=1)


def row_tiles(w, k_tiles):
    return np.ascontiguousarray(w.reshape(k_tiles, P, -1).transpose(1, 0, 2)).reshape(P, -1)


def channels(v):
    return np.ascontiguousarray(v.reshape(-1, P).T)


def everywhere(v):
    return np.broadcast_to(v.reshape(1, -1), (P, v.size))


def kernel(**inputs):
    import numpy as _np
    import concourse.bacc as _bacc
    from concourse import mybir as _mybir
    from concourse.bass_utils import run_bass_kernel_spmd as _run

    a = {k: _np.asarray(v) for k, v in inputs.items()}
    w_in, w_in2 = a["w_in"][0], a["w_in_2"][0]
    at, cut = 0, {}
    for name, n in (("z", 1024), ("xbc", 1536), ("dt", 16), ("q", 1024), ("k", 512), ("v", 512), ("qi", 1024),
                    ("ki", 64), ("wi", 16)):
        cut[name] = w_in[:, at:at + n]
        at += n
    at = 0
    for name, n in (("nq", 1024), ("kv", 1536), ("gate", 24), ("qkv", 3072), ("gz", 1024), ("a", 8), ("b", 8),
                    ("merge", 4096)):
        cut[name] = w_in2[:, at:at + n]
        at += n
    kv = [cut["kv"][:, 256 * i:256 * i + 256] for i in range(6)]
    half = [_np.concatenate([cut["qkv"][:, 1024 * m + 512 * h:1024 * m + 512 * h + 512] for m in range(3)], axis=1)
            for h in range(2)]
    conv2 = a["conv_w_2"][0]
    conv2 = _np.concatenate([conv2[:, 1024 * m + 512 * h:1024 * m + 512 * h + 512] for h in range(2)
                             for m in range(3)], axis=1)
    cmp1 = [columns(a[n][0], 2 * KD).reshape(2, P, 2, PIECE).transpose(0, 2, 1, 3).reshape(4, P, PIECE)
            for n in ("cmp_w1_k_2", "cmp_w1_v_2")]
    papb = [columns(a[n][0], 8).reshape(KD // 2, 2, P, UNIT).transpose(0, 2, 1, 3).reshape(KD // 2, P, PIECE)
            for n in ("w_pa_2", "w_pb_2")]

    def down(w):
        return _np.concatenate([columns(w[D * f:D * (f + 1)]) for f in range(FF // D)])

    mats, hot = constants()
    vec_parts = dict(
        g_mix=channels(a["g_mix"][0]), g_ssd=channels(a["g_ssd"][0]), g_q=channels(a["g_q"][0]),
        g_k=channels(a["g_k"][0]), g_ki=channels(_np.concatenate([a["g_kidx"][0], a["g_kidx"][0]])),
        conv_w=channels(a["conv_w"][0]), conv_b=channels(a["conv_b"][0]),
        d_skip=channels(_np.repeat(a["d_skip"][0], 64)), dt_bias=everywhere(a["dt_bias"][0]),
        a_log=everywhere(a["a_log"][0]), g_mlp=channels(a["g_mlp"][0]), ln1=channels(a["ln1_w_2"][0]),
        conv_w2=channels(conv2), a_log2=everywhere(a["a_log_2"][0]), dt_bias2=everywhere(a["dt_bias_2"][0]),
        gdn_norm=channels(a["gdn_norm_w_2"][0]), ln2=channels(a["ln2_w_2"][0]), ln_f=channels(a["ln_f_w_2"]),
        pe_k=a["cmp_pe_k_2"][0].T, pe_v=a["cmp_pe_v_2"][0].T)
    arrays = {
        "x": row_tiles(a["x"][0].T, KD),
        "vecs": _np.concatenate([vec_parts[n] for n in VECS], axis=1),
        "mats": mats,
        "hot": hot,
        "rel": _np.concatenate([a["rel_table_2"], _np.full((1, NSA_HEADS), NEG, _np.float32)], axis=0),
        "w_dtwi": columns(padded(_np.concatenate([cut["dt"], cut["wi"]], axis=1))),
        "w_gab": columns(padded(_np.concatenate([cut["gate"], cut["a"], cut["b"]], axis=1))),
        "w_cmp2": _np.concatenate([row_tiles(a["cmp_w2_k_2"][0], 2), row_tiles(a["cmp_w2_v_2"][0], 2)], axis=1),
        "w_ki": columns(_np.concatenate([cut["ki"], cut["ki"]], axis=1)),
        "w_qi": columns(cut["qi"]),
        "w_q": columns(cut["q"]),
        "w_k": columns(cut["k"]),
        "w_v": pieces(cut["v"], 512),
        "w_xbc": columns(cut["xbc"]),
        "w_z": columns(cut["z"]),
        "w_out": columns(a["w_out"][0]),
        "w_up": columns(a["w_up"][0]),
        "w_down": down(a["w_down"][0]),
        "w_kv": columns(_np.concatenate([kv[0], kv[1], kv[2], kv[4]], axis=1)),
        "w_nq": columns(cut["nq"]),
        "w_vsvw": pieces(_np.concatenate([kv[3], kv[5]], axis=1), 512),
        "w_cmp1": _np.concatenate(cmp1),
        "w_gdn0": columns(half[0]),
        "w_gdn1": columns(half[1]),
        "w_gz0": columns(cut["gz"][:, 0:512]),
        "w_gz1": columns(cut["gz"][:, 512:1024]),
        "w_merge": columns(cut["merge"]),
        "w_papb": _np.concatenate(papb),
        "w_o": columns(a["w_o_2"][0]),
        "w_up2": columns(a["w_up_2"][0]),
        "w_down2": down(a["w_down_2"][0]),
    }
    nc = _bacc.Bacc("TRN2", target_bir_lowering=False, num_devices=1)
    t_in, feed = {}, {}
    for name, v in arrays.items():
        v = _np.ascontiguousarray(v)
        feed[f"in_{name}"] = v
        t_in[name] = nc.dram_tensor(f"in_{name}", v.shape, _mybir.dt.float32, kind="ExternalInput").ap()
    x_out = nc.dram_tensor("x_out", (P, KD * S), _mybir.dt.float32, kind="ExternalOutput").ap()
    bias_rows = nc.dram_tensor("bias_rows", (P, NSA_HEADS * 2 * S), _mybir.dt.float32).ap()
    x_kept = nc.dram_tensor("x_kept", (P, KD * S), _mybir.dt.float32).ap()
    build(nc, t_in, x_out, bias_rows, x_kept)
    r = _run(nc, [feed], core_ids=[0])
    y = r.results[0]["x_out"]
    return _np.ascontiguousarray(y.reshape(P, KD, S).transpose(2, 1, 0).reshape(1, S, D))
```

```python
from contextlib import ExitStack

import numpy as np

import concourse.bass as bass
from concourse import mybir

F32 = mybir.dt.float32
F32R = mybir.dt.float32r
ALU = mybir.AluOpType
ACT = mybir.ActivationFunctionType
AX_X = mybir.AxisListType.X

P = 128
D = 2048
S = 256
KD = D // P
FF = 4 * D
EPS = 1e-6
NEG = -1e30
PICKED = -3e38

SSD_W, SSD_HEADS, SSD_GROUPS = 1024, 16, 2
CONV_TAPS = 4
XBC = 1536
ATT_HEADS, ATT_KV = 8, 4
IDX_HEADS, IDX_DIM, TOPK = 16, 64, 64
Z_T, XBC_T, Q_T, K_T, QI_T = 8, 12, 8, 4, 8
NSA_HEADS, NSA_GROUPS = 8, 2
CMP_STRIDE, CMP_BLOCK, N_CMP, CMP_HID = 16, 32, 15, 256
GDN_HEADS, CHUNK = 8, 64
HALF_HEADS = 4
REL_BUCKETS = 32
SCALE = float(P) ** -0.5

PIECE = 2048
UNIT = 1024
UNIT_K = UNIT // P
PIECES = 4
UNITS = 4
ARENA = 18128
X_AT = ARENA - KD * S

VECS = dict(g_mix=16, g_ssd=8, g_q=1, g_k=1, g_ki=1, conv_w=48, conv_b=12, d_skip=8, dt_bias=16, a_log=16,
            g_mlp=16, ln1=16, conv_w2=96, a_log2=8, dt_bias2=8, gdn_norm=1, ln2=16, ln_f=16, pe_k=32, pe_v=32)
MATS = ["ident", "upto", "upto64", "ones64", "neg_after", "neg_after64", "neg_before"] + [
    f"level{b}" for b in (1, 2, 4, 8, 16, 32)]
LEVELS = (2, 4, 8, 16, 32)


def constants():
    i = np.arange(P)
    r, c = i[:, None], i[None, :]
    same = (r // CHUNK) == (c // CHUNK)
    m = {
        "ident": r == c,
        "upto": r <= c,
        "upto64": (r <= c) & same,
        "ones64": same,
        "neg_after": np.where(r <= c, 0.0, NEG),
        "neg_after64": np.where((r <= c) & same, 0.0, NEG),
        "neg_before": np.where(c <= r, 0.0, NEG),
    }
    for b in (1, 2, 4, 8, 16, 32):
        m[f"level{b}"] = (r // (2 * b) == c // (2 * b)) & (r % (2 * b) < b) & (c % (2 * b) >= b)
    mats = np.concatenate([np.asarray(m[n], np.float32) for n in MATS], axis=1)
    dist = (S - 1) - np.arange(2 * S)
    exact = REL_BUCKETS // 2
    near = np.maximum(dist, 1).astype(np.float32)
    far = exact + (np.log(near / exact) / np.log(np.float32(P / exact)) * (REL_BUCKETS - exact)).astype(np.int32)
    bucket = np.where(dist < exact, np.maximum(dist, 0), np.minimum(far, REL_BUCKETS - 1))
    hot = np.zeros((REL_BUCKETS + 1, 2 * S), np.float32)
    for j in range(2 * S):
        hot[bucket[j] if dist[j] >= 0 else REL_BUCKETS, j] = 1.0
    return mats, hot


class Engine:

    def __init__(self, sem):
        self.sem, self.count, self.items, self.seen = sem, 0, [], {}

    def wait(self, tokens):
        for t in tokens:
            if t is None:
                continue
            if isinstance(t, list):
                self.wait(t)
                continue
            sem, value = t
            if self.seen.get(id(sem), 0) < value:
                self.seen[id(sem)] = value
                self.items.append(lambda e, sem=sem, value=value: e.wait_ge(sem, value))

    def do(self, step, *after, signal=True):
        self.wait(after)
        if signal:
            self.count += 1
            self.items.append(lambda e: step(e).then_inc(self.sem, 1))
            return (self.sem, self.count)
        self.items.append(step)
        return None

    def run(self, e):
        for item in self.items:
            item(e)


def build(nc, t_in, x_out, bias_rows, x_kept):
    ctx = ExitStack()
    with ctx:
        def sb(name, shape):
            return ctx.enter_context(nc.sbuf_tensor(name, shape, F32))

        def sem(name):
            return ctx.enter_context(nc.semaphore(name))

        engine_sems = [sem(f"{n}_steps") for n in ("pe", "dve", "act", "pool", "sp")]

        def sb_r(name, shape):
            return ctx.enter_context(nc.sbuf_tensor(name, shape, F32R))

        ring = sb("weight_ring", [P, PIECES, PIECE])
        w_split = (sb_r("w_hi", [P, UNITS, UNIT]), sb_r("w_lo", [P, UNITS, UNIT]))
        hn = (sb_r("h_hi", [P, KD * S]), sb_r("h_lo", [P, KD * S]))
        mix = (sb_r("mix_hi", [P, KD * S]), sb_r("mix_lo", [P, KD * S]))
        mats = sb("const_mats", [P, len(MATS) * P])
        ones = sb("ones", [P, P])
        vecs = sb("vecs", [P, sum(VECS.values())])
        eps = sb("eps", [P, 1])
        arena = sb("arena", [P, ARENA])
        xT = arena[:, X_AT:ARENA]
        psum = [ctx.enter_context(nc.psum_tensor(f"bank{i}", [P, 512], F32)) for i in range(8)]

        piece_sem = [sem(f"piece_loaded{i}") for i in range(PIECES)]
        cmp2_sem = sem("w_cmp2_loaded")
        x_saved_sem = sem("x_saved")
        x_back_sem = sem("x_back")
        param_sem = sem("params_loaded")
        x_sems = [sem(f"x_loaded{i}") for i in range(4)]
        vecs_sem = sem("vecs_loaded")
        rows_sem = sem("bias_rows_written")
        toep_sem = sem("bias_grid_loaded")
        out_sem = sem("out_written")

        def emit(plan):
            pe, dve, act, pool, sp = [Engine(s) for s in engine_sems]

            def mat(name):
                i = MATS.index(name)
                return mats[:, i * P:(i + 1) * P]

            vec_at = {}
            at = 0
            for name, w in VECS.items():
                vec_at[name] = at
                at += w

            def vec(name, i=0, n=1):
                return vecs[:, vec_at[name] + i:vec_at[name] + i + n]

            def pair(buf, j):
                return buf[:, 2 * j * S:(2 * j + 2) * S]

            def tile(buf, k):
                return buf[:, k * S:(k + 1) * S]

            cursor = [0]

            def take(n):
                a = cursor[0]
                cursor[0] += n
                assert cursor[0] <= ARENA, cursor[0]
                return arena[:, a:a + n]

            def barrier():
                now = [(e.sem, e.count) for e in (pe, dve, act, pool) if e.count]
                for e in (pe, dve, act, pool):
                    e.wait([t for t in now if t[0] is not e.sem or e is not pe])
                return now

            class Turns:

                def __init__(self, bufs):
                    self.bufs, self.free, self.n, self.out = bufs, [None] * len(bufs), 0, set()

                def take(self):
                    i = self.n % len(self.bufs)
                    self.n += 1
                    assert i not in self.out
                    self.out.add(i)
                    return i, self.bufs[i], self.free[i]

                def give(self, i, *tokens):
                    self.out.remove(i)
                    self.free[i] = list(tokens)

            gemm_banks = Turns([psum[i] for i in (0, 1, 2)])
            side_banks = Turns([psum[i] for i in (3, 4, 5, 6, 7)])

            def mm(out, lhsT, rhs, start, stop, *after, signal=False):
                return pe.do(lambda e: nc.tensor.matmul(out, lhsT, rhs, start=start, stop=stop), *after, signal=signal)

            def turn(out, src, *after, signal=False):
                k = src.shape[0]
                return pe.do(lambda e: nc.tensor.transpose(out, src, mat("ident")[0:k, 0:k]), *after, signal=signal)

            def v_tt(out, a, b, op, *after):
                return dve.do(lambda e: nc.vector.tensor_tensor(out, a, b, op), *after)

            def v_ts(out, a, s1, s2, op0, op1, *after):
                if op1 is None:
                    return dve.do(lambda e: nc.vector.tensor_scalar(out, a, s1, None, op0), *after)
                return dve.do(lambda e: nc.vector.tensor_scalar(out, a, s1, s2, op0, op1), *after)

            def v_stt(out, a, s, b, op0, op1, *after):
                return dve.do(lambda e: nc.vector.scalar_tensor_tensor(out=out, in0=a, scalar=s, in1=b, op0=op0, op1=op1),
                              *after)

            def v_rec(out, a, *after):
                return dve.do(lambda e: nc.vector.reciprocal(out, a), *after)

            def v_copy(out, a, *after):
                return dve.do(lambda e: nc.vector.tensor_copy(out, a), *after)

            def v_red(out, a, op, *after, negate=None):
                return dve.do(lambda e: nc.vector.tensor_reduce(out, a, AX_X, op, negate=negate), *after)

            def a_act(out, a, func, *after, scale=1.0, bias=0.0, accum=None):
                kw = {} if accum is None else dict(accum_out=accum)
                return act.do(lambda e: nc.scalar.activation(out, a, func, bias=bias, scale=scale, **kw), *after)

            def a_copy(out, a, *after):
                return act.do(lambda e: nc.scalar.copy(out, a), *after)

            def wide(ap, n):
                return ap.unsqueeze(2).to_broadcast([ap.shape[0], ap.shape[1], n])

            def over(ap, n):
                return ap.unsqueeze(1).to_broadcast([ap.shape[0], n, ap.shape[1]])

            def split(ap, n):
                return ap.rearrange("p (a b) -> p a b", a=n)

            order = []
            planned = order if plan is None else plan
            ahead = 1 if plan is None else UNITS
            stream = dict(loaded=0, split=0, used=0)
            piece_free, unit_free, unit_ready = [None] * PIECES, [None] * UNITS, [None] * UNITS

            def load_next():
                n = stream["loaded"]
                if n < len(planned):
                    i, src = n % PIECES, planned[n]
                    sp.wait([piece_free[i]])
                    sp.items.append(lambda e: e.dma_start(ring[:, i, :], src).then_inc(piece_sem[i], 16))
                    stream["loaded"] += 1

            def split_next():
                u = stream["split"]
                n, i = u // 2, u % UNITS
                while stream["loaded"] <= n:
                    load_next()
                loaded = (piece_sem[n % PIECES], 16 * (n // PIECES + 1))
                src = ring[:, n % PIECES, (u % 2) * UNIT:(u % 2 + 1) * UNIT]
                hi, lo = w_split[0][:, i, :], w_split[1][:, i, :]
                high = a_copy(hi, src, loaded, unit_free[i])
                unit_ready[i] = v_tt(lo, src, hi.bitcast(F32), ALU.subtract, high, loaded, unit_free[i])
                stream["split"] += 1
                if u % 2:
                    piece_free[n % PIECES] = unit_ready[i]
                    load_next()

            def weights(src, held=0):
                u = stream["used"]
                if u % 2 == 0:
                    order.append(src)
                stream["used"] += 1
                while stream["split"] < min(u + max(1, ahead - held), 2 * len(planned)):
                    split_next()
                i = u % UNITS
                return i, (w_split[0][:, i, :], w_split[1][:, i, :]), unit_ready[i]

            def products(out, lhsT, rhs, first, last, *after, signal=False):
                mm(out, lhsT[0], rhs[0], first, False, *after)
                mm(out, lhsT[0], rhs[1], False, False)
                return mm(out, lhsT[1], rhs[0], False, last, signal=signal)

            def store_split(parts, src, *after):
                high = a_copy(parts[0], src, *after)
                return v_tt(parts[1], src, parts[0].bitcast(F32), ALU.subtract, high, *after)

            def both(x, a, b):
                return (x[0][:, a:b], x[1][:, a:b])

            def column(out, w, rhs, ready, k_tiles, *after, fine=True):
                for k in range(k_tiles):
                    if k % UNIT_K == 0:
                        i, unit, split_done = weights(w(k // UNIT_K))
                    o = (k % UNIT_K) * P
                    done = products(out, [part[:, o:o + P] for part in unit], rhs(k), k == 0, k == k_tiles - 1,
                                    split_done, ready[k], *after, signal=k % UNIT_K == UNIT_K - 1)
                    if k % UNIT_K == UNIT_K - 1:
                        unit_free[i] = done
                        if fine and k < k_tiles - 1:
                            yield
                return done

            def in_halves(dst, bank):
                if isinstance(bank, tuple):
                    return [(dst[:, 0:S], bank[0][:, 0:S]), (dst[:, S:2 * S], bank[1][:, 0:S])]
                return [(dst, bank[:, :])]

            def column_pair(banks, w, x, x_ready, *after):
                units = [weights(w[n // 2], held=n) for n in range(UNITS)]
                for k in range(KD):
                    o = (k % UNIT_K) * P
                    for j in range(2):
                        i, unit, split_done = units[2 * j + k // UNIT_K]
                        last = k % UNIT_K == UNIT_K - 1
                        done = products(banks[j][:, 0:S], [part[:, o:o + P] for part in unit],
                                        both(x, k * S, (k + 1) * S), k == 0, k == KD - 1, split_done,
                                        x_ready[k], *after, signal=last)
                        if last:
                            unit_free[i] = done
                return done

            def project(w, tiles, x, x_ready, evacuate, first=0, fine=True, behind_norm=False):
                for s in range((tiles + 1) // 2):
                    b, bank, bank_free = gemm_banks.take()
                    if behind_norm and s == 0:
                        b2, bank2, bank2_free = gemm_banks.take()
                        done = column_pair((bank, bank2), w[first:first + 2], x, x_ready, bank_free, bank2_free)
                        read = evacuate(0, (bank, bank2), done)
                        gemm_banks.give(b, *read)
                        gemm_banks.give(b2, *read)
                        yield
                        continue
                    for j in range(min(2, tiles - 2 * s)):
                        if j:
                            yield
                        done = yield from column(
                            bank[:, j * S:(j + 1) * S], lambda u: w[first + 2 * s + j],
                            lambda k: both(x, k * S, (k + 1) * S), x_ready, KD, bank_free, fine=fine)
                    gemm_banks.give(b, *evacuate(s, bank, done))
                    yield

            def project_tokens(w, width, n, x, x_ready, evacuate):
                banks = [gemm_banks.take() for _ in range(2)]
                per_unit = UNIT // width
                for k in range(KD):
                    if k % per_unit == 0:
                        i, unit, split_done = weights(w(k // per_unit))
                    o = (k % per_unit) * width
                    last = k % per_unit == per_unit - 1
                    for c in range(2):
                        done = products(banks[c][1][:, 0:n], both(x, k * S + c * P, k * S + (c + 1) * P),
                                        [part[:, o:o + n] for part in unit], k == 0, k == KD - 1, split_done,
                                        banks[c][2], x_ready[k], signal=last)
                    if last:
                        unit_free[i] = done
                        if k % (2 * per_unit) == 2 * per_unit - 1 and k < KD - 1:
                            yield
                for c in range(2):
                    gemm_banks.give(banks[c][0], evacuate(c, banks[c][1], done))

            def values(w, out, x, x_ready, ready):
                def evacuate(c, bank, done):
                    ready.append(a_copy(out[:, c * 512:(c + 1) * 512], bank[:, :], done))
                    return ready[-1]
                yield from project_tokens(lambda u: w[u // 2], 512, 512, x, x_ready, evacuate)
                yield

            def sums(bank, src, n, *after):
                return mm(bank[:, 0:n], ones[:, :], src, True, True, *after, signal=True)

            def rstd(out, bank, n, scale, *after):
                root = a_act(out[:, 0:n], bank[:, 0:n], ACT.Sqrt, *after, scale=scale, bias=eps[:, 0:1])
                return v_rec(out[:, 0:n], out[:, 0:n], root), root

            def norm(gain, x_ready, sq, root_buf, out=None, gathered=None):
                def split_ahead(n):
                    while plan is not None and stream["split"] < min(stream["used"] + n, 2 * len(planned)):
                        split_next()

                if gathered:
                    split_ahead(UNITS)
                b, bank, bank_free = side_banks.take()
                if gathered:
                    for n, (buf, squared) in enumerate(gathered):
                        mm(bank[:, 0:S], ones[:, :], buf[:, 0:S], n == 0, False, squared, bank_free)
                        done = mm(bank[:, 0:S], ones[:, :], buf[:, S:2 * S], False, n == 1, signal=True)
                for j in range(0 if gathered else KD // 2):
                    i, buf, buf_free = sq.take()
                    squared = a_act(buf, pair(xT, j), ACT.Square, x_ready[j], buf_free)
                    mm(bank[:, 0:S], ones[:, :], buf[:, 0:S], j == 0, False, squared, bank_free)
                    done = mm(bank[:, 0:S], ones[:, :], buf[:, S:2 * S], False, j == KD // 2 - 1, signal=True)
                    sq.give(i, done)
                split_ahead(UNITS // 2)
                ready, read = rstd(root_buf, bank, S, 1.0 / D, done)
                side_banks.give(b, read)
                split_ahead(UNITS)
                if out is not None:
                    return [v_stt(tile(out, k), tile(xT, k), vec(gain, k), root_buf[:, 0:S], ALU.mult, ALU.mult, ready)
                            for k in range(KD)]
                tokens = []
                for j in range(KD // 2):
                    i, buf, buf_free = sq.take()
                    for k in (2 * j, 2 * j + 1):
                        t = v_stt(buf[:, (k % 2) * S:(k % 2 + 1) * S], tile(xT, k), vec(gain, k), root_buf[:, 0:S],
                                  ALU.mult, ALU.mult, ready, buf_free)
                    t = store_split(both(hn, 2 * j * S, 2 * (j + 1) * S), buf, t)
                    sq.give(i, t)
                    tokens += [t, t]
                return tokens

            def head_norm(out, bank, gains, done, sq, roots, scale=1.0 / P, factor=None):
                i, buf, buf_free = sq.take()
                r, root, root_free = roots.take()
                squared = a_act(buf, bank, ACT.Square, done, buf_free)
                b, total, total_free = side_banks.take()
                summed = sums(total, buf, 512, squared, total_free)
                sq.give(i, summed)
                ready, read = rstd(root, total, 512, scale, summed, root_free)
                side_banks.give(b, read)
                t = v_stt(out, bank, gains if factor is None else factor, root, ALU.mult, ALU.mult, ready)
                roots.give(r, t)
                return t

            norm_bufs = [arena[:, X_AT - 512 * n:X_AT - 512 * (n - 1)] for n in (1, 2, 3)]

            def residual(x_ready, gathered=None):
                total, bufs = norm_bufs[0], norm_bufs[1:]

                def gather(s, t):
                    if s == 0:
                        gathered[:] = [(total, a_act(total, pair(xT, 0), ACT.Square, t))]
                        return
                    buf = bufs[s % 2]
                    squared = a_act(buf, pair(xT, s), ACT.Square, t, buf_free[s % 2])
                    if s == KD // 2 - 1:
                        gathered.append((buf, squared))
                        return
                    buf_free[s % 2] = pool.do(lambda e: nc.gpsimd.tensor_tensor(total, total, buf, ALU.add), squared,
                                              gathered[0][1])
                    gathered[0] = (total, buf_free[s % 2])

                buf_free = [None, None]

                def evacuate(s, bank, done):
                    t = v_tt(pair(xT, s), pair(xT, s), bank[:, :], ALU.add, done, x_ready[s])
                    x_ready[s] = t
                    if gathered is not None:
                        gather(s, t)
                    return [t]
                return evacuate

            def softplus(out, x, t0, ready):
                t = a_act(t0, x, ACT.Abs, ready)
                t = a_act(t0, t0, ACT.Exp, t, scale=-1.0)
                t = a_act(t0, t0, ACT.Ln, t, bias=ones[:, 0:1])
                return v_stt(out, x, 0.0, t0, ALU.max, ALU.add, t)

            def together(*gens):
                gens = list(gens)
                while gens:
                    for g in list(gens):
                        try:
                            next(g)
                        except StopIteration:
                            gens.remove(g)
                    yield

            def rounds(n):
                for _ in range(n):
                    yield

            def one_after_another(*gens):
                for g in gens:
                    yield from g

            def drain(*gens):
                for _ in together(*gens):
                    pass

            def mlp(w_up, w_down, gain, x_ready, gathered):
                sq = Turns([take(512), take(512)])
                root = take(S)
                relu = Turns([take(512), take(512), take(512)])
                h_ready = norm(gain, x_ready, sq, root, gathered=gathered)
                add, add_last = residual(x_ready), residual(x_ready, gathered)
                u_ready = [None] * KD

                def squared_relu(s, bank, done):
                    i, buf, buf_free = relu.take()
                    for part, src in in_halves(buf, bank):
                        r = a_act(part, src, ACT.Relu, done, buf_free)
                    t = v_tt(buf, buf, buf, ALU.mult, r)
                    t = store_split(both(mix, 2 * s * S, 2 * (s + 1) * S), buf, t)
                    relu.give(i, t)
                    u_ready[2 * s] = u_ready[2 * s + 1] = t
                    return [r]

                for f in range(FF // D):
                    drain(project(w_up, KD, hn, h_ready, squared_relu, first=f * KD, behind_norm=f == 0))
                    drain(project(w_down, KD, mix, u_ready, add if f < FF // D - 1 else add_last, first=f * KD))

            hot_at = X_AT - (XBC_T + Z_T) * S - 2 * S - NSA_HEADS
            hot = arena[0:REL_BUCKETS + 1, hot_at:hot_at + 2 * S]
            rel = arena[0:REL_BUCKETS + 1, hot_at + 2 * S:hot_at + 2 * S + NSA_HEADS]
            act.items.append(lambda e: e.dma_start(vecs[:, :], t_in["vecs"]).then_inc(vecs_sem, 16))
            for dst, name in ((hot, "hot"), (rel, "rel"), (mats[:, :], "mats")):
                act.items.append(lambda e, dst=dst, name=name: e.dma_start(dst, t_in[name]).then_inc(param_sem, 16))
            params = (param_sem, 16 * 3)
            x_ready = [(x_sems[j // 2], 16) for j in range(KD // 2)]
            for n, quarter in enumerate(x_sems):
                part = slice(n * KD * S // 4, (n + 1) * KD * S // 4)
                sp.items.append(lambda e, part=part, quarter=quarter: e.dma_start(
                    xT[:, part], t_in["x"][:, part]).then_inc(quarter, 16))
            ones_ready = pool.do(lambda e: nc.gpsimd.memset(ones[:, :], 1.0))
            eps_ready = pool.do(lambda e: nc.gpsimd.memset(eps[:, :], EPS))
            for e in (pe, dve, act):
                e.wait([ones_ready, eps_ready])
            dve.wait([(vecs_sem, 16)])

            rows = arena[:, X_AT - 5120:X_AT - 1024]

            def bias_table():
                for hd in range(NSA_HEADS):
                    b, bank, bank_free = side_banks.take()
                    rows_done = mm(bank[:, :], rel[:, hd:hd + 1].to_broadcast([REL_BUCKETS + 1, P]), hot, True, True,
                                   bank_free, signal=True)
                    rows_copied = a_copy(rows[:, 512 * hd:512 * hd + 512], bank[:, :], rows_done)
                    side_banks.give(b, rows_copied)
                    yield
                pool.wait([rows_copied])
                pool.items.append(lambda e: e.dma_start(bias_rows, rows).then_inc(rows_sem, 16))

            qT, kT = arena[:, X_AT:X_AT + Q_T * S], arena[:, X_AT + Q_T * S:X_AT + (Q_T + K_T) * S]
            val = arena[:, X_AT + (Q_T + K_T) * S:ARENA]
            xbcT = arena[:, X_AT - XBC_T * S:X_AT]
            zT = arena[:, X_AT - (XBC_T + Z_T) * S:X_AT - XBC_T * S]
            work_end = X_AT - (XBC_T + Z_T) * S
            small = take(2 * 32)
            dt, adt, acum, tmp = take(32), take(32), take(32), take(32)
            ea, dstate = take(16), take(16)
            kept_1 = cursor[0]
            qiT, kiT = take(QI_T * S), take(2 * S)
            sq = Turns([take(512), take(512)])
            roots = Turns([take(512)])
            conv_acc = Turns([take(512)])
            h_ready = norm("g_mix", x_ready, sq, roots.bufs[0])

            dtwi = split(small, 2)

            def evacuate_small(c, bank, done):
                small_tokens.append(v_copy(small[:, 32 * c:32 * c + 32], bank[:, 0:32], done))
                return small_tokens[-1]


            ki_clear = dve.do(lambda e: nc.vector.memset(kiT, 0.0))
            ki_ready = []

            def evacuate_ki(s, bank, done):
                i, buf, buf_free = sq.take()
                r, root, root_free = roots.take()
                squared = a_act(buf[:, 0:S], bank[:, 0:S], ACT.Square, done, buf_free)
                bb, total, total_free = side_banks.take()
                summed = sums(total, buf[:, 0:S], S, squared, total_free)
                sq.give(i, summed)
                ready, read = rstd(root, total, S, 1.0 / P, summed, root_free)
                side_banks.give(bb, read)
                for half in range(2):
                    p = slice(64 * half, 64 * half + 64)
                    t = v_stt(kiT[p, half * S:(half + 1) * S], bank[p, 0:S], vec("g_ki")[p, :], root[p, 0:S], ALU.mult,
                              ALU.mult, ready, ki_clear)
                ki_ready.append(t)
                roots.give(r, t)
                return [t]

            qi_ready = [None] * (QI_T // 2)

            def evacuate_qi(s, bank, done):
                for part, src in in_halves(pair(qiT, s), bank):
                    qi_ready[s] = a_copy(part, src, done)
                return [qi_ready[s]]

            drain(project(t_in["w_qi"], QI_T, hn, h_ready, evacuate_qi, behind_norm=True))
            for e in (pe, dve, act, pool):
                e.wait([params, (vecs_sem, 16)])
            small_tokens = []
            drain(project_tokens(lambda u: t_in["w_dtwi"][0], P, 32, hn, h_ready, evacuate_small))
            small_ready = small_tokens[-1]
            drain(project(t_in["w_ki"], 1, hn, h_ready, evacuate_ki), bias_table())

            score = [take(P), take(S)]
            sel_neg = [take(P), take(S)]
            best = take(8)
            relu_buf = Turns([take(512), take(512)])
            score_ready = [None, None]
            sel_ready = [None, None]
            wi = take(32)
            wi_ready = v_ts(split(wi, 2), dtwi[:, :, 16:32], float(IDX_HEADS) ** -0.5, None, ALU.mult, None, small_ready)

            def scoring():
                for t in range(QI_T):
                    for qb in range(2):
                        nk = P * (qb + 1)
                        b, bank, bank_free = side_banks.take()
                        done = mm(bank[:, :], tile(qiT, t)[:, qb * P:(qb + 1) * P], kiT, True, True, bank_free,
                                  ki_ready[0], qi_ready[t // 2], signal=True)
                        i, buf, buf_free = relu_buf.take()
                        relu = a_act(split(buf, 2)[:, :, 0:nk], split(bank[:, :], 2)[:, :, 0:nk], ACT.Relu, done, buf_free,
                                     scale=float(IDX_DIM) ** -0.5)
                        side_banks.give(b, relu)
                        for j in range(2):
                            h = 2 * t + j
                            col = wi[:, 16 * qb + h:16 * qb + h + 1]
                            src = buf[:, j * S:j * S + nk]
                            if h == 0:
                                score_ready[qb] = v_ts(score[qb], src, col, None, ALU.mult, None, relu, wi_ready)
                            else:
                                score_ready[qb] = v_stt(score[qb], src, col, score[qb], ALU.mult, ALU.add, relu,
                                                        score_ready[qb])
                        relu_buf.give(i, score_ready[qb])
                        yield
                for qb in range(2):
                    n = qb * P
                    ready = v_tt(score[qb][:, n:n + P], score[qb][:, n:n + P], mat("neg_before"), ALU.add,
                                 score_ready[qb])
                    for _ in range(TOPK // 8):
                        yield
                        top = dve.do(lambda e, qb=qb: nc.vector.max(best, score[qb]), ready)
                        ready = dve.do(lambda e, qb=qb: nc.vector.match_replace(score[qb], best, score[qb], PICKED), top)
                    ready = v_ts(sel_neg[qb], score[qb], PICKED / 2, NEG, ALU.is_gt, ALU.mult, ready)
                    sel_ready[qb] = v_tt(sel_neg[qb][:, n:n + P], sel_neg[qb][:, n:n + P], mat("neg_before"), ALU.add,
                                         ready)
                    yield

            q_ready, k_ready, v_ready = [None] * 4, [None] * 2, []

            def evacuate_q(s, bank, done):
                q_ready[s] = head_norm(pair(qT, s), bank[:, :], vec("g_q"), done, sq, roots)
                return [q_ready[s]]

            def evacuate_k(s, bank, done):
                k_ready[s] = head_norm(pair(kT, s), bank[:, :], vec("g_k"), done, sq, roots)
                return [k_ready[s]]

            def conv_silu(name, tiles, dst, ready, bias=None):
                def evacuate(s, bank, done):
                    i, acc, acc_free = conv_acc.take()
                    for j in range(2):
                        t = 2 * s + j
                        src, a = bank[:, j * S:(j + 1) * S], acc[:, j * S:(j + 1) * S]
                        tap = [vec(name, k * tiles + t) for k in range(CONV_TAPS)]
                        if bias:
                            step = v_ts(a, src, tap[3], vec(bias, t), ALU.mult, ALU.add, done, acc_free)
                        else:
                            step = v_ts(a, src, tap[3], None, ALU.mult, None, done, acc_free)
                        for back in (1, 2, 3):
                            step = v_stt(a[:, back:S], src[:, 0:S - back], tap[3 - back], a[:, back:S], ALU.mult, ALU.add,
                                         step)
                    ready[s] = a_act(dst(s), acc, ACT.Silu, step, (rows_sem, 16))
                    conv_acc.give(i, ready[s])
                    return [step]
                return evacuate

            xbc_ready = [None] * (XBC_T // 2)
            z_ready = [None] * (Z_T // 2)

            def evacuate_z(s, bank, done):
                z_ready[s] = a_act(pair(zT, s), bank[:, :], ACT.Silu, done, (rows_sem, 16))
                return [z_ready[s]]

            def projections_1():
                yield from project(t_in["w_q"], Q_T, hn, h_ready, evacuate_q)
                yield from project(t_in["w_k"], K_T, hn, h_ready, evacuate_k)
                yield from values(t_in["w_v"], val, hn, h_ready, v_ready)

            def projections_xbc():
                yield from project(t_in["w_xbc"], XBC_T, hn, h_ready,
                                   conv_silu("conv_w", XBC_T, lambda s: pair(xbcT, s), xbc_ready, "conv_b"))

            ssd_tokens = {}

            def ssd_decays():
                biased = v_tt(split(dt, 2), dtwi[:, :, 0:16], over(vec("dt_bias", 0, 16), 2), ALU.add, small_ready)
                dt_ready = softplus(dt, dt, tmp, biased)
                ea_ready = a_act(ea, vec("a_log", 0, 16), ACT.Exp)
                adt_ready = v_stt(split(adt, 2), split(dt, 2), -1.0, over(ea, 2), ALU.mult, ALU.mult, dt_ready, ea_ready)
                yield
                b, bank, bank_free = side_banks.take()
                for c in range(2):
                    mm(bank[:, 16 * c:16 * c + 16], mat("upto"), adt[:, 16 * c:16 * c + 16], True, True, bank_free, adt_ready)
                done = mm(bank[:, 32:48], ones[:, :], adt[:, 0:16], True, True, signal=True)
                acum_ready = v_copy(acum, bank[:, 0:32], done)
                t = v_tt(dstate, bank[:, 32:48], acum[:, 0:16], ALU.subtract, acum_ready)
                side_banks.give(b, t)
                ds_ready = a_act(dstate, dstate, ACT.Exp, t)
                ssd_tokens.update(dt=dt_ready, ds=ds_ready, adt=adt_ready, acum=acum_ready)

            drain(projections_1(), scoring(), ssd_decays())

            prob = Turns(relu_buf.bufs)
            prob.free = list(relu_buf.free)
            probT = Turns([take(512), take(512)])
            stats = Turns([take(8), take(8)])
            att_ready = []
            assert cursor[0] <= work_end

            att_batches = [(0, 0), (0, 4), (1, 0), (1, 2), (1, 4), (1, 6)]

            def attention(chain):
                for qb, h0 in att_batches[chain::2]:
                    nk, nh = P * (qb + 1), 4 // (qb + 1)
                    b, bank, bank_free = side_banks.take()
                    for j in range(nh):
                        h = h0 + j
                        done = mm(bank[:, j * nk:(j + 1) * nk], tile(qT, h)[:, qb * P:(qb + 1) * P],
                                  tile(kT, h // 2)[:, 0:nk], True, True, bank_free, q_ready[h // 2], k_ready[h // 4],
                                  signal=j == nh - 1)
                    i, pr, pr_free = prob.take()
                    si, st, st_free = stats.take()
                    masked = v_stt(split(pr, nh), split(bank[:, :], nh), SCALE, over(sel_neg[qb], nh), ALU.mult,
                                   ALU.add, done, pr_free, sel_ready[qb])
                    side_banks.give(b, masked)
                    top = v_red(st[:, 0:nh], split(pr, nh), ALU.max, masked, st_free, negate=True)
                    for j in range(nh):
                        e = a_act(pr[:, j * nk:(j + 1) * nk], pr[:, j * nk:(j + 1) * nk], ACT.Exp, top,
                                  bias=st[:, j:j + 1], accum=st[:, 4 + j:5 + j])
                    inv = v_rec(st[:, 4:4 + nh], st[:, 4:4 + nh], e)
                    normed = v_tt(split(pr, nh), split(pr, nh), wide(st[:, 4:4 + nh], nk), ALU.mult, inv)
                    stats.give(si, normed)
                    yield from rounds(2)
                    b, bank, bank_free = side_banks.take()
                    for j in range(4):
                        turned = turn(bank[:, j * P:(j + 1) * P], pr[:, j * P:(j + 1) * P], normed, bank_free,
                                      signal=j == 3)
                    prob.give(i, turned)
                    i, pt, pt_free = probT.take()
                    copied = a_copy(pt, bank[:, :], turned, pt_free)
                    side_banks.give(b, copied)
                    yield from rounds(2)
                    b, bank, bank_free = side_banks.take()
                    for j in range(nh):
                        kv = (h0 + j) // 2
                        for c in range(qb + 1):
                            o = (j * (qb + 1) + c) * P
                            done = mm(bank[:, j * P:(j + 1) * P], val[:, c * 512 + kv * P:c * 512 + (kv + 1) * P],
                                      pt[:, o:o + P], c == 0, c == qb, copied, bank_free, v_ready,
                                      signal=j == nh - 1 and c == qb)
                    probT.give(i, done)
                    dst = [split(part[:, (8 + h0) * S:(8 + h0 + nh) * S], nh)[:, :, qb * P:(qb + 1) * P]
                           for part in mix]
                    t = store_split(dst, split(bank[:, 0:nh * P], nh), done)
                    att_ready.append(t)
                    side_banks.give(b, t)
                    yield from rounds(2)

            drain(attention(0), attention(1), projections_xbc())
            now = barrier()
            pool.items.append(lambda e: e.dma_start(xT, t_in["x"]).then_inc(x_back_sem, 16))
            x_ready = [(x_back_sem, 16)] * (KD // 2)

            cursor[0] = kept_1
            state_T = take(1024)
            xdt = [take(1024), take(1024)]
            xds = take(1024)
            b_tok = take(2 * P)
            cbT = [[take(P), take(P)], [take(P), take(P)]]
            decay = Turns([take(512), take(512)])
            c_decayed = Turns([take(512)])
            ysq = Turns([take(512), take(512)])
            roots = Turns([take(512)])
            assert cursor[0] <= work_end

            xdt_ready = [[None, None], [None, None]]
            y_ready = [[None] * 8, [None] * 8]
            ssd_ready = []

            def ssd_prepare():
                for c in range(2):
                    for g in range(2):
                        b, bank, bank_free = side_banks.take()
                        for j in range(4):
                            done = turn(bank[:, j * P:(j + 1) * P], tile(xbcT, 4 * g + j)[:, c * P:(c + 1) * P], bank_free,
                                        xbc_ready[2 * g + j // 2], signal=j == 3)
                        dst = xdt[c][:, 512 * g:512 * g + 512]
                        t = v_tt(split(dst, 8), split(bank[:, :], 8), wide(dt[:, 16 * c + 8 * g:16 * c + 8 * g + 8], 64),
                                 ALU.mult, done, ssd_tokens["dt"])
                        xdt_ready[c][g] = t
                        side_banks.give(b, t)
                        if c == 1:
                            yield
                        if c == 0:
                            xds_ready = v_tt(split(xds[:, 512 * g:512 * g + 512], 8), split(dst, 8),
                                             wide(dstate[:, 8 * g:8 * g + 8], 64), ALU.mult, t, ssd_tokens["ds"])
                b, bank, bank_free = side_banks.take()
                for g in range(2):
                    done = turn(bank[:, g * P:(g + 1) * P], tile(xbcT, 8 + g)[:, 0:P], bank_free, xbc_ready[4],
                                signal=g == 1)
                b_ready = a_copy(b_tok, bank[:, 0:2 * P], done)
                side_banks.give(b, b_ready)
                b, bank, bank_free = side_banks.take()
                for g in range(2):
                    for c in range(2):
                        done = mm(bank[:, (2 * g + c) * P:(2 * g + c + 1) * P], tile(xbcT, 8 + g)[:, c * P:(c + 1) * P],
                                  tile(xbcT, 10 + g)[:, c * P:(c + 1) * P], True, True, bank_free, xbc_ready[4:6],
                                  signal=g + c == 2)
                for g in range(2):
                    for c in range(2):
                        cb_ready = a_copy(cbT[g][c], bank[:, (2 * g + c) * P:(2 * g + c + 1) * P], done)
                side_banks.give(b, cb_ready)
                for g in range(2):
                    b, bank, bank_free = side_banks.take()
                    done = mm(bank[:, :], b_tok[:, g * P:(g + 1) * P], xds[:, 512 * g:512 * g + 512], True, True, bank_free,
                              b_ready, xds_ready, signal=True)
                    state_ready = a_copy(state_T[:, 512 * g:512 * g + 512], bank[:, :], done)
                    side_banks.give(b, state_ready)
                    yield
                ssd_tokens.update(cb=cb_ready, state=state_ready)

            def ssd_output(c):
                for q4 in range(4):
                    g = q4 // 2
                    b, bank, bank_free = side_banks.take()
                    for j in range(4):
                        h = 4 * q4 + j
                        done = mm(bank[:, j * P:(j + 1) * P],
                                  adt[:, 16 * c + h:16 * c + h + 1].to_broadcast([P, P]), mat("upto"), True, True,
                                  bank_free, ssd_tokens["adt"], signal=j == 3)
                    i, dec, dec_free = decay.take()
                    t = v_tt(split(dec, 4), split(bank[:, :], 4),
                             wide(acum[:, 16 * c + 4 * q4:16 * c + 4 * q4 + 4], P), ALU.subtract, done, dec_free, ssd_tokens["acum"])
                    readers = [t]
                    if c == 1:
                        ci, cd, cd_free = c_decayed.take()
                        grown = a_act(cd, bank[:, :], ACT.Exp, t, cd_free)
                        readers.append(grown)
                        cd_ready = v_tt(split(cd, 4), split(cd, 4), over(tile(xbcT, 10 + g)[:, P:2 * P], 4), ALU.mult,
                                        grown)
                    side_banks.give(b, *readers)
                    t = v_tt(split(dec, 4), split(dec, 4), over(mat("neg_after"), 4), ALU.add, t)
                    t = a_act(dec, dec, ACT.Exp, t)
                    t = v_tt(split(dec, 4), split(dec, 4), over(cbT[g][c], 4), ALU.mult, t, ssd_tokens["cb"])
                    yield from rounds(2)
                    b, bank, bank_free = side_banks.take()
                    for j in range(2):
                        ch = 2 * q4 + j
                        out = bank[:, j * 2 * P:(j + 1) * 2 * P]
                        done = mm(out, xdt[c][:, ch * P:(ch + 1) * P], dec[:, j * 2 * P:(j + 1) * 2 * P], True, c == 0, t,
                                  bank_free, xdt_ready[c][g], signal=j == 1)
                        if c == 1:
                            done = mm(out, state_T[:, ch * P:(ch + 1) * P], cd[:, j * 2 * P:(j + 1) * 2 * P], False, True,
                                      cd_ready, ssd_tokens["state"], signal=j == 1)
                    decay.give(i, done)
                    if c == 1:
                        c_decayed.give(ci, done)
                    for j in range(2):
                        ch = 2 * q4 + j
                        for half in range(2):
                            p = slice(64 * half, 64 * half + 64)
                            xs = tile(xbcT, ch)[p, c * P:(c + 1) * P]
                            t = v_stt(xs, xs, vec("d_skip", ch)[p, :], bank[p, (2 * j + half) * P:(2 * j + half + 1) * P],
                                      ALU.mult, ALU.add, done, xdt_ready[c][g])
                        y_ready[c][ch] = t
                    side_banks.give(b, t)
                    yield from rounds(2)

            def ssd_gate():
                while None in z_ready:
                    yield
                for g in range(2):
                    squares = []
                    for j in range(2):
                        s = 2 * g + j
                        t = v_tt(pair(zT, s), pair(zT, s), pair(xbcT, s), ALU.mult, z_ready[s], y_ready[1][2 * s + 1],
                                 y_ready[0][2 * s + 1])
                        i, buf, buf_free = ysq.take()
                        squares.append((i, buf, a_act(buf, pair(zT, s), ACT.Square, t, buf_free)))
                    yield
                    b, bank, bank_free = side_banks.take()
                    for j, (i, buf, squared) in enumerate(squares):
                        mm(bank[:, 0:S], ones[:, :], buf[:, 0:S], j == 0, False, squared, bank_free)
                        done = mm(bank[:, 0:S], ones[:, :], buf[:, S:2 * S], False, j == 1, signal=True)
                        ysq.give(i, done)
                    r, root, root_free = roots.take()
                    ready, read = rstd(root, bank, S, 1.0 / (SSD_W // SSD_GROUPS), done, root_free)
                    side_banks.give(b, read)
                    for k in range(4 * g, 4 * g + 4):
                        t = v_stt(tile(zT, k), tile(zT, k), vec("g_ssd", k), root[:, 0:S], ALU.mult, ALU.mult, ready)
                        if k % 2:
                            t = store_split(both(mix, (k - 1) * S, (k + 1) * S), pair(zT, k // 2), t)
                            ssd_ready.extend([t, t])
                    roots.give(r, t)
                    yield

            def project_part(w, k_first, x, x_part_ready, gathered=None):
                add = residual(x_ready, gathered)
                for s in range(KD // 2):
                    b, bank, bank_free = gemm_banks.take()
                    for j in range(2):
                        done = yield from column(
                            bank[:, j * S:(j + 1) * S], lambda u: w[s],
                            lambda k: both(x, (k_first + k) * S, (k_first + k + 1) * S), x_part_ready, 8, bank_free)
                        if j == 0:
                            yield
                    gemm_banks.give(b, *add(s, bank, done))
                    yield

            drain(one_after_another(ssd_prepare(), together(ssd_output(0), ssd_output(1)), ssd_gate()),
                  one_after_another(project(t_in["w_z"], Z_T, hn, h_ready, evacuate_z),
                                    project_part(t_in["w_out_att"], 8, mix, [att_ready[-1]] * 8)))

            gathered = []
            drain(project_part(t_in["w_out_ssd"], 0, mix, ssd_ready, gathered))
            barrier()
            cursor[0] = 0
            mlp(t_in["w_up"], t_in["w_down"], "g_mlp", x_ready, gathered)
            barrier()
            pool.items.append(lambda e: e.dma_start(x_kept, xT).then_inc(x_saved_sem, 16))
            x_saved = (x_saved_sem, 16)

            cursor[0] = 0
            bias = take(NSA_HEADS * S)
            bias3 = split(bias, NSA_HEADS)
            pool.wait([(rows_sem, 16)])
            grid = bass.AP(tensor=bias_rows.tensor, offset=P - 1,
                           ap=[[NSA_HEADS * 2 * S - 1, P], [2 * S, NSA_HEADS], [1, S]])
            pool.items.append(lambda e: e.dma_start(bias3, grid).then_inc(toep_sem, 16))
            bias_ready = (toep_sem, 16)
            first_half_at = cursor[0]
            gdn_in = [take(3 * HALF_HEADS * S), None]
            gdn_z = [take(HALF_HEADS * S), None]
            gab, gates, beta = take(80), take(48), take(16)
            keep2 = cursor[0]
            w_cmp2 = take(4 * P)
            pool.items.append(lambda e: e.dma_start(w_cmp2, t_in["w_cmp2"]).then_inc(cmp2_sem, 16))
            cmp2_ready = (cmp2_sem, 16)
            qT, kcvc, kskw = [arena[:, X_AT + a * S:X_AT + b * S] for a, b in ((0, 8), (8, 12), (12, 16))]
            vsvw = take(2 * 512)
            sq = Turns([take(512), take(512)])
            roots = Turns([take(512)])
            conv_acc = Turns([take(512)])
            shared_at = cursor[0]
            blocks = [take(CMP_BLOCK * 2 * N_CMP), take(CMP_BLOCK * 2 * N_CMP)]
            cursor[0] = shared_at + 2 * 512 + 2 * 640
            hid = [take(2 * 2 * N_CMP), take(2 * 2 * N_CMP)]
            hid_rows = [buf[0:2 * N_CMP, 0:CMP_HID] for buf in blocks]
            kcmpT = take(2 * N_CMP)
            vcmp = take(2 * P)
            h_ready = norm("ln1", x_ready, sq, roots.bufs[0], gathered=gathered)

            gab3 = split(gab, 2)
            gab_tokens = []

            def evacuate_gab(c, bank, done):
                gab_tokens.append(v_copy(gab[:, 40 * c:40 * c + 40], bank[:, 0:40], done))
                return gab_tokens[-1]

            kv_ready = [None] * 4

            def evacuate_kv(s, bank, done):
                for part, src in in_halves(pair(kcvc, s) if s < 2 else pair(kskw, s - 2), bank):
                    kv_ready[s] = a_copy(part, src, done, x_saved)
                return [kv_ready[s]]

            nq_ready = [None] * 4

            def evacuate_nq(s, bank, done):
                nq_ready[s] = a_copy(pair(qT, s), bank[:, :], done)
                return [nq_ready[s]]

            vs_ready = []
            drain(project(t_in["w_kv"], 8, hn, h_ready, evacuate_kv, behind_norm=True))
            drain(project_tokens(lambda u: t_in["w_gab"][0], P, 40, hn, h_ready, evacuate_gab))
            gab_ready = gab_tokens[-1]
            gates_ready = a_act(split(gates, 2), gab3[:, :, 0:24], ACT.Sigmoid, gab_ready)
            beta_ready = a_act(split(beta, 2), gab3[:, :, 32:40], ACT.Sigmoid, gab_ready)

            def compress():
                blk_ready, blk_parts = [None, None], [None, None]
                for m in range(2):
                    for g in range(2):
                        src = kcvc[:, (2 * m + g) * S:(2 * m + g + 1) * S].rearrange("p (m r) -> p r m", r=CMP_STRIDE)
                        dst = split(blocks[m], CMP_BLOCK)[:, :, g * N_CMP:(g + 1) * N_CMP]
                        for half in range(2):
                            rr = slice(half * CMP_STRIDE, (half + 1) * CMP_STRIDE)
                            pe_cols = vec(("pe_k", "pe_v")[m], half * CMP_STRIDE, CMP_STRIDE)
                            blk_ready[m] = v_tt(dst[:, rr, :], src[:, :, half:half + N_CMP], wide(pe_cols, N_CMP), ALU.add,
                                                kv_ready[m])
                    lo_at = 8 * S + m * CMP_BLOCK * 2 * N_CMP
                    blk_parts[m] = both(mix, lo_at, lo_at + CMP_BLOCK * 2 * N_CMP)
                    blk_ready[m] = store_split(blk_parts[m], blocks[m], blk_ready[m])
                yield
                n = 2 * N_CMP
                for m in range(2):
                    b, bank, bank_free = side_banks.take()
                    per_unit = UNIT // CMP_HID
                    for r in range(CMP_BLOCK):
                        if r % per_unit == 0:
                            i, unit, split_done = weights(t_in["w_cmp1"][4 * m + r // (2 * per_unit)])
                        o = (r % per_unit) * CMP_HID
                        last = r % per_unit == per_unit - 1
                        done = products(bank[0:n, 0:CMP_HID], both(blk_parts[m], r * n, (r + 1) * n),
                                        [part[:, o:o + CMP_HID] for part in unit], r == 0, r == CMP_BLOCK - 1,
                                        split_done, blk_ready[m], bank_free, signal=last)
                        if last:
                            unit_free[i] = done
                        if r % (2 * per_unit) == 2 * per_unit - 1 and r < CMP_BLOCK - 1:
                            yield
                    gelu = a_act(hid_rows[m], bank[0:n, 0:CMP_HID], ACT.Gelu_apprx_tanh, done)
                    side_banks.give(b, gelu)
                    yield
                    b, bank, bank_free = side_banks.take()
                    for hh in range(2):
                        done = turn(bank[:, hh * n:(hh + 1) * n], hid_rows[m][:, hh * P:(hh + 1) * P], gelu, bank_free,
                                    signal=hh == 1)
                    gelu = v_copy(hid[m], bank[:, 0:2 * n], done)
                    side_banks.give(b, gelu)
                    yield
                    b, bank, bank_free = side_banks.take()
                    if m == 0:
                        for hh in range(2):
                            done = mm(bank[:, 0:n], w_cmp2[:, hh * P:(hh + 1) * P], hid[0][:, hh * n:(hh + 1) * n],
                                      hh == 0, hh == 1, gelu, bank_free, cmp2_ready, signal=hh == 1)
                        cmp_ready.append(a_copy(kcmpT, bank[:, 0:n], done))
                    else:
                        for g in range(2):
                            for hh in range(2):
                                done = mm(bank[0:N_CMP, g * P:(g + 1) * P],
                                          hid[1][:, hh * n + g * N_CMP:hh * n + (g + 1) * N_CMP],
                                          w_cmp2[:, (2 + hh) * P:(3 + hh) * P], hh == 0, hh == 1, gelu, bank_free, cmp2_ready,
                                          signal=g + hh == 2)
                        cmp_ready.append(a_copy(vcmp[0:N_CMP, :], bank[0:N_CMP, 0:2 * P], done))
                    side_banks.give(b, cmp_ready[-1])
                    yield

            cmp_ready = []

            def nsa_projections():
                yield from project(t_in["w_nq"], 8, hn, h_ready, evacuate_nq, fine=False)
                yield from values(t_in["w_vsvw"], vsvw, hn, h_ready, vs_ready)

            decays_at = vecs[:, vec_at["g_mix"]:vec_at["g_mlp"]]
            graw, gcum, glast, gtmp, k_scale, kd_scale = [decays_at[:, 16 * n:16 * n + 16] for n in range(6)]
            ea2 = decays_at[:, 96:104]
            gdn_tokens = {}

            def gdn_decays():
                biased = v_tt(split(graw, 2), gab3[:, :, 24:32], over(vec("dt_bias2", 0, 8), 2), ALU.add, gab_ready)
                sp_ready = softplus(graw, graw, gtmp, biased)
                ea_ready = a_act(ea2, vec("a_log2", 0, 8), ACT.Exp)
                graw_ready = v_stt(split(graw, 2), split(graw, 2), -1.0, over(ea2, 2), ALU.mult, ALU.mult, sp_ready, ea_ready)
                yield
                b, bank, bank_free = side_banks.take()
                mm(bank[:, 0:16], mat("upto64"), graw, True, True, graw_ready, bank_free)
                done = mm(bank[:, 16:32], mat("ones64"), graw, True, True, signal=True)
                gcum_ready = v_copy(gcum, bank[:, 0:16], done)
                t = v_tt(glast, bank[:, 16:32], gcum, ALU.subtract, gcum_ready)
                side_banks.give(b, t)
                kd_ready = a_act(kd_scale, glast, ACT.Exp, t)
                t = a_act(k_scale, gcum, ACT.Exp, gcum_ready)
                ks_ready = v_tt(k_scale, k_scale, beta, ALU.mult, t, beta_ready)
                gdn_tokens.update(graw=graw_ready, gcum=gcum_ready, kd=kd_ready, ks=ks_ready)

            drain(compress(), nsa_projections(), gdn_decays())

            gdn_ready = [[None] * 6, [None] * 6]
            gdn_z_ready = [[None] * 2, [None] * 2]

            def gdn_projections(half):
                def evacuate_z2(s, bank, done):
                    gdn_z_ready[half][s] = a_act(pair(gdn_z[half], s), bank[:, :], ACT.Silu, done)
                    return [gdn_z_ready[half][s]]

                yield from project(t_in[f"w_gdn{half}"], 12, hn, h_ready,
                                   conv_silu2(half, lambda s: pair(gdn_in[half], s), gdn_ready[half]))
                yield from project(t_in[f"w_gz{half}"], 4, hn, h_ready, evacuate_z2)

            def conv_silu2(half, dst, ready):
                def evacuate(s, bank, done):
                    i, acc, acc_free = conv_acc.take()
                    for j in range(2):
                        t = 12 * half + 2 * s + j
                        src, a = bank[:, j * S:(j + 1) * S], acc[:, j * S:(j + 1) * S]
                        step = v_ts(a, src, vec("conv_w2", 3 * 24 + t), None, ALU.mult, None, done, acc_free)
                        for back in (1, 2, 3):
                            step = v_stt(a[:, back:S], src[:, 0:S - back], vec("conv_w2", (3 - back) * 24 + t),
                                         a[:, back:S], ALU.mult, ALU.add, step)
                    ready[s] = a_act(dst(s), acc, ACT.Silu, step)
                    conv_acc.give(i, ready[s])
                    return [step]
                return evacuate

            p_cmp = [take(NSA_HEADS * 7), take(NSA_HEADS * N_CMP)]
            cst = take(3 * NSA_HEADS)
            pc_ready = [None, None]

            def compressed():
                for qb in range(2):
                    nc_ = (7, N_CMP)[qb]
                    b, bank, bank_free = side_banks.take()
                    for h in range(NSA_HEADS):
                        g = h // 4
                        done = mm(bank[:, h * nc_:(h + 1) * nc_], tile(qT, h)[:, qb * P:(qb + 1) * P],
                                  kcmpT[:, g * N_CMP:g * N_CMP + nc_], True, True, bank_free, nq_ready[h // 2],
                                  cmp_ready[0], signal=h == NSA_HEADS - 1)
                    pc = p_cmp[qb].rearrange("p (h n) -> p h n", h=NSA_HEADS)
                    off = P - P * qb
                    grid_c = bias3[:, :, off + 31:off + 31 + CMP_STRIDE * (nc_ - 1) + 1:CMP_STRIDE]
                    t = v_stt(pc, bank[:, 0:NSA_HEADS * nc_].rearrange("p (h n) -> p h n", h=NSA_HEADS), SCALE, grid_c,
                              ALU.mult, ALU.add, done, bias_ready)
                    side_banks.give(b, t)
                    m, keep_m, s = cst[:, 0:8], cst[:, 8:16], cst[:, 16:24]
                    t = v_red(m, pc, ALU.max, t, pc_ready[0])
                    t = v_ts(keep_m, m, NEG / 10, None, ALU.is_gt, None, t)
                    t = v_tt(m, m, keep_m, ALU.mult, t)
                    t = v_tt(pc, pc, wide(m, nc_), ALU.subtract, t)
                    t = a_act(p_cmp[qb], p_cmp[qb], ACT.Exp, t)
                    t = v_red(s, pc, ALU.add, t)
                    t = v_ts(s, s, 1e-30, None, ALU.max, None, t)
                    t = v_rec(s, s, t)
                    gate = gates[:, 24 * qb:24 * qb + 24].rearrange("p (h b) -> p h b", b=3)[:, :, 0]
                    t = v_tt(s, s, gate, ALU.mult, t, gates_ready)
                    pc_ready[qb] = v_tt(pc, pc, wide(s, nc_), ALU.mult, t)
                    yield

            stats = Turns([take(4), take(4)])
            assert cursor[0] <= X_AT
            cursor[0] = shared_at
            prob = Turns([take(512), take(512)])
            probT = Turns([take(640), take(640)])
            nsa_ready = []

            def nsa(chain):
                for qb in range(2):
                    nk, nc_, off = P * (qb + 1), (7, N_CMP)[qb], P - P * qb
                    for hd in range(chain, NSA_HEADS, 2):
                        g = hd // 4
                        b, bank, bank_free = side_banks.take()
                        for br in range(2):
                            done = mm(bank[:, br * nk:(br + 1) * nk], tile(qT, hd)[:, qb * P:(qb + 1) * P],
                                      tile(kskw, 2 * br + g)[:, 0:nk], True, True, bank_free, nq_ready[hd // 2],
                                      kv_ready[2:4], signal=br == 1)
                        i, pr, pr_free = prob.take()
                        si, st, st_free = stats.take()
                        pr3 = split(pr[:, 0:2 * nk], 2)
                        t = v_stt(pr3, split(bank[:, 0:2 * nk], 2), SCALE, over(bias3[:, hd, off:off + nk], 2), ALU.mult,
                                  ALU.add, done, pr_free, bias_ready)
                        side_banks.give(b, t)
                        t = v_red(st[:, 0:2], pr3, ALU.max, t, st_free, negate=True)
                        for br in range(2):
                            e = a_act(pr3[:, br, :], pr3[:, br, :], ACT.Exp, t, bias=st[:, br:br + 1],
                                      accum=st[:, 2 + br:3 + br])
                        t = v_rec(st[:, 2:4], st[:, 2:4], e)
                        t = v_tt(st[:, 2:4], st[:, 2:4], gates[:, 24 * qb + 3 * hd + 1:24 * qb + 3 * hd + 3], ALU.mult, t,
                                 gates_ready)
                        normed = v_tt(pr3, pr3, wide(st[:, 2:4], nk), ALU.mult, t)
                        stats.give(si, normed)
                        yield from rounds(2)
                        b, bank, bank_free = side_banks.take()
                        blocks_n = 2 * (qb + 1)
                        for j in range(blocks_n):
                            turned = turn(bank[:, j * P:(j + 1) * P], pr[:, j * P:(j + 1) * P], normed, bank_free,
                                          signal=j == blocks_n - 1)
                        prob.give(i, turned)
                        bc, bank_c, bank_c_free = side_banks.take()
                        pc = p_cmp[qb].rearrange("p (h n) -> p h n", h=NSA_HEADS)
                        turned_c = turn(bank_c[0:nc_, 0:P], pc[:, hd, :], pc_ready[qb], bank_c_free, signal=True)
                        i, pt, pt_free = probT.take()
                        t1 = a_copy(pt[:, 0:blocks_n * P], bank[:, 0:blocks_n * P], turned, pt_free)
                        t2 = v_copy(pt[0:nc_, 512:640], bank_c[0:nc_, 0:P], turned_c, pt_free)
                        side_banks.give(b, t1)
                        side_banks.give(bc, t2)
                        yield
                        b, bank, bank_free = side_banks.take()
                        for j in range(blocks_n):
                            br, c = j // (qb + 1), j % (qb + 1)
                            mm(bank[:, 0:P], vsvw[:, c * 512 + br * S + g * P:c * 512 + br * S + (g + 1) * P],
                               pt[:, j * P:(j + 1) * P], j == 0, False, t1, bank_free, vs_ready)
                        done = mm(bank[:, 0:P], vcmp[0:nc_, g * P:(g + 1) * P], pt[0:nc_, 512:640], False, True, t2,
                                  cmp_ready[1], signal=True)
                        probT.give(i, done)
                        t = store_split(both(mix, hd * S + qb * P, hd * S + (qb + 1) * P), bank[:, 0:P], done)
                        nsa_ready.append(t)
                        side_banks.give(b, t)
                        yield

            drain(one_after_another(compressed(), together(nsa(0), nsa(1))), gdn_projections(0))
            barrier()

            cursor[0] = 0
            spare = NSA_HEADS * S
            state = take(HALF_HEADS * P)
            conv_acc = Turns([take(512)])
            D_ = take(512)
            assert cursor[0] <= spare
            cursor[0] = keep2
            eg = take(HALF_HEADS * S)
            chain_bufs = [[take(512), take(512), take(256), D_[:, 256 * c:256 * c + 256],
                           [take(256), take(256)], [take(256), take(256)], [take(256), take(256)],
                           [take(256), take(256)]] for c in range(2)]
            gdn_in[1], gdn_z[1] = take(3 * HALF_HEADS * S), take(HALF_HEADS * S)
            def delta_rule(half, chain):
                while None in gdn_ready[half] or None in gdn_z_ready[half]:
                    yield
                two = 2
                qkv, z = gdn_in[half], gdn_z[half]
                in_ready, z_ok = gdn_ready[half], gdn_z_ready[half][chain]
                nq, nk_, nv = [qkv[:, m * 1024 + 512 * chain:m * 1024 + 512 * chain + 512] for m in range(3)]
                q_in, k_in, v_in = [in_ready[2 * m + chain] for m in range(3)]
                h0 = HALF_HEADS * half + two * chain
                eg_c = eg[:, 512 * chain:512 * chain + 512]
                st = state[:, 256 * chain:256 * chain + 256]
                wide_a, wide_b, E_, D_, qkT, kd, u, wT = chain_bufs[chain]
                decT, LT, LTm, Xs = wide_a[:, 0:256], wide_a[:, 256:512], wide_b[:, 0:256], wide_b[:, 256:512]
                vb, kbg = LTm, Xs
                heads = [slice(j * P, (j + 1) * P) for j in range(two)]
                unit, root_free = [], chain_done[chain]
                for src, src_ready, factor in ((nq, q_in, SCALE), (nk_, k_in, 1.0)):
                    squared = a_act(wide_a, src, ACT.Square, src_ready, root_free)
                    yield
                    b, total, total_free = side_banks.take()
                    summed = sums(total, wide_a, 512, squared, total_free)
                    ready, read = rstd(wide_b, total, 512, 1.0, summed, root_free)
                    side_banks.give(b, read)
                    root_free = v_stt(src, src, factor, wide_b, ALU.mult, ALU.mult, ready)
                    unit.append(root_free)
                    yield
                prepared = [None, None]
                xe_done = None
                for p in range(2):
                    tok = slice(p * P, (p + 1) * P)
                    col = slice(8 * p + h0, 8 * p + h0 + two)
                    b, bank, bank_free = side_banks.take()
                    for j in range(two):
                        c0 = 8 * p + h0 + j
                        done = mm(bank[:, heads[j]], graw[:, c0:c0 + 1].to_broadcast([P, P]), mat("upto64"), True,
                                  True, gdn_tokens["graw"], bank_free)
                        done = mm(bank[:, 256 + j * P:256 + (j + 1) * P], beta[:, c0:c0 + 1].to_broadcast([P, P]),
                                  mat("ident"), True, True, beta_ready, signal=j == 1)
                    bk, bank_k, bank_k_free = side_banks.take()
                    for j in range(two):
                        kj = tile(nk_, j)[:, tok]
                        kk_done = mm(bank_k[:, heads[j]], kj, kj, True, True, bank_k_free, unit)
                        kk_done = mm(bank_k[:, 256 + j * P:256 + (j + 1) * P], kj, tile(nq, j)[:, tok], True, True,
                                     signal=j == 1)
                    t = v_tt(split(decT, two), split(bank[:, 0:256], two), wide(gcum[:, col], P), ALU.subtract, done,
                             gdn_tokens["gcum"], unit)
                    t2 = v_tt(split(decT, two), split(decT, two), over(mat("neg_after64"), two), ALU.add, t)
                    eg_p = split(eg_c, two)[:, :, tok]
                    grown = a_act(eg_p, split(bank[:, 0:256], two), ACT.Exp, t)
                    dec_ready = a_act(decT, decT, ACT.Exp, t2)
                    t = v_tt(LT, bank_k[:, 0:256], decT, ALU.mult, kk_done, dec_ready)
                    lt_ready = v_tt(LT, LT, bank[:, 256:512], ALU.mult, t, grown)
                    side_banks.give(b, lt_ready)
                    t = v_tt(split(E_, two), split(LT, two), over(mat("level1"), two), ALU.mult, lt_ready)
                    e_ready = v_tt(split(E_, two), over(mat("ident"), two), split(E_, two), ALU.subtract, t)
                    qk_ready = v_tt(qkT[p], bank_k[:, 256:512], decT, ALU.mult, kk_done, dec_ready)
                    side_banks.give(bk, qk_ready)
                    yield from rounds(2)
                    b, bank, bank_free = side_banks.take()
                    for j in range(two):
                        done = turn(bank[:, heads[j]], E_[:, heads[j]], e_ready, bank_free, signal=j == 1)
                    d_ready = a_copy(D_, bank[:, 0:256], done)
                    side_banks.give(b, d_ready)
                    for b_size in LEVELS:
                        m_ready = v_tt(split(LTm, two), split(LT, two), over(mat(f"level{b_size}"), two), ALU.mult,
                                       lt_ready, xe_done, prepared[0])
                        yield
                        b, bank, bank_free = side_banks.take()
                        for q in heads:
                            done = mm(bank[:, q], LTm[:, q], D_[:, q], True, True, m_ready, d_ready, bank_free,
                                      signal=q is heads[1])
                        x_ok = a_copy(Xs, bank[:, 0:256], done, xe_done)
                        side_banks.give(b, x_ok)
                        yield
                        last_level = b_size == LEVELS[-1]
                        b, bank, bank_free = side_banks.take()
                        for q in heads:
                            xe_done = mm(bank[:, q], Xs[:, q], E_[:, q], True, True, x_ok, e_ready, bank_free,
                                         signal=last_level and q is heads[1])
                        if not last_level:
                            for q in heads:
                                xe_done = mm(bank[:, 256 + q.start:256 + q.stop], E_[:, q], Xs[:, q], True, True,
                                             signal=q is heads[1])
                            d_ready = v_tt(D_, D_, bank[:, 256:512], ALU.subtract, xe_done)
                        e_ready = v_tt(E_, E_, bank[:, 0:256], ALU.subtract, xe_done)
                        side_banks.give(b, e_ready)
                    b, bank, bank_free = side_banks.take()
                    for j in range(two):
                        turn(bank[:, heads[j]], tile(nk_, j)[:, tok], bank_free, unit)
                    for j in range(two):
                        done = turn(bank[:, 256 + j * P:256 + (j + 1) * P], tile(nv, j)[:, tok], v_in, signal=j == 1)
                    t1 = v_tt(split(kbg, two), split(bank[:, 0:256], two), wide(k_scale[:, col], P), ALU.mult, done,
                              gdn_tokens["ks"])
                    t2 = v_tt(split(kd[p], two), split(bank[:, 0:256], two), wide(kd_scale[:, col], P), ALU.mult,
                              gdn_tokens["kd"])
                    t3 = v_tt(split(vb, two), split(bank[:, 256:512], two), wide(beta[:, col], P), ALU.mult)
                    side_banks.give(b, t3)
                    q3 = split(nq, two)[:, :, tok]
                    qg_ok = v_tt(q3, q3, eg_p, ALU.mult, grown, qk_ready)
                    yield
                    b, bank, bank_free = side_banks.take()
                    for q in heads:
                        mm(bank[:, q], E_[:, q], vb[:, q], True, True, e_ready, t3, bank_free)
                    for q in heads:
                        done = mm(bank[:, 256 + q.start:256 + q.stop], kbg[:, q], E_[:, q], True, True,
                                  signal=q is heads[1])
                    u_ok = a_copy(u[p], bank[:, 0:256], done)
                    w_ok = a_copy(wT[p], bank[:, 256:512], done)
                    side_banks.give(b, w_ok)
                    xe_done = done
                    prepared[p] = [u_ok, w_ok, qg_ok, qk_ready, t2, done]
                    yield
                o3 = split(nv, two)
                o_ready = None
                state_ok = None
                for c in range(S // CHUNK):
                    p, odd = c // 2, c % 2
                    rows = slice(CHUNK * odd, CHUNK * odd + CHUNK)
                    ready = prepared[p]
                    if c:
                        b, bank, bank_free = side_banks.take()
                        for q in heads:
                            done = mm(bank[:, q], wT[p][:, q], st[:, q], True, True, ready, state_ok, bank_free,
                                      signal=q is heads[1])
                        new_v = v_tt(u[p][rows, :], u[p][rows, :], bank[rows, 0:256], ALU.subtract, done, ready,
                                     state_ok, o_ready)
                        side_banks.give(b, new_v)
                        ready = [ready, new_v]
                        yield
                    b, bank, bank_free = side_banks.take()
                    for j in range(two):
                        q = heads[j]
                        out = bank[:, j * CHUNK:(j + 1) * CHUNK]
                        if c:
                            mm(out, st[:, q], tile(nq, j)[:, c * CHUNK:(c + 1) * CHUNK], True, False, ready, state_ok,
                               bank_free)
                        o_done = mm(out, u[p][:, q], qkT[p][:, j * P + CHUNK * odd:j * P + CHUNK * odd + CHUNK],
                                    c == 0, True, ready, bank_free, signal=j == 1)
                    bs, bank_s, bank_s_free = side_banks.take()
                    if c < S // CHUNK - 1:
                        for q in heads:
                            done = mm(bank_s[:, q], kd[p][rows, q], u[p][rows, q], True, True, ready, bank_s_free,
                                      signal=q is heads[1])
                        last = c * CHUNK + CHUNK - 1
                        for j in range(two):
                            q = heads[j]
                            if c == 0:
                                state_ok = v_copy(st[:, q], bank_s[:, q], done, o_done)
                            else:
                                state_ok = v_stt(st[:, q], st[:, q], eg_c[:, j * S + last:j * S + last + 1],
                                                 bank_s[:, q], ALU.mult, ALU.add, done, o_done, state_ok)
                    side_banks.give(bs, state_ok)
                    o_ready = a_copy(o3[:, :, c * CHUNK:(c + 1) * CHUNK], split(bank[:, 0:2 * CHUNK], two), o_done)
                    side_banks.give(b, o_ready)
                    yield
                squared = a_act(wide_a, nv, ACT.Square, o_ready)
                yield
                b, total, total_free = side_banks.take()
                summed = sums(total, wide_a, 512, squared, total_free)
                ready, read = rstd(wide_b, total, 512, 1.0 / P, summed, prepared)
                side_banks.give(b, read)
                t = v_stt(wide_b, nv, vec("gdn_norm"), wide_b, ALU.mult, ALU.mult, ready)
                t = v_tt(wide_b, wide_b, pair(z, chain), ALU.mult, t, z_ok)
                at = (8 + h0) * S
                chain_done[chain] = store_split(both(mix, at, at + 2 * S), wide_b, t)
                gdn_done.append(chain_done[chain])
                yield from rounds(2)

            gdn_done, chain_done = [], [None, None]
            merged = arena[:, first_half_at:first_half_at + KD * S]
            merge_ready = [None] * (KD // 2)

            def merge(m, out_ready, gate_buf):
                while len(gdn_done) < 2:
                    yield
                room = gdn_done[0:2]
                for s in range(KD // 2):
                    gb, bank, bank_free = gemm_banks.take()
                    for j in range(2):
                        done = yield from column(
                            bank[:, j * S:(j + 1) * S], lambda u: t_in["w_merge"][KD * m + 2 * s + j],
                            lambda k: both(hn, k * S, (k + 1) * S), h_ready, KD, bank_free)
                        yield
                    i, gate, gate_free = gate_buf.take()
                    open_ = a_act(gate, bank[:, :], ACT.Sigmoid, done, gate_free)
                    gemm_banks.give(gb, open_)
                    b, bank, bank_free = gemm_banks.take()
                    for j in range(2):
                        done = yield from column(
                            bank[:, j * S:(j + 1) * S], lambda u: t_in["w_papb"][(KD // 2) * m + s],
                            lambda k: both(mix, (8 * m + k) * S, (8 * m + k + 1) * S), [out_ready] * 8, 8, bank_free)
                        if j == 0:
                            yield
                    if m == 0:
                        t = v_tt(pair(merged, s), bank[:, :], gate, ALU.mult, done, open_, room)
                        gate_buf.give(i, t)
                        gemm_banks.give(b, t)
                    else:
                        t = v_tt(gate, bank[:, :], gate, ALU.mult, done, open_)
                        gemm_banks.give(b, t)
                        t = v_tt(pair(merged, s), pair(merged, s), gate, ALU.add, t, merge_ready[s])
                        gate_buf.give(i, t)
                    merge_ready[s] = t
                    yield

            drain(one_after_another(delta_rule(0, 0), delta_rule(1, 0)), one_after_another(delta_rule(0, 1), delta_rule(1, 1)),
                  one_after_another(gdn_projections(1), merge(0, nsa_ready, Turns([conv_acc.bufs[0]]))))
            barrier()

            pool.items.append(lambda e: e.dma_start(xT, x_kept).then_inc(x_back_sem, 16))
            x_ready = [(x_back_sem, 32)] * (KD // 2)
            cursor[0] = 0
            drain(merge(1, gdn_done, Turns([take(512), take(512)])))
            h_free = (pe.sem, pe.count)
            merged_ready = []
            for s in range(KD // 2):
                t = store_split(both(hn, 2 * s * S, 2 * (s + 1) * S), pair(merged, s), merge_ready[s], h_free)
                merged_ready += [t, t]
            drain(project(t_in["w_o"], KD, hn, merged_ready, residual(x_ready, gathered)))
            barrier()
            cursor[0] = 0
            mlp(t_in["w_up2"], t_in["w_down2"], "ln2", x_ready, gathered)
            barrier()
            cursor[0] = 0
            sq = Turns([take(512), take(512)])
            root = take(S)
            y = take(KD * S)
            y_tok = norm("ln_f", x_ready, sq, root, out=y, gathered=gathered)
            for j in range(4):
                sp.wait([y_tok[4 * j + 3]])
                sp.items.append(lambda e, j=j: e.dma_start(x_out[:, j * 1024:(j + 1) * 1024],
                                                           y[:, j * 1024:(j + 1) * 1024]).then_inc(out_sem, 16))
            sp.wait([(out_sem, 64), (rows_sem, 16), x_saved])
            return (pe, dve, act, pool, sp), order

        _, plan = emit(None)
        (pe, dve, act, pool, sp), _ = emit(plan)

        block = ctx.enter_context(nc.Block())

        @block.sync
        def _(e):
            sp.run(e)

        @block.tensor
        def _(e):
            pe.run(e)

        @block.vector
        def _(e):
            dve.run(e)

        @block.scalar
        def _(e):
            act.run(e)

        @block.gpsimd
        def _(e):
            pool.run(e)


def columns(w, k_tiles=KD):
    n = w.shape[1] // P
    return np.ascontiguousarray(w.reshape(k_tiles, P, n, P).transpose(2, 1, 0, 3)).reshape(n, P, -1)


def halves(w):
    return np.ascontiguousarray(columns(w, 8).reshape(-1, 2, P, UNIT).transpose(0, 2, 1, 3)).reshape(-1, P, PIECE)


def pieces(w, width):
    return np.ascontiguousarray(w.reshape(KD, P, width).transpose(1, 0, 2).reshape(P, -1, PIECE).transpose(1, 0, 2))


def padded(w):
    return np.concatenate([w, np.zeros((w.shape[0], P - w.shape[1]), w.dtype)], axis=1)


def row_tiles(w, k_tiles):
    return np.ascontiguousarray(w.reshape(k_tiles, P, -1).transpose(1, 0, 2)).reshape(P, -1)


def channels(v):
    return np.ascontiguousarray(v.reshape(-1, P).T)


def everywhere(v):
    return np.broadcast_to(v.reshape(1, -1), (P, v.size))


def kernel(**inputs):
    import numpy as _np
    import concourse.bacc as _bacc
    from concourse import mybir as _mybir
    from concourse.bass_utils import run_bass_kernel_spmd as _run

    a = {k: _np.asarray(v) for k, v in inputs.items()}
    w_in, w_in2 = a["w_in"][0], a["w_in_2"][0]
    at, cut = 0, {}
    for name, n in (("z", 1024), ("xbc", 1536), ("dt", 16), ("q", 1024), ("k", 512), ("v", 512), ("qi", 1024),
                    ("ki", 64), ("wi", 16)):
        cut[name] = w_in[:, at:at + n]
        at += n
    at = 0
    for name, n in (("nq", 1024), ("kv", 1536), ("gate", 24), ("qkv", 3072), ("gz", 1024), ("a", 8), ("b", 8),
                    ("merge", 4096)):
        cut[name] = w_in2[:, at:at + n]
        at += n
    kv = [cut["kv"][:, 256 * i:256 * i + 256] for i in range(6)]
    half = [_np.concatenate([cut["qkv"][:, 1024 * m + 512 * h:1024 * m + 512 * h + 512] for m in range(3)], axis=1)
            for h in range(2)]
    conv2 = a["conv_w_2"][0]
    conv2 = _np.concatenate([conv2[:, 1024 * m + 512 * h:1024 * m + 512 * h + 512] for h in range(2)
                             for m in range(3)], axis=1)
    cmp1 = [row_tiles(a[n][0], CMP_BLOCK).reshape(P, -1, PIECE).transpose(1, 0, 2) for n in ("cmp_w1_k_2", "cmp_w1_v_2")]
    papb = [halves(a[n][0]) for n in ("w_pa_2", "w_pb_2")]

    def down(w):
        return _np.concatenate([columns(w[D * f:D * (f + 1)]) for f in range(FF // D)])

    mats, hot = constants()
    vec_parts = dict(
        g_mix=channels(a["g_mix"][0]), g_ssd=channels(a["g_ssd"][0]), g_q=channels(a["g_q"][0]),
        g_k=channels(a["g_k"][0]), g_ki=channels(_np.concatenate([a["g_kidx"][0], a["g_kidx"][0]])),
        conv_w=channels(a["conv_w"][0]), conv_b=channels(a["conv_b"][0]),
        d_skip=channels(_np.repeat(a["d_skip"][0], 64)), dt_bias=everywhere(a["dt_bias"][0]),
        a_log=everywhere(a["a_log"][0]), g_mlp=channels(a["g_mlp"][0]), ln1=channels(a["ln1_w_2"][0]),
        conv_w2=channels(conv2), a_log2=everywhere(a["a_log_2"][0]), dt_bias2=everywhere(a["dt_bias_2"][0]),
        gdn_norm=channels(a["gdn_norm_w_2"][0]), ln2=channels(a["ln2_w_2"][0]), ln_f=channels(a["ln_f_w_2"]),
        pe_k=a["cmp_pe_k_2"][0].T, pe_v=a["cmp_pe_v_2"][0].T)
    arrays = {
        "x": row_tiles(a["x"][0].T, KD),
        "vecs": _np.concatenate([vec_parts[n] for n in VECS], axis=1),
        "mats": mats,
        "hot": hot,
        "rel": _np.concatenate([a["rel_table_2"], _np.full((1, NSA_HEADS), NEG, _np.float32)], axis=0),
        "w_dtwi": columns(padded(_np.concatenate([cut["dt"], cut["wi"]], axis=1))),
        "w_gab": columns(padded(_np.concatenate([cut["gate"], cut["a"], cut["b"]], axis=1))),
        "w_cmp2": _np.concatenate([row_tiles(a["cmp_w2_k_2"][0], 2), row_tiles(a["cmp_w2_v_2"][0], 2)], axis=1),
        "w_ki": columns(_np.concatenate([cut["ki"], cut["ki"]], axis=1)),
        "w_qi": columns(cut["qi"]),
        "w_q": columns(cut["q"]),
        "w_k": columns(cut["k"]),
        "w_v": pieces(cut["v"], 512),
        "w_xbc": columns(cut["xbc"]),
        "w_z": columns(cut["z"]),
        "w_out_ssd": halves(a["w_out"][0][0:1024]),
        "w_out_att": halves(a["w_out"][0][1024:2048]),
        "w_up": columns(a["w_up"][0]),
        "w_down": down(a["w_down"][0]),
        "w_kv": columns(_np.concatenate([kv[0], kv[1], kv[2], kv[4]], axis=1)),
        "w_nq": columns(cut["nq"]),
        "w_vsvw": pieces(_np.concatenate([kv[3], kv[5]], axis=1), 512),
        "w_cmp1": _np.concatenate(cmp1),
        "w_gdn0": columns(half[0]),
        "w_gdn1": columns(half[1]),
        "w_gz0": columns(cut["gz"][:, 0:512]),
        "w_gz1": columns(cut["gz"][:, 512:1024]),
        "w_merge": columns(cut["merge"]),
        "w_papb": _np.concatenate(papb),
        "w_o": columns(a["w_o_2"][0]),
        "w_up2": columns(a["w_up_2"][0]),
        "w_down2": down(a["w_down_2"][0]),
    }
    nc = _bacc.Bacc("TRN2", target_bir_lowering=False, num_devices=1)
    t_in, feed = {}, {}
    for name, v in arrays.items():
        v = _np.ascontiguousarray(v)
        feed[f"in_{name}"] = v
        t_in[name] = nc.dram_tensor(f"in_{name}", v.shape, _mybir.dt.float32, kind="ExternalInput").ap()
    x_out = nc.dram_tensor("x_out", (P, KD * S), _mybir.dt.float32, kind="ExternalOutput").ap()
    bias_rows = nc.dram_tensor("bias_rows", (P, NSA_HEADS * 2 * S), _mybir.dt.float32).ap()
    x_kept = nc.dram_tensor("x_kept", (P, KD * S), _mybir.dt.float32).ap()
    build(nc, t_in, x_out, bias_rows, x_kept)
    r = _run(nc, [feed], core_ids=[0])
    y = r.results[0]["x_out"]
    return _np.ascontiguousarray(y.reshape(P, KD, S).transpose(2, 1, 0).reshape(1, S, D))
```
